# Optimizing a Trainium2 kernel written in Bass

```python
import jax
import jax.numpy as jnp
from jax import lax
import numpy as np

D_MODEL = 1024
BATCH = 1
SEQ = 1024
DEPTH = 1
DEC_BATCH = 1
DEC_SEQ = 256
PAST_LEN = 128

N_META = 16
HEAD_DIM = 64
N_HEADS = 8
N_KV_HEADS = 2
Q_PER_KV = N_HEADS // N_KV_HEADS
ATTN_W = N_HEADS * HEAD_DIM
KV_W = N_KV_HEADS * HEAD_DIM
REC_W = D_MODEL // 2
REC_BLOCKS = 8
REC_BW = REC_W // REC_BLOCKS
MIX_W = ATTN_W + REC_W
IN_COLS = ATTN_W + 2 * KV_W + 2 * REC_W
CONV_W = 4
CONV_LEFT = 2
RG_C = 8.0
WINDOW = 128
ATTN_BLK = 128
ROT_DIM = HEAD_DIM // 4
ROPE_THETA = 500000.0
N_GROUPS = 4
EXP_PER_GROUP = 8
N_EXPERTS = N_GROUPS * EXP_PER_GROUP
TOP_K = 2
D_EXPERT = D_MODEL // 2
MOE_BLK = 256
EPS = 1e-6

kernel_name = 'hymba_rglru_swa_hier_moe_encoder'

def rmsnorm(x, g):
    x32 = x.astype(jnp.float32)
    y = x32 * lax.rsqrt(jnp.mean(x32 * x32, axis=-1, keepdims=True) + EPS)
    return (y * g.astype(jnp.float32)).astype(x.dtype)

def rope_tables(t):
    inv = ROPE_THETA ** (-jnp.arange(0, ROT_DIM, 2, dtype=jnp.float32) / ROT_DIM)
    ang = jnp.arange(t, dtype=jnp.float32)[:, None] * inv[None, :]
    return jnp.cos(ang), jnp.sin(ang)

def apply_partial_rope(x, cos, sin):
    half = ROT_DIM // 2
    c = cos[None, :, None, :]
    s = sin[None, :, None, :]
    x1 = x[..., :half]
    x2 = x[..., half:ROT_DIM]
    return jnp.concatenate([x1 * c - x2 * s, x2 * c + x1 * s, x[..., ROT_DIM:]], axis=-1)

def sink_softmax_av(s_win, v_win, s_meta, v_meta, sink):
    sk = sink[None, :, :, None, None]
    m = jnp.maximum(jnp.maximum(s_win.max(-1, keepdims=True), s_meta.max(-1, keepdims=True)), sk)
    p_win = jnp.exp(s_win - m)
    p_meta = jnp.exp(s_meta - m)
    denom = p_win.sum(-1, keepdims=True) + p_meta.sum(-1, keepdims=True) + jnp.exp(sk - m)
    out = jnp.einsum('bgrqk,bkgd->bgrqd', p_win, v_win) + jnp.einsum('bgrqk,bkgd->bgrqd', p_meta, v_meta)
    return out / denom

def windowed_gqa(q, k, v, sink):
    b, t = q.shape[0], q.shape[1]
    s_len = t - N_META
    nb = s_len // ATTN_BLK
    q = q.reshape(b, t, N_KV_HEADS, Q_PER_KV, HEAD_DIM) * (HEAD_DIM ** -0.5)
    sk = sink.astype(jnp.float32).reshape(N_KV_HEADS, Q_PER_KV)
    qm, qr = q[:, :N_META], q[:, N_META:]
    km, kr = k[:, :N_META], k[:, N_META:]
    vm, vr = v[:, :N_META], v[:, N_META:]
    pad = ((0, 0), (ATTN_BLK, ATTN_BLK), (0, 0), (0, 0))
    kpad = jnp.pad(kr, pad)
    vpad = jnp.pad(vr, pad)
    qq = jnp.arange(ATTN_BLK)[:, None]
    kk = jnp.arange(3 * ATTN_BLK)[None, :]

    def band(n):
        qb = lax.dynamic_slice_in_dim(qr, n * ATTN_BLK, ATTN_BLK, axis=1)
        kb = lax.dynamic_slice_in_dim(kpad, n * ATTN_BLK, 3 * ATTN_BLK, axis=1)
        vb = lax.dynamic_slice_in_dim(vpad, n * ATTN_BLK, 3 * ATTN_BLK, axis=1)
        qi = n * ATTN_BLK + qq
        ki = (n - 1) * ATTN_BLK + kk
        valid = (jnp.abs(ki - qi) <= WINDOW) & (ki >= 0) & (ki < s_len)
        s_win = jnp.where(valid, jnp.einsum('bqgrd,bkgd->bgrqk', qb, kb), -jnp.inf)
        s_met = jnp.einsum('bqgrd,bkgd->bgrqk', qb, km)
        return sink_softmax_av(s_win, vb, s_met, vm, sk)

    out_r = lax.map(band, jnp.arange(nb))
    out_r = out_r.transpose(1, 0, 4, 2, 3, 5).reshape(b, s_len, ATTN_W)
    qpos = jnp.arange(N_META)[:, None]
    kpos = N_META + jnp.arange(ATTN_BLK)[None, :]
    s_mr = jnp.where(kpos - qpos <= WINDOW,
                     jnp.einsum('bqgrd,bkgd->bgrqk', qm, kr[:, :ATTN_BLK]), -jnp.inf)
    s_mm = jnp.einsum('bqgrd,bkgd->bgrqk', qm, km)
    out_m = sink_softmax_av(s_mr, vr[:, :ATTN_BLK], s_mm, vm, sk)
    out_m = out_m.transpose(0, 3, 1, 2, 4).reshape(b, N_META, ATTN_W)
    return jnp.concatenate([out_m, out_r], axis=1)

def _lin_combine(c1, c2):
    a1, b1 = c1
    a2, b2 = c2
    return a1 * a2, a2 * b1 + b2

def centred_depthwise_conv(x, w, b):
    t = x.shape[1]
    xp = jnp.pad(x, ((0, 0), (CONV_LEFT, CONV_W - 1 - CONV_LEFT), (0, 0)))
    return sum(xp[:, j:j + t] * w[j] for j in range(CONV_W)) + b

def rglru_scan(xc, w_r, b_r, w_i, b_i, lam, reverse):
    b, t, c = xc.shape
    xblk = xc.reshape(b, t, REC_BLOCKS, REC_BW)
    gate_r = jax.nn.sigmoid(jnp.einsum('btni,nij->btnj', xblk, w_r).reshape(b, t, c) + b_r)
    gate_i = jax.nn.sigmoid(jnp.einsum('btni,nij->btnj', xblk, w_i).reshape(b, t, c) + b_i)
    log_a = -RG_C * gate_r * jax.nn.softplus(-lam)
    a = jnp.exp(log_a)
    u = jnp.sqrt(-jnp.expm1(2.0 * log_a)) * (gate_i * xc)
    if reverse:
        a = jnp.flip(a, axis=1)
        u = jnp.flip(u, axis=1)
    _, h = lax.associative_scan(_lin_combine, (a, u), axis=1)
    return jnp.flip(h, axis=1) if reverse else h

def mixer(h, cos, sin, p):
    f32 = jnp.float32
    b, t, _ = h.shape
    proj = h @ p['w_in']
    q, k, v, xr, yg = jnp.split(
        proj, [ATTN_W, ATTN_W + KV_W, ATTN_W + 2 * KV_W, ATTN_W + 2 * KV_W + REC_W], axis=-1)
    q = apply_partial_rope(q.astype(f32).reshape(b, t, N_HEADS, HEAD_DIM), cos, sin)
    k = apply_partial_rope(k.astype(f32).reshape(b, t, N_KV_HEADS, HEAD_DIM), cos, sin)
    v = v.astype(f32).reshape(b, t, N_KV_HEADS, HEAD_DIM)
    attn = windowed_gqa(q, k, v, p['attn_sink'])
    xc = centred_depthwise_conv(xr.astype(f32), p['conv_w'].astype(f32), p['conv_b'].astype(f32))
    rec = (rglru_scan(xc, p['w_rgate_fwd'].astype(f32), p['b_rgate_fwd'].astype(f32),
                      p['w_igate_fwd'].astype(f32), p['b_igate_fwd'].astype(f32),
                      p['lam_fwd'].astype(f32), False)
           + rglru_scan(xc, p['w_rgate_bwd'].astype(f32), p['b_rgate_bwd'].astype(f32),
                        p['w_igate_bwd'].astype(f32), p['b_igate_bwd'].astype(f32),
                        p['lam_bwd'].astype(f32), True))
    rec = rec * jax.nn.gelu(yg.astype(f32))
    mixed = jnp.concatenate([rmsnorm(attn, p['g_attn_out']), rmsnorm(rec, p['g_rec_out'])], axis=-1)
    return mixed.astype(h.dtype) @ p['w_out']

def expert_dispatch(u, eid, gates, w_g, w_u, w_d):
    n, d = u.shape
    a_len = n * TOP_K
    rows = -(-(a_len + N_EXPERTS * (MOE_BLK - 1)) // MOE_BLK) * MOE_BLK
    nblk = rows // MOE_BLK
    flat_e = eid.reshape(-1)
    flat_tok = jnp.repeat(jnp.arange(n, dtype=jnp.int32), TOP_K)
    flat_g = gates.reshape(-1)
    order = jnp.argsort(flat_e)
    se = flat_e[order]
    counts = jnp.zeros((N_EXPERTS,), jnp.int32).at[flat_e].add(1)
    padded = (counts + MOE_BLK - 1) // MOE_BLK * MOE_BLK
    start = jnp.cumsum(counts) - counts
    pend = jnp.cumsum(padded)
    pstart = pend - padded
    dest = pstart[se] + (jnp.arange(a_len, dtype=jnp.int32) - start[se])
    row_tok = jnp.full((rows,), n, jnp.int32).at[dest].set(flat_tok[order])
    row_gate = jnp.zeros((rows,), jnp.float32).at[dest].set(flat_g[order])
    blk_e = jnp.minimum(
        jnp.searchsorted(pend, jnp.arange(nblk, dtype=jnp.int32) * MOE_BLK, side='right'),
        N_EXPERTS - 1)
    u_pad = jnp.concatenate([u, jnp.zeros((1, d), u.dtype)], axis=0)

    def run_block(args):
        tok, e = args
        xb = u_pad[tok]
        hid = jax.nn.silu(xb @ w_g[e]) * (xb @ w_u[e])
        return hid @ w_d[e]

    yb = lax.map(run_block, (row_tok.reshape(nblk, MOE_BLK), blk_e)).reshape(rows, d)
    yb = yb * row_gate[:, None].astype(yb.dtype)
    return jnp.zeros((n + 1, d), yb.dtype).at[row_tok].add(yb)[:n]

def hier_moe(u, p):
    f32 = jnp.float32
    b, t, d = u.shape
    n = b * t
    uf = u.reshape(n, d)
    grp_logits = (uf @ p['w_router_grp']).astype(f32) + p['b_router_grp'].astype(f32)
    grp = jnp.argmax(grp_logits, axis=-1).astype(jnp.int32)
    p_grp = jnp.take_along_axis(jax.nn.softmax(grp_logits, axis=-1), grp[:, None], axis=-1)
    exp_logits = (uf @ p['w_router_exp']).astype(f32) + p['b_router_exp'].astype(f32)
    idx = grp[:, None] * EXP_PER_GROUP + jnp.arange(EXP_PER_GROUP, dtype=jnp.int32)[None, :]
    in_grp = jnp.take_along_axis(exp_logits, idx, axis=-1)
    top_v, top_i = lax.top_k(in_grp, TOP_K)
    gates = jax.nn.softmax(top_v, axis=-1) * p_grp
    eid = grp[:, None] * EXP_PER_GROUP + top_i.astype(jnp.int32)
    y = expert_dispatch(uf, eid, gates, p['w_exp_gate'], p['w_exp_up'], p['w_exp_down'])
    return y.reshape(b, t, d)

def encode(x, meta_tokens, layers, ln_final_g):
    b = x.shape[0]
    meta = jnp.broadcast_to(meta_tokens.astype(x.dtype)[None], (b, N_META, D_MODEL))
    h = jnp.concatenate([meta, x], axis=1)
    cos, sin = rope_tables(h.shape[1])
    for l in range(DEPTH):
        p = {name: arr[l] for name, arr in layers.items()}
        h = h + mixer(rmsnorm(h, p['ln_mix_g']), cos, sin, p)
        h = h + hier_moe(rmsnorm(h, p['ln_ffn_g']), p)
    return rmsnorm(h, ln_final_g)[:, N_META:]

def setup_inputs(seed: int = 0) -> dict:
    key = jax.random.key(seed)
    ks = jax.random.split(key, 32)
    f32 = jnp.float32

    def nrm(k, shape, scale):
        return jax.random.normal(k, shape, f32) * scale

    def lam_init(k):
        a_c = jax.random.uniform(k, (DEPTH, REC_W), f32, 0.9, 0.999)
        a0 = a_c ** (1.0 / RG_C)
        return jnp.log(a0) - jnp.log1p(-a0)

    return {
        'x_prompt': nrm(ks[0], (BATCH, SEQ, D_MODEL), 1.0),
        'x_sample': nrm(ks[1], (DEC_BATCH, DEC_SEQ, D_MODEL), 1.0),
        'meta_tokens': nrm(ks[2], (N_META, D_MODEL), 1.0),
        'ln_mix_g': 1.0 + nrm(ks[3], (DEPTH, D_MODEL), 0.02),
        'w_in': nrm(ks[4], (DEPTH, D_MODEL, IN_COLS), D_MODEL ** -0.5),
        'conv_w': nrm(ks[5], (DEPTH, CONV_W, REC_W), CONV_W ** -0.5),
        'conv_b': nrm(ks[6], (DEPTH, REC_W), 0.01),
        'w_rgate_fwd': nrm(ks[7], (DEPTH, REC_BLOCKS, REC_BW, REC_BW), REC_BW ** -0.5),
        'b_rgate_fwd': nrm(ks[8], (DEPTH, REC_W), 0.01),
        'w_igate_fwd': nrm(ks[9], (DEPTH, REC_BLOCKS, REC_BW, REC_BW), REC_BW ** -0.5),
        'b_igate_fwd': nrm(ks[10], (DEPTH, REC_W), 0.01),
        'lam_fwd': lam_init(ks[11]),
        'w_rgate_bwd': nrm(ks[12], (DEPTH, REC_BLOCKS, REC_BW, REC_BW), REC_BW ** -0.5),
        'b_rgate_bwd': nrm(ks[13], (DEPTH, REC_W), 0.01),
        'w_igate_bwd': nrm(ks[14], (DEPTH, REC_BLOCKS, REC_BW, REC_BW), REC_BW ** -0.5),
        'b_igate_bwd': nrm(ks[15], (DEPTH, REC_W), 0.01),
        'lam_bwd': lam_init(ks[16]),
        'attn_sink': nrm(ks[17], (DEPTH, N_HEADS), 1.0),
        'g_attn_out': 1.0 + nrm(ks[18], (DEPTH, ATTN_W), 0.02),
        'g_rec_out': 1.0 + nrm(ks[19], (DEPTH, REC_W), 0.02),
        'w_out': nrm(ks[20], (DEPTH, MIX_W, D_MODEL), MIX_W ** -0.5),
        'ln_ffn_g': 1.0 + nrm(ks[21], (DEPTH, D_MODEL), 0.02),
        'w_router_grp': nrm(ks[22], (DEPTH, D_MODEL, N_GROUPS), D_MODEL ** -0.5),
        'b_router_grp': nrm(ks[23], (DEPTH, N_GROUPS), 0.01),
        'w_router_exp': nrm(ks[24], (DEPTH, D_MODEL, N_EXPERTS), D_MODEL ** -0.5),
        'b_router_exp': nrm(ks[25], (DEPTH, N_EXPERTS), 0.01),
        'w_exp_gate': nrm(ks[26], (DEPTH, N_EXPERTS, D_MODEL, D_EXPERT), D_MODEL ** -0.5),
        'w_exp_up': nrm(ks[27], (DEPTH, N_EXPERTS, D_MODEL, D_EXPERT), D_MODEL ** -0.5),
        'w_exp_down': nrm(ks[28], (DEPTH, N_EXPERTS, D_EXPERT, D_MODEL), D_EXPERT ** -0.5),
        'ln_final_g': 1.0 + nrm(ks[29], (D_MODEL,), 0.02),
    }

def reference(x_prompt, x_sample, meta_tokens, ln_mix_g, w_in, conv_w, conv_b,
              w_rgate_fwd, b_rgate_fwd, w_igate_fwd, b_igate_fwd, lam_fwd,
              w_rgate_bwd, b_rgate_bwd, w_igate_bwd, b_igate_bwd, lam_bwd,
              attn_sink, g_attn_out, g_rec_out, w_out, ln_ffn_g,
              w_router_grp, b_router_grp, w_router_exp, b_router_exp,
              w_exp_gate, w_exp_up, w_exp_down, ln_final_g):
    layers = {
        'ln_mix_g': ln_mix_g, 'w_in': w_in, 'conv_w': conv_w, 'conv_b': conv_b,
        'w_rgate_fwd': w_rgate_fwd, 'b_rgate_fwd': b_rgate_fwd,
        'w_igate_fwd': w_igate_fwd, 'b_igate_fwd': b_igate_fwd, 'lam_fwd': lam_fwd,
        'w_rgate_bwd': w_rgate_bwd, 'b_rgate_bwd': b_rgate_bwd,
        'w_igate_bwd': w_igate_bwd, 'b_igate_bwd': b_igate_bwd, 'lam_bwd': lam_bwd,
        'attn_sink': attn_sink, 'g_attn_out': g_attn_out, 'g_rec_out': g_rec_out,
        'w_out': w_out, 'ln_ffn_g': ln_ffn_g,
        'w_router_grp': w_router_grp, 'b_router_grp': b_router_grp,
        'w_router_exp': w_router_exp, 'b_router_exp': b_router_exp,
        'w_exp_gate': w_exp_gate, 'w_exp_up': w_exp_up, 'w_exp_down': w_exp_down,
    }
    y_prompt = encode(x_prompt, meta_tokens, layers, ln_final_g)
    y_sample = encode(x_sample, meta_tokens, layers, ln_final_g)
    return (y_prompt, y_sample)


_drawn_inputs = setup_inputs


def setup_inputs(seed=0):
    import zlib

    import numpy as np

    out = dict(_drawn_inputs(seed))
    spreads = {}
    factors = {'b_rgate_fwd': 39.194,
     'b_igate_fwd': 29.283,
     'b_rgate_bwd': 41.709,
     'b_igate_bwd': 32.558,
     'attn_sink': 8.0,
     'g_attn_out': 11.923,
     'g_rec_out': 12.187,
     'b_router_grp': 36.114,
     'b_router_exp': 31.12,
     'ln_final_g': 8.495,
     'ln_ffn_g': 5.912}
    for name, (base, spread) in spreads.items():
        noise = np.random.default_rng([zlib.crc32(name.encode()), seed]).standard_normal(out[name].shape)
        drawn = base * np.exp(spread * noise) if base else spread * noise
        out[name] = jnp.asarray(drawn.astype(out[name].dtype))
    for name, factor in factors.items():
        out[name] = (out[name] * factor).astype(out[name].dtype)
    return out
```

```python
from contextlib import ExitStack, contextmanager

import numpy as np

import concourse.bass as bass
from concourse import mybir

F32 = mybir.dt.float32
F32R = mybir.dt.float32r
I32 = mybir.dt.int32
U32 = mybir.dt.uint32
ALU = mybir.AluOpType
ACT = mybir.ActivationFunctionType
AX = mybir.AxisListType

P = 128
D = 1024
META = 16
SEQS = (1024, 256)
REAL = sum(SEQS)
NB = REAL // P
COLS = META + REAL
KD = D // P
HEADS = 8
HD = 64
ATTN = HEADS * HD
REC = 512
FT = REC // P
FTILES = 14
NCH = 3
CH = COLS // NCH
BANK = 512
EXP = 32
FE = 512
EPS = 1e-6
NEG = -1e30
RING = 2
WIN = 3 * P
KEYS = WIN + META
T0 = META + SEQS[0]
T1 = META + SEQS[1]
XRW = 2 + T0 + 1 + 2 + T1 + 1
RW = XRW - 3
OFF1 = T0 + 3
LIST = 1280
MAXBLK = 64
MAXPAIRS = (2 * REAL // P + EXP) // 2
YROWS = 2 * REAL + P
ROUT = 40


def done(t):
    return t + 1 + RING


def free(t):
    return t + 1


@contextmanager
def semaphores(nc):
    with ExitStack() as ctx:
        made = []

        def sem(name):
            made.append(ctx.enter_context(nc.semaphore(name)))
            return made[-1]

        yield sem
        with nc.Block() as block:
            @block.sync
            def _(sp):
                for one in made:
                    sp.sem_clear(one)


def encoder(nc, a, out):
    top = ExitStack()
    with top:
        def dram(name, shape, dt):
            return nc.dram_tensor(name, shape, dt, kind="Internal").ap()

        h2_dram = dram("h2_dram", [REAL, D], F32)
        u_dram = dram("u_dram", [REAL, D], F32)
        y_dram = dram("y_dram", [YROWS, D], F32)
        list_dram = dram("list_dram", [(EXP + 1) * LIST, 1], I32)
        table_dram = dram("table_dram", [MAXBLK, 4], I32)

        def keep(name, shape, dt=F32):
            return top.enter_context(nc.sbuf_tensor(name, shape, dt))

        gate1 = keep("gate1", [P, NB])
        gate2 = keep("gate2", [P, NB])
        expert1 = keep("expert1", [P, NB])
        expert2 = keep("expert2", [P, NB])
        place1 = keep("place1", [P, NB])
        place2 = keep("place2", [P, NB])
        counts = keep("counts", [P, EXP])
        iota_e = keep("iota_e", [P, EXP])
        ident = keep("ident", [P, P])
        eps_t = keep("eps_t", [P, 1])

        with ExitStack() as mixer:
            def mk(name, shape, dt=F32):
                return mixer.enter_context(nc.sbuf_tensor(name, shape, dt))

            q_pre = mk("q_pre", [P, 4, COLS])
            yg = mk("yg", [P, FT, COLS])
            rstd_rec = mk("rstd_rec", [P, NB])
            k_rot = mk("k_rot", [P, META + P + REAL + P])
            v_tok = mk("v_tok", [P, (NB + 2) * P])
            v_meta = mk("v_meta", [P, ATTN])
            with ExitStack() as front:
                def fk(name, shape, dt=F32):
                    return front.enter_context(nc.sbuf_tensor(name, shape, dt))

                k_pre = fk("k_pre", [P, COLS])
                v_pre = fk("v_pre", [P, COLS])
                xr = fk("xr", [P, FT, XRW])
                with semaphores(nc) as sem:
                    project(nc, sem, a, q_pre, k_pre, v_pre, xr, yg, ident, eps_t, iota_e, list_dram, y_dram)
                with semaphores(nc) as sem:
                    recurrence(nc, sem, a, k_pre, v_pre, xr, yg, k_rot, v_tok, v_meta, rstd_rec, ident, eps_t)
            rec = yg[:, :, META:COLS]
            with semaphores(nc) as sem:
                mix(nc, sem, a, q_pre, rec, rstd_rec, k_rot, v_tok, v_meta, ident, eps_t, iota_e,
                    gate1, gate2, expert1, expert2, place1, place2, counts, h2_dram, u_dram, list_dram)
        slots = [top.enter_context(nc.sbuf_tensor(f"slot{j}", [P, NB], I32)) for j in range(2)]
        table = top.enter_context(nc.sbuf_tensor("table", [1, MAXBLK * 4], I32))
        with semaphores(nc) as sem:
            plan(nc, sem, iota_e, counts, expert1, expert2, place1, place2, slots, table, table_dram)
        with semaphores(nc) as sem:
            experts(nc, sem, a, ident, table, list_dram, u_dram, y_dram)
        with semaphores(nc) as sem:
            combine(nc, sem, a, eps_t, gate1, gate2, slots, h2_dram, y_dram, out)


def project(nc, sem, a, q_pre, k_pre, v_pre, xr, yg, ident, eps_t, iota_e, list_dram, y_dram):
    with ExitStack() as ctx:
        def sb(name, shape, dt=F32):
            return ctx.enter_context(nc.sbuf_tensor(name, shape, dt))

        h_hi = sb("h_hi", [P, KD, COLS], F32R)
        h_lo = sb("h_lo", [P, KD, COLS], F32R)
        w_raw = [sb(f"w_raw{s}", [P, KD, P]) for s in range(RING)]
        w_hi = [sb(f"w_hi{s}", [P, KD, P], F32R) for s in range(RING)]
        w_lo = [sb(f"w_lo{s}", [P, KD, P], F32R) for s in range(RING)]
        x_in = [yg[:, s, 0:D] for s in range(RING)]
        xn = [sb(f"xn{s}", [P, D]) for s in range(RING)]
        g_bc = w_raw[1][:, :, :].rearrange("p k c -> p (k c)")
        ssq = [sb(f"ssq{s}", [P, 1]) for s in range(RING)]
        rms = [sb(f"rms{s}", [P, 1]) for s in range(RING)]
        rstd = [sb(f"rstd{s}", [P, 1]) for s in range(RING)]
        bank = [ctx.enter_context(nc.psum_tensor(f"pj{n}", [P, BANK], F32)) for n in range(6)]
        tr = ctx.enter_context(nc.psum_tensor("pj_tr", [P, 2, BANK], F32))

        consts_in = sem("consts_in")
        x_arrived = [sem(f"x_arrived{s}") for s in range(RING)]
        w_arrived = [sem(f"w_arrived{s}") for s in range(RING)]
        fills = sem("fills")
        fill_dma = sem("fill_dma")
        eps_set = sem("eps_set")
        squared = sem("squared")
        rms_done = sem("rms_done")
        rstd_done = sem("rstd_done")
        xn_done = sem("xn_done")
        x_turned = sem("x_turned")
        h_hi_done = sem("h_hi_done")
        h_lo_done = sem("h_lo_done")
        w_hi_done = sem("w_hi_done")
        w_lo_done = sem("w_lo_done")
        proj_done = sem("proj_done")
        proj_out = sem("proj_out")
        xr_cleared = sem("xr_cleared")

        block = ctx.enter_context(nc.Block())
        TILES = NB + 1

        def rows(t):
            return META if isinstance(t, int) and t == NB else P

        def col(t):
            return 0 if isinstance(t, int) and t == NB else META + t * P

        @block.sync
        def _(sp):
            sp.dma_start(ident[:, :], a["ident"]).then_inc(consts_in, 16)
            sp.dma_start(g_bc, a["ln_mix_g"][0].partition_broadcast(P)).then_inc(consts_in, 16)

            def load_x(t, s, round_):
                sp.wait_ge(xn_done, free(t))
                src = a["meta"] if isinstance(t, int) and t == NB else a["x"][bass.ds(t * P, P), :]
                sp.dma_start(x_in[s][0:rows(t), :], src).then_inc(x_arrived[s], 16)

            load_x(0, 0, 0)
            with sp.Fori(0, 4) as i:
                load_x(2 * i + 1, 1, i)
                load_x(2 * i + 2, 0, i + 1)
            load_x(9, 1, 4)
            load_x(10, 0, 5)

            def load_w(f, s):
                sp.wait_ge(w_lo_done, free(f))
                sp.dma_start(w_raw[s][:, :, :], a["w_in"][bass.ds(f, 1), :, :, :].rearrange("o p k c -> p (o k) c")
                             ).then_inc(w_arrived[s], 16)

            sp.wait_ge(xn_done, done(NB))
            with sp.Fori(0, FTILES // 2) as i:
                load_w(2 * i, 0)
                load_w(2 * i + 1, 1)
            sp.wait_ge(fills, 3)
            sp.dma_start(list_dram.rearrange("(p c) o -> p (c o)", p=P),
                         xn[0][:, 0:(EXP + 1) * LIST // P].bitcast(I32)).then_inc(fill_dma, 16)
            sp.dma_start(y_dram[2 * REAL:YROWS, :], xn[1][:, :]).then_inc(fill_dma, 16)
            sp.wait_ge(fill_dma, 32)

        @block.gpsimd
        def _(pool):
            pool.memset(xr[:, :, :], 0.0).then_inc(xr_cleared, 1)
            pool.iota(iota_e[:, :], pattern=[[1, EXP]], base=0, channel_multiplier=0,
                      allow_small_or_imprecise_dtypes=True).then_inc(fills, 1)
            pool.wait_ge(x_turned, done(NB))
            pool.memset(xn[0][:, :], 0.0).then_inc(fills, 1)
            pool.memset(xn[1][:, :], 0.0).then_inc(fills, 1)

        @block.scalar
        def _(act):
            act.sem_inc(h_hi_done, RING)
            act.sem_inc(w_hi_done, RING)
            act.sem_inc(proj_out, 2 * NCH)

            def norm(t, s, round_):
                n = rows(t)
                act.wait_ge(x_arrived[s], 16 * (round_ + 1))
                act.wait_ge(x_turned, free(t))
                act.activation(xn[s][0:n, :], x_in[s][0:n, :], ACT.Square, accum_out=ssq[s][0:n, :]).then_inc(squared, 1)
                act.wait_ge(squared, t + 1)
                act.activation(rms[s][0:n, :], ssq[s][0:n, :], ACT.Sqrt, bias=eps_t[0:n, :], scale=1.0 / D).then_inc(rms_done, 1)

            def hi(t, s):
                n = rows(t)
                act.wait_ge(x_turned, done(t))
                act.activation(h_hi[:, :, bass.ds(col(t), n)],
                               tr[:, :, :].rearrange("p b (k c) -> p (b k) c", c=P)[:, :, 0:n],
                               ACT.Copy).then_inc(h_hi_done, 1)

            act.wait_ge(eps_set, 1)
            norm(0, 0, 0)
            with act.Fori(0, 4) as i:
                norm(2 * i + 1, 1, i)
                hi(2 * i, 0)
                norm(2 * i + 2, 0, i + 1)
                hi(2 * i + 1, 1)
            norm(9, 1, 4)
            hi(8, 0)
            norm(10, 0, 5)
            hi(9, 1)
            hi(10, 0)

            def split_w(f, s, round_):
                act.wait_ge(w_arrived[s], 16 * (round_ + 1))
                act.wait_ge(proj_done, NCH * f + NCH)
                act.activation(w_hi[s][:, :, :], w_raw[s][:, :, :], ACT.Copy).then_inc(w_hi_done, 1)

            def evacuate(f, s, put):
                for c in range(NCH):
                    act.wait_ge(proj_done, NCH * f + c + 1 + 2 * NCH)
                    put(bank[NCH * s + c], c).then_inc(proj_out, 1)

            def put_flat(dst, func=ACT.Copy):
                def put(ps, c):
                    return act.activation(dst(c), ps[:, 0:CH], func)
                return put

            def put_xr(ft):
                def piece(dst, ps, lo, n):
                    return act.activation(xr[:, bass.ds(ft, 1), dst:dst + n].rearrange("p o c -> p (o c)"), ps[:, lo:lo + n], ACT.Copy)

                def put(ps, c):
                    if c == 0:
                        piece(2 + OFF1, ps, 0, META)
                        return piece(2, ps, 0, CH)
                    if c == 1:
                        return piece(2 + CH, ps, 0, CH)
                    n = T0 - 2 * CH
                    piece(2 + 2 * CH, ps, 0, n)
                    return piece(2 + OFF1 + META, ps, n, CH - n)
                return put

            split_w(0, 0, 0)
            with act.Fori(0, 2) as i:
                split_w(2 * i + 1, 1, i)
                evacuate(2 * i, 0, put_flat(lambda c: q_pre[:, bass.ds(2 * i, 1), c * CH:(c + 1) * CH].rearrange("p o c -> p (o c)")))
                split_w(2 * i + 2, 0, i + 1)
                evacuate(2 * i + 1, 1, put_flat(lambda c: q_pre[:, bass.ds(2 * i + 1, 1), c * CH:(c + 1) * CH].rearrange("p o c -> p (o c)")))
            split_w(5, 1, 2)
            evacuate(4, 0, put_flat(lambda c: k_pre[:, c * CH:(c + 1) * CH]))
            split_w(6, 0, 3)
            evacuate(5, 1, put_flat(lambda c: v_pre[:, c * CH:(c + 1) * CH]))
            act.wait_ge(xr_cleared, 1)
            with act.Fori(0, 2) as i:
                split_w(2 * i + 7, 1, i + 3)
                evacuate(2 * i + 6, 0, put_xr(2 * i))
                split_w(2 * i + 8, 0, i + 4)
                evacuate(2 * i + 7, 1, put_xr(2 * i + 1))
            for f in range(10, FTILES):
                if f + 1 < FTILES:
                    split_w(f + 1, (f + 1) % 2, (f + 1) // 2)
                evacuate(f, f % 2, put_flat(lambda c: yg[:, f - 10, c * CH:(c + 1) * CH], ACT.Gelu_apprx_tanh))

        @block.vector
        def _(dve):
            dve.memset(eps_t[:, :], EPS).then_inc(eps_set, 1)
            dve.sem_inc(xn_done, RING)
            dve.sem_inc(h_lo_done, RING)
            dve.sem_inc(w_lo_done, RING)

            def norm(t, s):
                n = rows(t)
                dve.wait_ge(rms_done, t + 1)
                dve.reciprocal(rstd[s][0:n, :], rms[s][0:n, :]).then_inc(rstd_done, 1)
                dve.wait_ge(rstd_done, t + 1)
                dve.scalar_tensor_tensor(out=xn[s][0:n, :], in0=x_in[s][0:n, :], scalar=rstd[s][0:n, :],
                                         in1=g_bc[0:n, :], op0=ALU.mult, op1=ALU.mult).then_inc(xn_done, 1)

            def lo(t):
                n = rows(t)
                dve.wait_ge(h_hi_done, done(t))
                dst = bass.ds(col(t), n)
                dve.tensor_tensor(h_lo[:, :, dst], tr[:, :, :].rearrange("p b (k c) -> p (b k) c", c=P)[:, :, 0:n],
                                  h_hi[:, :, dst].bitcast(F32), ALU.subtract).then_inc(h_lo_done, 1)

            dve.wait_ge(consts_in, 32)
            norm(0, 0)
            with dve.Fori(0, 4) as i:
                norm(2 * i + 1, 1)
                lo(2 * i)
                norm(2 * i + 2, 0)
                lo(2 * i + 1)
            norm(9, 1)
            lo(8)
            norm(10, 0)
            lo(9)
            lo(10)
            with dve.Fori(0, FTILES // 2) as i:
                for s in range(RING):
                    dve.wait_ge(w_hi_done, done(2 * i + s))
                    dve.tensor_tensor(w_lo[s][:, :, :], w_raw[s][:, :, :], w_hi[s][:, :, :].bitcast(F32),
                                      ALU.subtract).then_inc(w_lo_done, 1)

        @block.tensor
        def _(pe):
            pe.sem_inc(x_turned, RING)
            pe.sem_inc(proj_done, 2 * NCH)
            pe.wait_ge(consts_in, 32)

            def turn(t, s):
                n = rows(t)
                pe.wait_ge(xn_done, done(t))
                pe.wait_ge(h_lo_done, t + RING)
                for k in range(KD):
                    mm = pe.transpose(tr[:, k // 4, (k % 4) * P:(k % 4) * P + n], xn[s][0:n, k * P:(k + 1) * P],
                                      ident[0:n, 0:n])
                mm.then_inc(x_turned, 1)

            turn(0, 0)
            with pe.Fori(0, 4) as i:
                turn(2 * i + 1, 1)
                turn(2 * i + 2, 0)
            turn(9, 1)
            turn(10, 0)
            pe.wait_ge(h_lo_done, done(NB))
            with pe.Fori(0, FTILES // 2) as i:
                for s in range(RING):
                    f = 2 * i + s
                    pe.wait_ge(w_lo_done, done(f))
                    for c in range(NCH):
                        pe.wait_ge(proj_out, NCH * f + c + 1)
                        cols = slice(c * CH, (c + 1) * CH)
                        for k in range(KD):
                            for n, (w, h) in enumerate(((w_hi, h_hi), (w_hi, h_lo), (w_lo, h_hi))):
                                mm = pe.matmul(bank[NCH * s + c][:, 0:CH], w[s][:, k, :], h[:, k, cols],
                                               start=(k == 0 and n == 0), stop=(k == KD - 1 and n == 2))
                        mm.then_inc(proj_done, 1)


def recurrence(nc, sem, a, k_pre, v_pre, xr, yg, k_rot, v_tok, v_meta, rstd_rec, ident, eps_t):
    with ExitStack() as ctx:
        def sb(name, shape, dt=F32):
            return ctx.enter_context(nc.sbuf_tensor(name, shape, dt))

        cos = sb("cos_k", [P, COLS])
        sin = sb("sin_k", [P, COLS])
        swap = sb("swap_k", [P, P])
        vecs = sb("vecs", [P, FT, 11])
        decay = sb("decay", [P, FT, 2])
        ndecay = sb("ndecay", [P, FT, 2])
        sp_e = sb("sp_e", [P, FT, 2])
        sp_z = sb("sp_z", [P, FT, 2])
        sp_z2 = sb("sp_z2", [P, FT, 2])
        sp_p = sb("sp_p", [P, FT, 2])
        lam_pos = sb("lam_pos", [P, FT, 2])
        gates = sb("gates", [P, 4, P])
        ones = sb("ones_r", [P, 1])
        acc = sb("acc", [P, RW])
        r_g = [sb(f"r_g{d}", [P, RW]) for d in range(2)]
        i_g = [sb(f"i_g{d}", [P, RW]) for d in range(2)]
        t_g = [sb(f"t_g{d}", [P, RW]) for d in range(2)]
        a_g = [sb(f"a_g{d}", [P, RW]) for d in range(2)]
        a_sq = [sb(f"a_sq{d}", [P, RW]) for d in range(2)]
        h_g = [sb(f"h_g{d}", [P, RW]) for d in range(2)]
        square = sb("square", [P, REAL])
        rms_r = sb("rms_r", [P, NB])
        ssq_r = sb("ssq_r", [P, NB])
        SS = BANK // 2
        k_cos = h_g[0][:, 0:COLS]
        k_sin = h_g[1][:, 0:COLS]
        v_small = acc[0:META, 0:P]

        ps_r = ctx.enter_context(nc.psum_tensor("ps_r", [P, 3, BANK], F32))
        ps_i = ctx.enter_context(nc.psum_tensor("ps_i", [P, 3, BANK], F32))
        ps_s = ctx.enter_context(nc.psum_tensor("ps_s", [P, BANK], F32))
        flat_r = ps_r[:, :, :].rearrange("p b c -> p (b c)")
        flat_i = ps_i[:, :, :].rearrange("p b c -> p (b c)")

        tables_in = sem("r_tables_in")
        vecs_in = sem("r_vecs_in")
        gates_in = sem("r_gates_in")
        cleared = sem("r_cleared")
        vmeta_in = sem("r_vmeta_in")
        k_swapped = sem("r_k_swapped")
        v_turned = sem("r_v_turned")
        k_cos_done = sem("r_k_cos_done")
        k_sin_done = sem("r_k_sin_done")
        v_out = sem("r_v_out")
        v_out_dve = sem("r_v_out_dve")
        lam_e = sem("r_lam_e")
        lam_step = sem("r_lam_step")
        conv_step = sem("r_conv_step")
        conv_done = sem("r_conv_done")
        gates_done = sem("r_gates_done")
        r_done = sem("r_r_done")
        i_done = sem("r_i_done")
        ta_done = sem("r_ta_done")
        a_cut = sem("r_a_cut")
        v_done = sem("r_v_done")
        s_done = sem("r_s_done")
        ix_done = sem("r_ix_done")
        u_done = sem("r_u_done")
        scanned = sem("r_scanned")
        summed = sem("r_summed")
        rec_done = sem("r_rec_done")
        sq_done = sem("r_sq_done")
        ss_done = sem("r_ss_done")
        ss_summed = sem("r_ss_summed")
        rms_done = sem("r_rms_done")

        block = ctx.enter_context(nc.Block())

        def xc(ft):
            return xr[:, bass.ds(ft, 1), 0:RW].rearrange("p o c -> p (o c)")

        def vec(ft, j):
            return vecs[:, bass.ds(ft, 1), j:j + 1].rearrange("p o c -> p (o c)")

        @block.sync
        def _(sp):
            sp.dma_start(vecs[:, :, :], a["vecs"]).then_inc(vecs_in, 16)
            sp.dma_start(cos[:, :], a["cos"]).then_inc(tables_in, 16)
            sp.dma_start(sin[:, :], a["sin"]).then_inc(tables_in, 16)
            sp.dma_start(swap[:, :], a["swap"]).then_inc(tables_in, 16)

            def load_gates(ft):
                sp.wait_ge(gates_done, 4 * ft + 1)
                sp.dma_start(gates[:, :, :], a["gates"][bass.ds(ft, 1), :, :, :].rearrange("o p g c -> p (o g) c")
                             ).then_inc(gates_in, 16)

            load_gates(0)
            sp.wait_ge(v_out, 2)
            sp.wait_ge(cleared, 4)
            for h in range(HEADS):
                g = h // 4
                sp.dma_start(v_meta[h * META:(h + 1) * META, h * HD:(h + 1) * HD],
                             v_small[:, g * HD:(g + 1) * HD]).then_inc(vmeta_in, 16)
            with sp.Fori(1, FT) as ft:
                load_gates(ft)
            sp.wait_ge(vmeta_in, 16 * HEADS)

        @block.gpsimd
        def _(pool):
            pool.memset(k_rot[:, :], 0.0).then_inc(cleared, 1)
            pool.memset(v_tok[:, :], 0.0).then_inc(cleared, 1)
            pool.memset(v_meta[:, :], 0.0).then_inc(cleared, 1)
            pool.memset(ones[:, :], 1.0).then_inc(cleared, 1)
            pool.wait_ge(tables_in, 48)
            pool.tensor_tensor(k_cos, k_pre[:, :], cos[:, :], ALU.mult).then_inc(k_cos_done, 1)
            with pool.Fori(0, FT) as ft:
                pool.wait_ge(rec_done, 2 * ft + 2)
                pool.wait_ge(ss_done, ft + 1)
                r = yg[:, bass.ds(ft, 1), META:COLS].rearrange("p o c -> p (o c)")
                pool.tensor_tensor(square[:, :], r, r, ALU.mult).then_inc(sq_done, 1)

        @block.tensor
        def _(pe):
            pe.sem_inc(gates_done, 1)
            pe.sem_inc(ss_done, 1)
            pe.wait_ge(tables_in, 48)
            for c in range(NCH):
                mm = pe.matmul(ps_r[:, c, 0:CH], swap[:, :], k_pre[:, c * CH:(c + 1) * CH], start=True, stop=True)
            mm.then_inc(k_swapped, 1)
            for b in range(NB):
                mm = pe.transpose(ps_i[:, b // 4, (b % 4) * P:(b % 4 + 1) * P],
                                  v_pre[:, META + b * P:META + (b + 1) * P], ident[:, :])
            mm.then_inc(v_turned, 1)
            pe.transpose(ps_s[0:META, 0:P], v_pre[:, 0:META], ident[:, :]).then_inc(v_turned, 1)
            pe.wait_ge(k_sin_done, 1)
            pe.wait_ge(v_out, 2)

            def gate_products(ft):
                pe.wait_ge(gates_in, 16 * ft + 16)
                pe.wait_ge(conv_done, ft + 2)
                for d in range(2):
                    for ps, g, read in ((ps_r, 2 * d, r_done), (ps_i, 2 * d + 1, i_done)):
                        pe.wait_ge(read, 2 * ft + d + 1)
                        for c in range(3):
                            n = min(BANK, RW - c * BANK)
                            mm = pe.matmul(ps[:, c, 0:n], gates[:, g, :],
                                           xr[:, bass.ds(ft, 1), c * BANK:c * BANK + n].rearrange("p o c -> p (o c)"),
                                           start=True, stop=True)
                        mm.then_inc(gates_done, 1)

            def sum_squares(ft):
                pe.wait_ge(sq_done, ft + 1)
                for b in range(NB):
                    mm = pe.matmul(ps_s[:, bass.ds(ft * NB + SS + b, 1)], square[:, b * P:(b + 1) * P], ones[:, :],
                                   start=True, stop=True)
                mm.then_inc(ss_done, 1)

            gate_products(0)
            with pe.Fori(1, FT) as ft:
                gate_products(ft)
                sum_squares(ft - 1)
            sum_squares(FT - 1)

        @block.scalar
        def _(act):
            act.sem_inc(r_done, 1)
            act.sem_inc(i_done, 1)
            act.wait_ge(lam_step, 1)
            act.activation(sp_e[:, :, :], sp_z[:, :, :], ACT.Exp).then_inc(lam_e, 1)
            act.wait_ge(cleared, 4)
            act.wait_ge(v_turned, 2)
            act.activation(v_tok[:, P:(NB + 1) * P], flat_i[:, 0:REAL], ACT.Copy).then_inc(v_out, 1)
            act.activation(v_small, ps_s[0:META, 0:P], ACT.Copy).then_inc(v_out, 1)
            act.wait_ge(lam_step, LAM_STEPS)

            with act.Fori(0, FT) as ft:
                for d in range(2):
                    n = 2 * ft + d
                    act.wait_ge(scanned, n + 1)
                    act.wait_ge(gates_done, 4 * ft + 2 * d + 2)
                    act.activation(r_g[d][:, :], flat_r[:, 0:RW], ACT.Sigmoid, bias=vec(ft, 5 + 2 * d)).then_inc(r_done, 1)
                    act.wait_ge(gates_done, 4 * ft + 2 * d + 3)
                    act.activation(i_g[d][:, :], flat_i[:, 0:RW], ACT.Sigmoid, bias=vec(ft, 6 + 2 * d)).then_inc(i_done, 1)
                    act.wait_ge(r_done, n + 2)
                    dk = decay[:, bass.ds(ft, 1), d:d + 1].rearrange("p o c -> p (o c)")
                    ndk = ndecay[:, bass.ds(ft, 1), d:d + 1].rearrange("p o c -> p (o c)")
                    act.activation(t_g[d][:, :], r_g[d][:, :], ACT.Tanh, scale=dk).then_inc(ta_done, 1)
                    act.activation(a_g[d][:, :], r_g[d][:, :], ACT.Exp, scale=ndk).then_inc(ta_done, 1)
                    act.wait_ge(ta_done, 3 * n + 2)
                    act.activation(a_sq[d][:, :], a_g[d][:, :], ACT.Square).then_inc(ta_done, 1)
                    act.wait_ge(v_done, n + 1)
                    act.activation(r_g[d][:, :], t_g[d][:, :], ACT.Sqrt).then_inc(s_done, 1)
            act.wait_ge(ss_summed, 1)
            act.activation(rms_r[:, :], ssq_r[:, :], ACT.Sqrt, bias=eps_t[:, :], scale=1.0 / REC).then_inc(rms_done, 1)

        @block.vector
        def _(dve):
            dve.sem_inc(scanned, 2)
            dve.sem_inc(conv_done, 1)
            dve.wait_ge(vecs_in, 16)
            step = [0]

            def then(ins):
                step[0] += 1
                ins.then_inc(lam_step, 1)
                dve.wait_ge(lam_step, step[0])

            lam = vecs[:, :, 9:11]
            then(dve.scalar_tensor_tensor(out=sp_z[:, :, :], in0=lam, scalar=-1.0, in1=lam, op0=ALU.mult, op1=ALU.min))
            then(dve.tensor_scalar(lam_pos[:, :, :], lam, -1.0, 0.0, ALU.mult, ALU.max))
            dve.wait_ge(lam_e, 1)
            then(dve.tensor_scalar(sp_z2[:, :, :], sp_e[:, :, :], 2.0, None, ALU.add))
            then(dve.reciprocal(sp_p[:, :, :], sp_z2[:, :, :]))
            then(dve.tensor_tensor(sp_z[:, :, :], sp_e[:, :, :], sp_p[:, :, :], ALU.mult))
            then(dve.tensor_tensor(sp_z2[:, :, :], sp_z[:, :, :], sp_z[:, :, :], ALU.mult))
            then(dve.memset(sp_p[:, :, :], 1.0 / 17))
            for j in range(15, 0, -2):
                then(dve.tensor_tensor(sp_p[:, :, :], sp_p[:, :, :], sp_z2[:, :, :], ALU.mult))
                then(dve.tensor_scalar(sp_p[:, :, :], sp_p[:, :, :], 1.0 / j, None, ALU.add))
            then(dve.scalar_tensor_tensor(out=sp_p[:, :, :], in0=sp_p[:, :, :], scalar=2.0, in1=sp_z[:, :, :], op0=ALU.mult, op1=ALU.mult))
            then(dve.tensor_tensor(sp_p[:, :, :], sp_p[:, :, :], lam_pos[:, :, :], ALU.add))
            then(dve.tensor_scalar(decay[:, :, :], sp_p[:, :, :], 8.0, None, ALU.mult))
            then(dve.tensor_scalar(ndecay[:, :, :], sp_p[:, :, :], -8.0, None, ALU.mult))
            assert step[0] == LAM_STEPS

            dve.wait_ge(k_swapped, 1)
            for c in range(NCH):
                ins = dve.tensor_tensor(k_sin[:, c * CH:(c + 1) * CH], ps_r[:, c, 0:CH], sin[:, c * CH:(c + 1) * CH], ALU.mult)
            ins.then_inc(k_sin_done, 1)
            dve.wait_ge(k_sin_done, 1)
            dve.wait_ge(k_cos_done, 1)
            dve.wait_ge(cleared, 4)
            dve.tensor_tensor(k_rot[:, 0:META], k_cos[:, 0:META], k_sin[:, 0:META], ALU.add)
            dve.tensor_tensor(k_rot[:, META + P:META + P + REAL], k_cos[:, META:COLS], k_sin[:, META:COLS],
                              ALU.add).then_inc(k_sin_done, 1)
            dve.wait_ge(vmeta_in, 16 * HEADS)

            with dve.Fori(0, FT) as ft:
                def src(j):
                    return xr[:, bass.ds(ft, 1), j:j + RW].rearrange("p o c -> p (o c)")
                dve.wait_ge(conv_done, ft + 1)
                dve.tensor_scalar(acc[:, :], src(0), vec(ft, 0), vec(ft, 4), ALU.mult, ALU.add).then_inc(conv_step, 1)
                for j in range(1, 4):
                    dve.wait_ge(conv_step, 3 * ft + j)
                    dst = acc[:, :] if j < 3 else xc(ft)
                    dve.scalar_tensor_tensor(out=dst, in0=src(j), scalar=vec(ft, j), in1=acc[:, :], op0=ALU.mult,
                                             op1=ALU.add).then_inc(conv_step if j < 3 else conv_done, 1)

            with dve.Fori(0, FT) as ft:
                for d in range(2):
                    n = 2 * ft + d
                    dve.wait_ge(ta_done, 3 * n + 3)
                    dve.scalar_tensor_tensor(out=t_g[d][:, :], in0=a_sq[d][:, :], scalar=1.0, in1=t_g[d][:, :],
                                             op0=ALU.add, op1=ALU.mult).then_inc(v_done, 1)
                    cut = OFF1 if d == 0 else T0 - 1
                    dve.memset(a_g[d][:, cut:cut + 1], 0.0).then_inc(a_cut, 1)
                    dve.wait_ge(i_done, n + 2)
                    dve.wait_ge(conv_done, ft + 2)
                    dve.tensor_tensor(i_g[d][:, :], i_g[d][:, :], xc(ft), ALU.mult).then_inc(ix_done, 1)
                    dve.wait_ge(ix_done, n + 1)
                    dve.wait_ge(s_done, n + 1)
                    dve.tensor_tensor(i_g[d][:, :], i_g[d][:, :], r_g[d][:, :], ALU.mult).then_inc(u_done, 1)
                    dve.wait_ge(u_done, n + 1)
                    dve.wait_ge(a_cut, n + 1)
                    if d == 0:
                        dve.tensor_tensor_scan(h_g[0][:, :], a_g[0][:, :], i_g[0][:, :], 0.0, ALU.mult, ALU.add).then_inc(scanned, 1)
                    else:
                        dve.tensor_tensor_scan(h_g[1][:, ::-1], a_g[1][:, ::-1], i_g[1][:, ::-1], 0.0, ALU.mult,
                                               ALU.add).then_inc(scanned, 1)
                dve.wait_ge(scanned, 2 * ft + 4)
                dve.tensor_tensor(h_g[0][:, :], h_g[0][:, :], h_g[1][:, :], ALU.add).then_inc(summed, 1)
                dve.wait_ge(summed, ft + 1)
                for lo, hi, at in ((META, T0, META), (OFF1 + META, RW, T0)):
                    dst = yg[:, bass.ds(ft, 1), at:at + hi - lo].rearrange("p o c -> p (o c)")
                    dve.tensor_tensor(dst, dst, h_g[0][:, lo:hi], ALU.mult).then_inc(rec_done, 1)
            dve.wait_ge(ss_done, FT + 1)
            dve.tensor_reduce(ssq_r[:, :], ps_s[:, SS:SS + FT * NB].rearrange("p (f b) -> p b f", b=NB), AX.X,
                              ALU.add).then_inc(ss_summed, 1)
            dve.wait_ge(rms_done, 1)
            dve.reciprocal(rstd_rec[:, :], rms_r[:, :])


LAM_STEPS = 27


def mix(nc, sem, a, q_pre, rec, rstd_rec, k_rot, v_tok, v_meta, ident, eps_t, iota_e,
        gate1, gate2, expert1, expert2, place1, place2, counts, h2_dram, u_dram, list_dram):
    with ExitStack() as ctx:
        def sb(name, shape, dt=F32):
            return ctx.enter_context(nc.sbuf_tensor(name, shape, dt))

        w_hi = sb("wo_hi", [P, KD, D], F32R)
        w_lo = sb("wo_lo", [P, KD, D], F32R)
        g_out = sb("g_out", [P, KD])
        g_ffn = sb("g_ffn", [P, D])
        router = sb("router", [P, KD, ROUT])
        rbias = sb("rbias_bc", [P, ROUT])
        sink = sb("sink_bc", [P, HEADS])
        swap = sb("swap_q", [P, P])
        before = sb("before_sb", [P, P])
        ones = sb("ones_m", [P, P])
        group_of = sb("group_of", [P, EXP])
        token = sb("token", [P, NB], I32)
        mask = [sb(f"mask{s}", [P, KEYS]) for s in range(RING)]
        cos = [sb(f"cos_q{s}", [P, P]) for s in range(RING)]
        sin = [sb(f"sin_q{s}", [P, P]) for s in range(RING)]
        xh = [sb(f"xh{s}", [P, D]) for s in range(RING)]
        u = sb("u_sb", [P, D])
        q_cos = sb("q_cos", [P, ATTN])
        q_sin = sb("q_sin", [P, ATTN])
        qz = sb("qz", [P, HEADS, P])
        probs = sb("probs", [P, HEADS, KEYS])
        probs_t = sb("probs_t", [P, HEADS, WIN])
        meta_p = sb("meta_p", [P, P])
        meta_t = sb("meta_t", [P, P])
        smax = sb("smax", [P, HEADS])
        nmax = sb("nmax", [P, HEADS])
        rowsum = sb("rowsum", [P, HEADS])
        sink_d = sb("sink_d", [P, HEADS])
        sink_e = sb("sink_e", [P, HEADS])
        den = sb("den", [P, HEADS])
        rden = sb("rden", [P, HEADS])
        attn_o = sb("attn_o", [P, ATTN])
        junk = sb("junk", [P, ATTN])
        ssq_a = sb("ssq_a", [P, 1])
        rms_a = sb("rms_a", [P, 1])
        rstd_a = sb("rstd_a", [P, 1])
        a_hi = sb("a_hi", [P, FT, P], F32R)
        a_lo = sb("a_lo", [P, FT, P], F32R)
        r_hi = sb("rec_hi", [P, FT, P], F32R)
        r_lo = sb("rec_lo", [P, FT, P], F32R)
        ssq_h = sb("ssq_h", [P, 1])
        rms_h = sb("rms_h", [P, 1])
        rstd_h = sb("rstd_h", [P, 1])
        u_t = sb("u_t", [P, KD, P])
        logits = sb("logits", [P, ROUT])
        gtop = sb("gtop", [P, 8])
        gidx = sb("gidx", [P, 8], U32)
        gidx_f = sb("gidx_f", [P, 1])
        ngtop = sb("ngtop", [P, 1])
        gexp = sb("gexp", [P, 4])
        gsum = sb("gsum", [P, 1])
        mlog = sb("mlog", [P, EXP])
        etop = sb("etop", [P, 8])
        eidx = sb("eidx", [P, 8], U32)
        ediff = sb("ediff", [P, 1])
        eexp = sb("eexp", [P, 1])
        gden = sb("gden", [P, 1])
        hot1 = sb("hot1", [P, EXP])
        hot2 = sb("hot2", [P, EXP])
        hot = sb("hot", [P, EXP])
        base = sb("base", [P, EXP])
        prod = [sb(f"prod{j}", [P, EXP]) for j in range(2)]
        token_s = [sb(f"token_s{s}", [P, 1], I32) for s in range(RING)]
        addr = [[sb(f"addr{j}{s}", [P, 1], I32) for s in range(RING)] for j in range(2)]

        ps_sc = [ctx.enter_context(nc.psum_tensor(f"ps_sc{s}", [P, BANK], F32)) for s in range(2)]
        ps_t = [ctx.enter_context(nc.psum_tensor(f"ps_t{s}", [P, BANK], F32)) for s in range(2)]
        ps_o = ctx.enter_context(nc.psum_tensor("ps_o", [P, BANK], F32))
        ps_y = [ctx.enter_context(nc.psum_tensor(f"ps_y{s}", [P, BANK], F32)) for s in range(2)]
        ps_x = ctx.enter_context(nc.psum_tensor("ps_x", [P, BANK], F32))

        waited = sem("m_waited")
        consts_in = sem("m_consts_in")
        w_in = [sem(f"m_w_in{s}") for s in range(RING)]
        w_hi_done = sem("m_w_hi_done")
        w_lo_done = sem("m_w_lo_done")
        cleared = sem("m_cleared")
        tables_in = [sem(f"m_tables_in{s}") for s in range(RING)]
        x_in = [sem(f"m_x_in{s}") for s in range(RING)]
        h2_out = sem("m_h2_out")
        u_out = sem("m_u_out")
        q_swapped = sem("m_q_swapped")
        q_cos_done = sem("m_q_cos_done")
        q_sin_done = sem("m_q_sin_done")
        qz_done = sem("m_qz_done")
        scored = sem("m_scored")
        scaled = sem("m_scaled")
        nmax_done = sem("m_nmax_done")
        exp_done = sem("m_exp_done")
        sink_d_done = sem("m_sink_d_done")
        sink_e_done = sem("m_sink_e_done")
        turned = sem("m_turned")
        pt_out = sem("m_pt_out")
        meta_packed = sem("m_meta_packed")
        meta_turned = sem("m_meta_turned")
        meta_out = sem("m_meta_out")
        av_done = sem("m_av_done")
        den_done = sem("m_den_done")
        ao_done = sem("m_ao_done")
        ssq_a_done = sem("m_ssq_a_done")
        rms_a_done = sem("m_rms_a_done")
        rstd_a_done = sem("m_rstd_a_done")
        ao_turned = sem("m_ao_turned")
        a_hi_done = sem("m_a_hi_done")
        a_lo_done = sem("m_a_lo_done")
        r_hi_done = sem("m_r_hi_done")
        r_lo_done = sem("m_r_lo_done")
        y_done = sem("m_y_done")
        y_read = sem("m_y_read")
        ssq_h_done = sem("m_ssq_h_done")
        rms_h_done = sem("m_rms_h_done")
        rstd_h_done = sem("m_rstd_h_done")
        u_done = sem("m_u_done")
        u_turned = sem("m_u_turned")
        u_t_out = sem("m_u_t_out")
        logits_done = sem("m_logits_done")
        route_step = sem("m_route_step")
        gexp_done = sem("m_gexp_done")
        eexp_done = sem("m_eexp_done")
        ranked = sem("m_ranked")
        place_step = sem("m_place_step")
        token_done = sem("m_token_done")
        addr_done = sem("m_addr_done")
        listed = [sem(f"m_listed{s}") for s in range(RING)]

        AT_LOGITS, AT_NGTOP, AT_EDIFF, AT_HOT, ROUTE_STEPS = 1, 5, 9, 18, 18
        PLACE_STEPS = 8
        PLACE0 = 2 * PLACE_STEPS

        block = ctx.enter_context(nc.Block())

        def schedule(attn, route, outer, place, finish):
            def step(t, b1, b2, s):
                if not isinstance(t, int) or t < NB:
                    attn(t, s)
                if b2 is not None:
                    route(b2, s)
                if b1 is not None:
                    outer(b1, 1 - s)
                if b2 is not None:
                    place(b2, s)
                if not isinstance(t, int) or t < NB:
                    finish(t, s)
            return step

        def run(eng, step, peeled=0):
            step(0, None, None, 0)
            step(1, 0, None, 1)
            with eng.Fori(0, (NB - peeled) // 2 - 1) as i:
                step(2 * i + 2, 2 * i + 1, 2 * i, 0)
                step(2 * i + 3, 2 * i + 2, 2 * i + 1, 1)
            for t in range(NB - peeled, NB):
                step(t, t - 1, t - 2, t % 2)
            step(NB, NB - 1, NB - 2, 0)
            step(NB + 1, None, NB - 1, 1)

        def take_waits(eng):
            eng.sem_inc(waited, 1)

        def nothing(b, s):
            pass

        def at_most_blocks(v):
            return min(v, NB) if isinstance(v, int) else v

        def half(i):
            return slice(i * BANK, (i + 1) * BANK)

        @block.sync
        def _(sp):
            for dst, src in ((g_out[:, :], a["g_out"]), (g_ffn[:, :], a["ln_ffn_g"][0].partition_broadcast(P)),
                             (router[:, :, :], a["router"]), (rbias[:, :], a["rbias"][0].partition_broadcast(P)),
                             (sink[:, :], a["sink"][0].partition_broadcast(P)), (swap[:, :], a["swap"]),
                             (before[:, :], a["before"])):
                sp.dma_start(dst, src).then_inc(consts_in, 16)

            def tables(t, s):
                sp.dma_start(mask[s][:, :], a["masks"][bass.ds(t, 1), :, :].rearrange("o p c -> (o p) c")).then_inc(tables_in[s], 16)
                sp.dma_start(cos[s][:, :], a["cos"][:, bass.ds(META + t * P, P)]).then_inc(tables_in[s], 16)
                sp.dma_start(sin[s][:, :], a["sin"][:, bass.ds(META + t * P, P)]).then_inc(tables_in[s], 16)

            def load_x(t, s):
                sp.dma_start(xh[s][:, :], a["x"][bass.ds(t * P, P), :]).then_inc(x_in[s], 16)

            tables(0, 0)
            for k in range(KD):
                if k >= RING:
                    sp.wait_ge(w_lo_done, k - RING + 1)
                sp.dma_start(xh[k % RING][:, :], a["w_out"][:, k, :]).then_inc(w_in[k % RING], 16)
            sp.wait_ge(w_lo_done, KD)
            load_x(0, 0)

            def attn(t, s):
                if isinstance(t, int) and t == 0:
                    tables(1, 1)
                    return
                if isinstance(t, int) and t == NB - 1:
                    return
                sp.wait_ge(nmax_done, 2 * t)
                sp.wait_ge(q_cos_done, t)
                sp.wait_ge(q_sin_done, t)
                tables(t + 1, 1 - s)

            def outer(b, s):
                sp.wait_ge(u_done, b + 1)
                sp.dma_start(h2_dram[bass.ds(b * P, P), :], xh[s][:, :]).then_inc(h2_out, 16)
                sp.dma_start(u_dram[bass.ds(b * P, P), :], u[:, :]).then_inc(u_out, 16)
                sp.wait_ge(h2_out, 16 * b + 16)
                if not isinstance(b, int) or b + 2 < NB:
                    load_x(b + 2, s)

            load_x(1, 1)
            run(sp, schedule(attn, nothing, outer, nothing, nothing), peeled=2)
            sp.wait_ge(u_out, 16 * NB)
            for s in range(RING):
                sp.wait_ge(listed[s], 32 * NB // 2)

        @block.gpsimd
        def _(pool):
            pool.memset(qz[:, :, :], 0.0).then_inc(cleared, 1)
            pool.memset(ones[:, :], 1.0).then_inc(cleared, 1)
            pool.memset(counts[:, :], 0.0).then_inc(cleared, 1)
            pool.iota(group_of[:, :], pattern=[[1, 4], [0, 8]], base=0, channel_multiplier=0,
                      allow_small_or_imprecise_dtypes=True).then_inc(cleared, 1)
            pool.iota(token[:, :], pattern=[[P, NB]], base=0, channel_multiplier=1).then_inc(cleared, 1)
            pool.wait_ge(cleared, 5)

            def attn(t, s):
                pool.wait_ge(tables_in[s], 48 * (t // 2 + 1) if isinstance(t, int) else 24 * (t - s) + 48)
                pool.wait_ge(qz_done, t + 1)
                pool.tensor_tensor(q_cos[:, :].rearrange("p (h c) -> p h c", c=P), q_pre[:, :, bass.ds(META + t * P, P)],
                                   cos[s][:, :].unsqueeze(1).to_broadcast([P, 4, P]), ALU.mult).then_inc(q_cos_done, 1)
                pool.wait_ge(exp_done, HEADS * t + HEADS)
                pool.wait_ge(meta_turned, t) if not isinstance(t, int) or t > 0 else None
                take_waits(pool)
                pool.tensor_copy(meta_p[:, :].rearrange("p (h m) -> p h m", m=META), probs[:, :, WIN:KEYS]).then_inc(meta_packed, 1)

            def outer(b, s):
                pool.wait_ge(r_hi_done, b + 1)
                pool.tensor_tensor(r_lo[:, :, :], rec[:, :, bass.ds(b * P, P)], r_hi[:, :, :].bitcast(F32),
                                   ALU.subtract).then_inc(r_lo_done, 1)

            def place(b, s):
                pool.wait_ge(addr_done, 2 * b + 2)
                if not isinstance(b, int) or b >= 2:
                    pool.wait_ge(listed[s], 16 * (b - s))
                take_waits(pool)
                pool.tensor_copy(token_s[s][:, :], token[:, bass.ds(b, 1)]).then_inc(token_done, 1)
                pool.wait_ge(token_done, b + 1)
                take_waits(pool)
                for j in range(2):
                    pool.indirect_dma_start(list_dram, bass.IndirectOffsetOnAxis(ap=addr[j][s][:, 0:1], axis=0),
                                            token_s[s][:, 0:1], None).then_inc(listed[s], 16)

            run(pool, schedule(attn, nothing, outer, place, nothing))

        @block.tensor
        def _(pe):
            pe.wait_ge(consts_in, 112)
            pe.wait_ge(cleared, 5)
            pe.sem_inc(av_done, 1)
            pe.sem_inc(logits_done, 1)

            def attn(t, s):
                pe.wait_ge(a_lo_done, t + 1)
                if not isinstance(t, int) or t >= 2:
                    pe.wait_ge(place_step, PLACE_STEPS * t - PLACE_STEPS + 2)
                pe.matmul(ps_x[:, :], swap[:, :], q_pre[:, :, bass.ds(META + t * P, P)], start=True, stop=True
                          ).then_inc(q_swapped, 1)
                pe.wait_ge(qz_done, t + 2)
                for h in range(HEADS):
                    n = HEADS * t + h
                    pe.wait_ge(scaled, n + 1)
                    pe.matmul(ps_sc[h % 2][:, 0:WIN], qz[:, h, :], k_rot[:, bass.ds(META + t * P, WIN)], start=True, stop=True,
                              skip_group_check=True)
                    pe.matmul(ps_sc[h % 2][:, WIN:KEYS], qz[:, h, :], k_rot[:, 0:META], start=True, stop=True,
                              skip_group_check=True).then_inc(scored, 1)
                for h in range(HEADS):
                    n = HEADS * t + h
                    pe.wait_ge(exp_done, n + 1)
                    pe.wait_ge(pt_out, n + 1)
                    for j in range(3):
                        mm = pe.transpose(ps_t[h % 2][:, j * P:(j + 1) * P], probs[:, h, j * P:(j + 1) * P], ident[:, :])
                    mm.then_inc(turned, 1)
                pe.wait_ge(ao_done, t + 1)
                pe.wait_ge(meta_packed, t + 1)
                pe.transpose(ps_o[:, 0:P], meta_p[:, :], ident[:, :]).then_inc(meta_turned, 1)
                pe.wait_ge(meta_out, t + 1)
                pe.matmul(ps_o[:, :], meta_t[:, :], v_meta[:, :], start=True, stop=False, skip_group_check=True)
                for h in range(HEADS):
                    pe.wait_ge(pt_out, HEADS * t + h + 3)
                    for j in range(3):
                        last = h == HEADS - 1 and j == 2
                        mm = pe.matmul(ps_o[:, h * HD:(h + 1) * HD], probs_t[:, h, j * P:(j + 1) * P],
                                       v_tok[:, bass.ds(t * P + j * P + (h // 4) * HD, HD)], start=False, stop=last,
                                       skip_group_check=True)
                mm.then_inc(av_done, 1)

            def route(b, s):
                pe.wait_ge(u_done, b + 1)
                for i in range(2):
                    if i == 0:
                        pe.wait_ge(q_sin_done, at_most_blocks(b + 3))
                        if isinstance(b, int) and b >= NB - 2:
                            pe.wait_ge(place_step, PLACE_STEPS * (b - 1) + PLACE0 + 2)
                    else:
                        pe.wait_ge(u_t_out, 2 * b + 3)
                    for k in range(4):
                        mm = pe.transpose(ps_x[:, k * P:(k + 1) * P], u[:, (4 * i + k) * P:(4 * i + k + 1) * P], ident[:, :])
                    mm.then_inc(u_turned, 1)
                pe.wait_ge(u_t_out, 2 * b + 4)
                for k in range(KD):
                    mm = pe.matmul(ps_x[:, 0:ROUT], u_t[:, k, :], router[:, k, :], start=(k == 0), stop=(k == KD - 1))
                mm.then_inc(logits_done, 1)

            def outer(b, s):
                pe.wait_ge(ao_done, b + 2)
                pe.wait_ge(route_step, ROUTE_STEPS * b - ROUTE_STEPS + AT_LOGITS) if not isinstance(b, int) or b > 0 else None
                for k in range(FT):
                    mm = pe.transpose(ps_x[:, k * P:(k + 1) * P], attn_o[:, k * P:(k + 1) * P], ident[:, :])
                mm.then_inc(ao_turned, 1)
                if isinstance(b, int) and b == 0:
                    pe.wait_ge(w_lo_done, KD)
                for part, (x_hi, x_lo, k0) in enumerate(((a_hi, a_lo, 0), (r_hi, r_lo, FT))):
                    if part == 0:
                        pe.wait_ge(a_lo_done, b + 3)
                    else:
                        pe.wait_ge(r_lo_done, b + 1)
                    for i in range(2):
                        pe.wait_ge(y_read, 4 * b + 2 * part + i + 1)
                        for k in range(FT):
                            for n, (x, w) in enumerate(((x_hi, w_hi), (x_hi, w_lo), (x_lo, w_hi))):
                                mm = pe.matmul(ps_y[i][:, :], x[:, k, :], w[:, k0 + k, half(i)],
                                               start=(k == 0 and n == 0), stop=(k == FT - 1 and n == 2))
                        mm.then_inc(y_done, 1)

            def place(b, s):
                pe.wait_ge(route_step, ROUTE_STEPS * b + AT_HOT)
                pe.wait_ge(a_lo_done, at_most_blocks(b + 2) + 2)
                pe.matmul(ps_x[:, 0:EXP], before[:, :], hot[:, :], start=True, stop=True)
                pe.matmul(ps_x[:, EXP:2 * EXP], ones[:, :], hot[:, :], start=True, stop=True).then_inc(ranked, 1)

            run(pe, schedule(attn, route, outer, place, nothing))

        @block.scalar
        def _(act):
            act.wait_ge(consts_in, 112)
            for k in range(KD):
                act.wait_ge(w_in[k % RING], 16 * (k // RING + 1))
                act.activation(w_hi[:, k, :], xh[k % RING][:, :], ACT.Copy, scale=g_out[:, k:k + 1]).then_inc(w_hi_done, 1)

            def attn(t, s):
                for h in range(HEADS):
                    if h % 4 == 0:
                        act.wait_ge(nmax_done, 2 * t + h // 4 + 1)
                    if h == 0:
                        act.wait_ge(den_done, 2 * t + 1)
                    act.activation(probs[:, h, :], probs[:, h, :], ACT.Exp, bias=nmax[:, h:h + 1],
                                   accum_out=rowsum[:, h:h + 1]).then_inc(exp_done, 1)
                act.wait_ge(sink_d_done, t + 1)
                act.activation(sink_e[:, :], sink_d[:, :], ACT.Exp).then_inc(sink_e_done, 1)
                for h in range(HEADS):
                    act.wait_ge(turned, HEADS * t + h + 1)
                    if h == 0:
                        act.wait_ge(av_done, t + 1)
                    act.activation(probs_t[:, h, :], ps_t[h % 2][:, 0:WIN], ACT.Copy).then_inc(pt_out, 1)
                act.wait_ge(meta_turned, t + 1)
                act.activation(meta_t[:, :], ps_o[:, 0:P], ACT.Copy).then_inc(meta_out, 1)

            def route(b, s):
                act.wait_ge(logits_done, b + 1)
                for i in range(2):
                    act.wait_ge(u_turned, 2 * b + i + 1)
                    act.activation(u_t[:, 4 * i:4 * i + 4, :], ps_x[:, :].rearrange("p (k c) -> p k c", c=P), ACT.Copy
                                   ).then_inc(u_t_out, 1)
                act.wait_ge(route_step, ROUTE_STEPS * b + AT_NGTOP)
                act.activation(gexp[:, :], logits[:, 0:4], ACT.Exp, bias=ngtop[:, :], accum_out=gsum[:, :]).then_inc(gexp_done, 1)
                act.wait_ge(route_step, ROUTE_STEPS * b + AT_EDIFF)
                act.activation(eexp[:, :], ediff[:, :], ACT.Exp).then_inc(eexp_done, 1)

            def outer(b, s):
                if not isinstance(b, int) or b > 0:
                    act.wait_ge(y_done, 4 * b)
                    act.wait_ge(r_lo_done, b)
                act.activation(r_hi[:, :, :], rec[:, :, bass.ds(b * P, P)], ACT.Copy).then_inc(r_hi_done, 1)
                act.wait_ge(ao_turned, b + 1)
                act.activation(a_hi[:, :, :], ps_x[:, :].rearrange("p (k c) -> p k c", c=P), ACT.Copy).then_inc(a_hi_done, 1)
                act.wait_ge(y_read, 4 * b + 6)
                if not isinstance(b, int) or b > 0:
                    act.wait_ge(u_turned, 2 * b)
                    act.wait_ge(u_out, 16 * b)
                    act.wait_ge(rms_h_done, b)
                act.activation(u[:, :], xh[s][:, :], ACT.Square, accum_out=ssq_h[:, :]).then_inc(ssq_h_done, 1)
                act.wait_ge(ssq_h_done, b + 1)
                act.wait_ge(rstd_h_done, b) if not isinstance(b, int) or b > 0 else None
                act.activation(rms_h[:, :], ssq_h[:, :], ACT.Sqrt, bias=eps_t[:, :], scale=1.0 / D).then_inc(rms_h_done, 1)

            def finish(t, s):
                act.wait_ge(ao_done, t + 2)
                if not isinstance(t, int) or t > 0:
                    act.wait_ge(ssq_a_done, t)
                    act.wait_ge(rms_a_done, t)
                act.activation(junk[:, :], attn_o[:, :], ACT.Square, accum_out=ssq_a[:, :]).then_inc(ssq_a_done, 1)
                act.wait_ge(ssq_a_done, t + 1)
                act.wait_ge(rstd_a_done, t) if not isinstance(t, int) or t > 0 else None
                act.activation(rms_a[:, :], ssq_a[:, :], ACT.Sqrt, bias=eps_t[:, :], scale=1.0 / ATTN).then_inc(rms_a_done, 1)

            act.sem_inc(u_t_out, 2)
            act.sem_inc(pt_out, 2)
            run(act, schedule(attn, route, outer, nothing, finish))

        @block.vector
        def _(dve):
            dve.sem_inc(a_lo_done, 2)
            dve.sem_inc(scaled, 2)
            dve.sem_inc(place_step, PLACE0)
            dve.sem_inc(ao_done, 1)
            dve.sem_inc(qz_done, 1)
            dve.sem_inc(den_done, 1)
            dve.sem_inc(y_read, 2)
            dve.wait_ge(consts_in, 112)
            for k in range(KD):
                dve.wait_ge(w_hi_done, k + 1)
                dve.scalar_tensor_tensor(out=w_lo[:, k, :], in0=xh[k % RING][:, :], scalar=g_out[:, k:k + 1],
                                         in1=w_hi[:, k, :].bitcast(F32), op0=ALU.mult, op1=ALU.subtract).then_inc(w_lo_done, 1)
            dve.wait_ge(cleared, 5)

            def attn(t, s):
                dve.wait_ge(q_swapped, t + 1)
                dve.wait_ge(tables_in[s], 48 * (t // 2 + 1) if isinstance(t, int) else 24 * (t - s) + 48)
                dve.wait_ge(qz_done, t + 1)
                dve.tensor_tensor(q_sin[:, :].rearrange("p (h c) -> p h c", c=P), ps_x[:, :].rearrange("p (h c) -> p h c", c=P),
                                  sin[s][:, :].unsqueeze(1).to_broadcast([P, 4, P]), ALU.mult).then_inc(q_sin_done, 1)
                dve.wait_ge(q_sin_done, t + 1)
                dve.wait_ge(q_cos_done, t + 1)
                dve.wait_ge(scored, HEADS * t) if not isinstance(t, int) or t > 0 else None
                dve.tensor_tensor(qz[0:HD, 0:4, :], q_cos[0:HD, :].rearrange("p (h c) -> p h c", c=P),
                                  q_sin[0:HD, :].rearrange("p (h c) -> p h c", c=P), ALU.add)
                dve.tensor_tensor(qz[HD:P, 4:8, :], q_cos[HD:P, :].rearrange("p (h c) -> p h c", c=P),
                                  q_sin[HD:P, :].rearrange("p (h c) -> p h c", c=P), ALU.add).then_inc(qz_done, 1)
                for h in range(HEADS):
                    n = HEADS * t + h
                    dve.wait_ge(scored, n + 1)
                    if h == 0:
                        if not isinstance(t, int) or t > 0:
                            dve.wait_ge(meta_turned, t)
                            dve.wait_ge(exp_done, HEADS * t)
                            dve.wait_ge(sink_d_done, t)
                            dve.wait_ge(nmax_done, 2 * t)
                    take_waits(dve)
                    dve.tensor_tensor_reduce(probs[:, h, :], ps_sc[h % 2][:, 0:KEYS], mask[s][:, :], HD ** -0.5, sink[:, h:h + 1],
                                             ALU.add, ALU.max, smax[:, h:h + 1]).then_inc(scaled, 1)
                    if h % 4 == 3:
                        dve.wait_ge(scaled, n + 3)
                        dve.tensor_scalar(nmax[:, h - 3:h + 1], smax[:, h - 3:h + 1], -1.0, None, ALU.mult).then_inc(nmax_done, 1)
                dve.wait_ge(nmax_done, 2 * t + 2)
                dve.wait_ge(sink_e_done, t) if not isinstance(t, int) or t > 0 else None
                dve.tensor_tensor(sink_d[:, :], sink[:, :], nmax[:, :], ALU.add).then_inc(sink_d_done, 1)

            def route(b, s):
                n = [0]

                def then(ins):
                    n[0] += 1
                    ins.then_inc(route_step, 1)
                    dve.wait_ge(route_step, ROUTE_STEPS * b + n[0])

                dve.wait_ge(logits_done, b + 2)
                if not isinstance(b, int) or b > 0:
                    dve.wait_ge(ranked, b)
                    dve.wait_ge(gexp_done, b)
                    dve.wait_ge(place_step, PLACE_STEPS * b + PLACE0)
                here = bass.ds(b, 1)
                then(dve.tensor_tensor(logits[:, :], ps_x[:, 0:ROUT], rbias[:, :], ALU.add))
                take_waits(dve)
                then(dve.max(gtop[:, :], logits[:, 0:8]))
                take_waits(dve)
                then(dve.max_index(gidx[:, :], gtop[:, :], logits[:, 0:8]))
                then(dve.tensor_copy(gidx_f[:, :], gidx[:, 0:1]))
                then(dve.tensor_scalar(ngtop[:, :], gtop[:, 0:1], -1.0, None, ALU.mult))
                assert n[0] == AT_NGTOP
                then(dve.tensor_scalar(mlog[:, :], group_of[:, :], gidx_f[:, 0:1], NEG, ALU.not_equal, ALU.mult))
                then(dve.tensor_tensor(mlog[:, :], mlog[:, :], logits[:, 8:ROUT], ALU.add))
                take_waits(dve)
                then(dve.max(etop[:, :], mlog[:, :]))
                then(dve.tensor_tensor(ediff[:, :], etop[:, 1:2], etop[:, 0:1], ALU.subtract))
                assert n[0] == AT_EDIFF
                take_waits(dve)
                then(dve.max_index(eidx[:, :], etop[:, :], mlog[:, :]))
                then(dve.tensor_copy(expert1[:, here], eidx[:, 0:1]))
                then(dve.tensor_copy(expert2[:, here], eidx[:, 1:2]))
                dve.wait_ge(gexp_done, b + 1)
                dve.wait_ge(eexp_done, b + 1)
                then(dve.scalar_tensor_tensor(out=gden[:, :], in0=eexp[:, :], scalar=1.0, in1=gsum[:, :], op0=ALU.add, op1=ALU.mult))
                then(dve.reciprocal(gate1[:, here], gden[:, :]))
                then(dve.tensor_tensor(gate2[:, here], gate1[:, here], eexp[:, :], ALU.mult))
                then(dve.tensor_scalar(hot1[:, :], iota_e[:, :], expert1[:, here], None, ALU.is_equal))
                then(dve.tensor_scalar(hot2[:, :], iota_e[:, :], expert2[:, here], None, ALU.is_equal))
                then(dve.tensor_tensor(hot[:, :], hot1[:, :], hot2[:, :], ALU.add))
                assert n[0] == ROUTE_STEPS

            def outer(b, s):
                dve.wait_ge(a_hi_done, b + 1)
                dve.wait_ge(rms_a_done, b + 1)
                dve.wait_ge(y_done, 4 * b) if not isinstance(b, int) or b > 0 else None
                dve.wait_ge(y_read, 4 * b + 2)
                dve.reciprocal(rstd_a[:, :], rms_a[:, :]).then_inc(rstd_a_done, 1)
                dve.tensor_tensor(a_lo[:, :, :], ps_x[:, :].rearrange("p (k c) -> p k c", c=P), a_hi[:, :, :].bitcast(F32),
                                  ALU.subtract).then_inc(a_lo_done, 1)
                dve.wait_ge(rstd_a_done, b + 1)
                dve.wait_ge(x_in[s], 16 * (b // 2 + 1) if isinstance(b, int) else 8 * (b - s) + 16)
                for i in range(2):
                    dve.wait_ge(y_done, 4 * b + i + 1)
                    dve.scalar_tensor_tensor(out=xh[s][:, half(i)], in0=ps_y[i][:, :], scalar=rstd_a[:, 0:1], in1=xh[s][:, half(i)],
                                             op0=ALU.mult, op1=ALU.add).then_inc(y_read, 1)
                for i in range(2):
                    dve.wait_ge(y_done, 4 * b + i + 3)
                    dve.wait_ge(y_read, 4 * b + i + 3)
                    dve.scalar_tensor_tensor(out=xh[s][:, half(i)], in0=ps_y[i][:, :], scalar=rstd_rec[:, bass.ds(b, 1)],
                                             in1=xh[s][:, half(i)], op0=ALU.mult, op1=ALU.add).then_inc(y_read, 1)
                dve.wait_ge(rms_h_done, b + 1)
                dve.wait_ge(u_done, b) if not isinstance(b, int) or b > 0 else None
                dve.reciprocal(rstd_h[:, :], rms_h[:, :]).then_inc(rstd_h_done, 1)
                dve.wait_ge(rstd_h_done, b + 1)
                dve.scalar_tensor_tensor(out=u[:, :], in0=xh[s][:, :], scalar=rstd_h[:, 0:1], in1=g_ffn[:, :],
                                         op0=ALU.mult, op1=ALU.mult).then_inc(u_done, 1)

            def place(b, s):
                n = [0]

                def then(ins):
                    n[0] += 1
                    ins.then_inc(place_step, 1)
                    dve.wait_ge(place_step, PLACE_STEPS * b + PLACE0 + n[0])

                dve.wait_ge(ranked, b + 1)
                if not isinstance(b, int) or b >= 2:
                    dve.wait_ge(listed[s], 16 * (b - s))
                here = bass.ds(b, 1)
                then(dve.tensor_tensor(base[:, :], ps_x[:, 0:EXP], counts[:, :], ALU.add))
                then(dve.tensor_tensor(counts[:, :], counts[:, :], ps_x[:, EXP:2 * EXP], ALU.add))
                for j, (hot_j, place_j, expert_j) in enumerate(((hot1, place1, expert1), (hot2, place2, expert2))):
                    then(dve.tensor_tensor(prod[j][:, :], base[:, :], hot_j[:, :], ALU.mult))
                    then(dve.tensor_reduce(place_j[:, here], prod[j][:, :], AX.X, ALU.add))
                    then(dve.scalar_tensor_tensor(out=gden[:, :], in0=expert_j[:, here], scalar=float(LIST), in1=place_j[:, here],
                                                  op0=ALU.mult, op1=ALU.add))
                    dve.tensor_copy(addr[j][s][:, :], gden[:, :]).then_inc(addr_done, 1)
                    dve.wait_ge(addr_done, 2 * b + j + 1)
                assert n[0] == PLACE_STEPS

            def finish(t, s):
                dve.wait_ge(exp_done, HEADS * t + HEADS)
                dve.wait_ge(sink_e_done, t + 1)
                dve.wait_ge(den_done, 2 * t + 1)
                dve.tensor_tensor(den[:, :], rowsum[:, :], sink_e[:, :], ALU.add).then_inc(den_done, 1)
                dve.wait_ge(den_done, 2 * t + 2)
                dve.wait_ge(ao_done, t + 1)
                dve.reciprocal(rden[:, :], den[:, :]).then_inc(den_done, 1)
                dve.wait_ge(den_done, 2 * t + 3)
                dve.wait_ge(av_done, t + 2)
                if not isinstance(t, int) or t > 0:
                    dve.wait_ge(ao_turned, t)
                    dve.wait_ge(ssq_a_done, t)
                dve.tensor_tensor(attn_o[:, :].rearrange("p (h c) -> p h c", c=HD), ps_o[:, :].rearrange("p (h c) -> p h c", c=HD),
                                  rden[:, :].unsqueeze(2).to_broadcast([P, HEADS, HD]), ALU.mult).then_inc(ao_done, 1)

            run(dve, schedule(attn, route, outer, place, finish))


PLAN_STEPS = 31


def plan(nc, sem, iota_e, counts, expert1, expert2, place1, place2, slots, table, table_dram):
    with ExitStack() as ctx:
        def sb(name, shape, dt=F32):
            return ctx.enter_context(nc.sbuf_tensor(name, shape, dt))

        ones = sb("p_ones", [P, EXP])
        blocks_i = sb("blocks_i", [P, EXP], I32)
        blocks = sb("blocks", [P, EXP])
        block_end = sb("block_end", [P, EXP])
        count_end = sb("count_end", [P, EXP])
        start = sb("start", [P, EXP])
        n_col = sb("n_col", [P, 1])
        before_n = sb("before_n", [P, EXP])
        weighed = sb("weighed", [P, EXP])
        n_experts = sb("n_experts", [P, 1])
        n_blocks = sb("n_blocks", [P, 1])
        n_tokens = sb("n_tokens", [P, 1])
        offset = sb("offset", [P, 1])
        row = sb("row", [P, 4])
        row_i = sb("row_i", [P, 4], I32)
        pairs_i = sb("pairs_i", [P, 1], I32)
        hot = sb("p_hot", [P, NB, EXP])
        slot_f = sb("slot_f", [P, NB])

        set_up = sem("p_set_up")
        step = sem("p_step")
        table_out = sem("p_table_out")
        table_in = sem("p_table_in")
        block = ctx.enter_context(nc.Block())

        @block.gpsimd
        def _(pool):
            pool.memset(ones[:, :], 1.0).then_inc(set_up, 1)
            pool.iota(n_col[:, :], pattern=[[0, 1]], base=0, channel_multiplier=1,
                      allow_small_or_imprecise_dtypes=True).then_inc(set_up, 1)

        @block.vector
        def _(dve):
            n = [0]

            def then(ins):
                n[0] += 1
                ins.then_inc(step, 1)
                dve.wait_ge(step, n[0])

            dve.wait_ge(set_up, 2)
            then(dve.tensor_scalar(blocks_i[:, :], counts[:, :], float(P - 1), None, ALU.add))
            then(dve.tensor_single_scalar(blocks_i[:, :], blocks_i[:, :], P.bit_length() - 1, ALU.arith_shift_right))
            then(dve.tensor_copy(blocks[:, :], blocks_i[:, :]))
            then(dve.tensor_tensor_scan(block_end[:, :], ones[:, :], blocks[:, :], 0.0, ALU.mult, ALU.add))
            then(dve.tensor_tensor_scan(count_end[:, :], ones[:, :], counts[:, :], 0.0, ALU.mult, ALU.add))
            then(dve.tensor_tensor(start[:, :], count_end[:, :], counts[:, :], ALU.subtract))
            then(dve.tensor_scalar(before_n[:, :], block_end[:, :], n_col[:, 0:1], None, ALU.is_le))
            then(dve.tensor_reduce(n_experts[:, :], before_n[:, :], AX.X, ALU.add))
            for total, each in ((n_blocks, blocks), (n_tokens, counts)):
                then(dve.tensor_tensor(weighed[:, :], before_n[:, :], each[:, :], ALU.mult))
                then(dve.tensor_reduce(total[:, :], weighed[:, :], AX.X, ALU.add))
            then(dve.tensor_tensor(offset[:, :], n_col[:, :], n_blocks[:, :], ALU.subtract))
            then(dve.tensor_scalar(offset[:, :], offset[:, :], float(P), None, ALU.mult))
            then(dve.tensor_scalar(row[:, 0:1], n_experts[:, :], float(EXP - 1), None, ALU.min))
            then(dve.scalar_tensor_tensor(out=row[:, 1:2], in0=n_experts[:, :], scalar=float(LIST), in1=offset[:, :],
                                          op0=ALU.mult, op1=ALU.add))
            then(dve.tensor_tensor(row[:, 2:3], n_tokens[:, :], offset[:, :], ALU.add))
            then(dve.tensor_scalar(pairs_i[:, :], block_end[:, EXP - 1:EXP], -1.0, None, ALU.add))
            then(dve.tensor_single_scalar(pairs_i[:, :], pairs_i[:, :], 1, ALU.arith_shift_right))
            then(dve.tensor_copy(row_i[:, 0:3], row[:, 0:3]))
            then(dve.tensor_copy(row_i[:, 3:4], pairs_i[:, :]))
            assert n[0] == PLAN_STEPS - 10
            for expert_j, place_j, slot in ((expert1, place1, slots[0]), (expert2, place2, slots[1])):
                wide = [P, NB, EXP]
                then(dve.tensor_tensor(hot[:, :, :], iota_e[:, :].unsqueeze(1).to_broadcast(wide),
                                       expert_j[:, :].unsqueeze(2).to_broadcast(wide), ALU.is_equal))
                then(dve.tensor_tensor(hot[:, :, :], hot[:, :, :], start[:, :].unsqueeze(1).to_broadcast(wide), ALU.mult))
                then(dve.tensor_reduce(slot_f[:, :], hot[:, :, :], AX.X, ALU.add))
                then(dve.tensor_tensor(slot_f[:, :], slot_f[:, :], place_j[:, :], ALU.add))
                then(dve.tensor_copy(slot[:, :], slot_f[:, :]))
            assert n[0] == PLAN_STEPS

        @block.sync
        def _(sp):
            sp.wait_ge(step, PLAN_STEPS - 10)
            sp.dma_start(table_dram, row_i[0:MAXBLK, :]).then_inc(table_out, 16)
            sp.wait_ge(table_out, 16)
            sp.dma_start(table[:, :], table_dram.rearrange("(o n) c -> o (n c)", o=1)).then_inc(table_in, 16)
            sp.wait_ge(table_in, 16)


def experts(nc, sem, a, ident, table, list_dram, u_dram, y_dram):
    with ExitStack() as ctx:
        def sb(name, shape, dt=F32):
            return ctx.enter_context(nc.sbuf_tensor(name, shape, dt))

        KG, KDN = 4, 2
        CHUNK = KG * FE
        SLOTS = 6
        D0, D1, U0, U1, G0, G1 = range(SLOTS)
        raw = [sb(f"raw{s}", [P, CHUNK]) for s in range(SLOTS)]
        w_hi = [sb(f"e_hi{s}", [P, CHUNK], F32R) for s in range(SLOTS)]
        w_lo = [sb(f"e_lo{s}", [P, CHUNK], F32R) for s in range(SLOTS)]
        ix = [sb(f"ix{s}", [P, 1], I32) for s in range(RING)]
        x = [sb(f"ex{s}", [P, D]) for s in range(RING)]
        x_hi = [sb(f"ex_hi{s}", [P, KD, P], F32R) for s in range(RING)]
        x_lo = [sb(f"ex_lo{s}", [P, KD, P], F32R) for s in range(RING)]
        silu = sb("silu", [P, FE])
        hid = sb("hid", [P, FE])
        h_hi = sb("hid_hi", [P, FT, P], F32R)
        h_lo = sb("hid_lo", [P, FT, P], F32R)
        y = sb("y_sb", [P, D])
        ps_g = ctx.enter_context(nc.psum_tensor("ps_g", [P, FE], F32))
        ps_u = ctx.enter_context(nc.psum_tensor("ps_u", [P, FE], F32))
        ps_y = ctx.enter_context(nc.psum_tensor("ps_ey", [P, 2, BANK], F32))
        ps_x = ctx.enter_context(nc.psum_tensor("ps_ex", [P, 2, BANK], F32))
        ps_h = ctx.enter_context(nc.psum_tensor("ps_eh", [P, FE], F32))

        waited = sem("e_waited")
        waited_act = sem("e_waited_act")
        waited_sp = sem("e_waited_sp")
        arrived = [sem(f"e_arrived{s}") for s in range(SLOTS)]
        ix_in = [sem(f"e_ix_in{s}") for s in range(RING)]
        x_in = [sem(f"e_x_in{s}") for s in range(RING)]
        hi_done = sem("e_hi_done")
        lo_done = sem("e_lo_done")
        used = sem("e_used")
        x_turned = sem("e_x_turned")
        x_hi_done = sem("e_x_hi_done")
        x_lo_done = sem("e_x_lo_done")
        silu_done = sem("e_silu_done")
        hid_done = sem("e_hid_done")
        hid_turned = sem("e_hid_turned")
        h_hi_done = sem("e_h_hi_done")
        h_lo_done = sem("e_h_lo_done")
        y_out = sem("e_y_out")
        y_stored = sem("e_y_stored")

        block = ctx.enter_context(nc.Block())

        def field(eng, n, c, top):
            at = 4 * n + c
            where = slice(at, at + 1) if isinstance(n, int) else bass.ds(at, 1)
            return eng.value_load(table[0:1, where], min_val=0, max_val=top)

        def more_pairs(eng):
            return eng.value_load(table[0:1, 3:4], min_val=0, max_val=MAXPAIRS - 1)

        def chunk_of(n, s):
            return SLOTS * n + SLOTS + s

        def up_used(n):
            return SLOTS + SLOTS * n + 4

        def gate_used(n):
            return SLOTS + (2 if isinstance(n, int) and n == 0 else SLOTS * n)

        def down_used(n):
            return SLOTS + SLOTS * n + 8

        @block.sync
        def _(sp):
            def load(weights, k, e, c, idx, s, round_):
                sp.wait_ge(lo_done, idx + 1)
                src = weights[bass.ds(e, 1), :, :].rearrange("o (c p k) f -> c p (o k f)", p=P, k=k)[c]
                sp.dma_start(raw[s][:, :], src).then_inc(arrived[s], 16)

            def lists(m, s):
                at = field(sp, m, 1, EXP * LIST + 2 * P)
                sp.dma_start(ix[s][:, :], list_dram[bass.ds(at, P), :]).then_inc(ix_in[s], 16)

            def expert(n):
                return field(sp, n, 0, EXP - 1)

            for m in range(2):
                lists(m, m)
            e0, e1 = expert(0), expert(1)
            for c in range(2):
                load(a["w_gate"], KG, e0, c, c, D0 + c, 0)
            for c in range(2):
                load(a["w_up"], KG, e0, c, 2 + c, U0 + c, 0)
            for c in range(2):
                load(a["w_gate"], KG, e1, c, 4 + c, G0 + c, 0)

            def step(n, s):
                sp.wait_ge(x_in[s], 8 * (n - s) + 16)
                lists(n + 2, s)
                for weights, k, m, s0 in ((a["w_down"], KDN, n, D0), (a["w_up"], KG, n + 1, U0), (a["w_gate"], KG, n + 2, G0)):
                    e = expert(m)
                    for c in range(2):
                        load(weights, k, e, c, chunk_of(n, s0 + c), s0 + c, n + 1)

            more = more_pairs(sp)
            with sp.Fori(0, more + 1) as i:
                step(2 * i, 0)
                step(2 * i + 1, 1)
            last = 2 * more + 2
            for s in range(SLOTS):
                sp.wait_ge(arrived[s], 16 * last + 16)
            for s in range(RING):
                sp.wait_ge(x_in[s], 8 * last + 16)
            sp.sem_inc(waited_sp, 1)

        @block.gpsimd
        def _(pool):
            def gather(m, s):
                pool.wait_ge(ix_in[s], 8 * (m - s) + 16)
                if not isinstance(m, int):
                    pool.wait_ge(x_turned, m - 1)
                pool.sem_inc(waited, 1)
                pool.indirect_dma_start(x[s][:, :], None, u_dram, bass.IndirectOffsetOnAxis(ap=ix[s][:, 0:1], axis=0)
                                        ).then_inc(x_in[s], 16)

            gather(0, 0)
            gather(1, 1)
            with pool.Fori(0, more_pairs(pool) + 1) as i:
                gather(2 * i + 2, 0)
                gather(2 * i + 3, 1)

        @block.tensor
        def _(pe):
            def turn_x(m, s):
                pe.wait_ge(x_in[s], 8 * (m - s) + 16)
                pe.wait_ge(x_lo_done, m + 1)
                for c in range(2):
                    for k in range(KG):
                        mm = pe.transpose(ps_x[:, c, k * P:(k + 1) * P], x[s][:, c * FE + k:(c + 1) * FE:KG], ident[:, :])
                mm.then_inc(x_turned, 1)

            def half_product(ps, s, c, idx, slot):
                pe.wait_ge(lo_done, idx + 1 + SLOTS)
                for k in range(KG):
                    for n, (xs, w) in enumerate(((x_hi, w_hi), (x_hi, w_lo), (x_lo, w_hi))):
                        mm = pe.matmul(ps[:, :], xs[s][:, c * KG + k, :], w[slot][:, k * FE:(k + 1) * FE],
                                       start=(c == 0 and k == 0 and n == 0), stop=(c == 1 and k == KG - 1 and n == 2))
                mm.then_inc(used, 1)

            def up(n, s):
                pe.wait_ge(hid_done, n + 1)
                for c in range(2):
                    half_product(ps_u, s, c, SLOTS * n + 2 + c, U0 + c)

            def gate(m, s, c, idx, slot):
                if c == 0:
                    pe.wait_ge(x_lo_done, m + 2)
                    pe.wait_ge(silu_done, m + 1)
                half_product(ps_g, s, c, idx, slot)

            def down(n):
                pe.wait_ge(h_lo_done, n + 2)
                pe.wait_ge(y_out, n + 1)
                for c in range(2):
                    pe.wait_ge(lo_done, chunk_of(n, D0 + c) + 1 + SLOTS)
                    for k in range(KDN):
                        for i in range(2):
                            for j, (h, w) in enumerate(((h_hi, w_hi), (h_hi, w_lo), (h_lo, w_hi))):
                                mm = pe.matmul(ps_y[:, i, :], h[:, c * KDN + k, :], w[D0 + c][:, k * D + i * BANK:k * D + (i + 1) * BANK],
                                               start=(c == 0 and k == 0 and j == 0), stop=(c == 1 and k == KDN - 1 and j == 2))
                    mm.then_inc(used, 1)

            def step(n, s):
                turn_x(n + 1, 1 - s)
                up(n, s)
                gate(n + 1, 1 - s, 0, SLOTS * n + 4, G0)
                pe.wait_ge(hid_done, n + 2)
                pe.wait_ge(h_lo_done, n + 1)
                for c in range(2):
                    for k in range(KDN):
                        mm = pe.transpose(ps_h[:, (c * KDN + k) * P:(c * KDN + k + 1) * P],
                                          hid[:, c * 2 * P + k:(c + 1) * 2 * P:KDN], ident[:, :])
                mm.then_inc(hid_turned, 1)
                gate(n + 1, 1 - s, 1, SLOTS * n + 5, G1)
                down(n)

            turn_x(0, 0)
            for c in range(2):
                gate(0, 0, c, c, D0 + c)
            with pe.Fori(0, more_pairs(pe) + 1) as i:
                step(2 * i, 0)
                step(2 * i + 1, 1)

        def square_x(t):
            return t[:, :, :].rearrange("p b (k c) -> p (b k) c", c=P)

        @block.scalar
        def _(act):
            act.sem_inc(used, SLOTS)

            def split(idx, s, round_):
                act.wait_ge(arrived[s], 16 * round_ + 16)
                act.wait_ge(used, idx + 1)
                act.activation(w_hi[s][:, :], raw[s][:, :], ACT.Copy).then_inc(hi_done, 1)

            def x_split(m, s):
                act.wait_ge(x_turned, m + 1)
                act.activation(x_hi[s][:, :, :], square_x(ps_x), ACT.Copy).then_inc(x_hi_done, 1)

            def store(n):
                act.wait_ge(used, down_used(n))
                act.wait_ge(y_stored, 16 * n) if not isinstance(n, int) or n > 0 else None
                act.activation(y[:, :], ps_y[:, :, :].rearrange("p b c -> p (b c)"), ACT.Copy).then_inc(y_out, 1)
                act.wait_ge(y_out, n + 2)
                at = field(act, n, 2, 2 * REAL)
                act.dma_start(y_dram[bass.ds(at, P), :], y[:, :]).then_inc(y_stored, 16)

            def step(n, s, before):
                act.wait_ge(used, gate_used(n))
                act.wait_ge(hid_done, n + 1)
                act.activation(silu[:, :], ps_g[:, :], ACT.Silu).then_inc(silu_done, 1)
                if before is not None:
                    store(before)
                x_split(n + 1, 1 - s)
                for s_ in (D0, D1, U0):
                    split(chunk_of(n, s_), s_, n + 1)
                act.wait_ge(hid_turned, n + 1)
                act.activation(h_hi[:, :, :], ps_h[:, :].rearrange("p (k c) -> p k c", c=P), ACT.Copy).then_inc(h_hi_done, 1)
                for s_ in (U1, G0, G1):
                    split(chunk_of(n, s_), s_, n + 1)

            x_split(0, 0)
            for s in range(SLOTS):
                split(s, s, 0)
            act.sem_inc(y_out, 1)
            act.sem_inc(silu_done, 1)
            step(0, 0, None)
            step(1, 1, 0)
            more = more_pairs(act)
            with act.Fori(0, more) as i:
                step(2 * i + 2, 0, 2 * i + 1)
                step(2 * i + 3, 1, 2 * i + 2)
            store(2 * more + 1)
            act.wait_ge(y_stored, 32 * more + 32)
            act.sem_inc(waited_act, 1)

        @block.vector
        def _(dve):
            dve.sem_inc(lo_done, SLOTS)
            dve.sem_inc(x_lo_done, 1)
            dve.sem_inc(h_lo_done, 1)
            dve.sem_inc(hid_done, 1)

            def split(idx, s):
                dve.wait_ge(hi_done, idx + 1)
                dve.tensor_tensor(w_lo[s][:, :], raw[s][:, :], w_hi[s][:, :].bitcast(F32), ALU.subtract).then_inc(lo_done, 1)

            def x_split(m, s):
                dve.wait_ge(x_hi_done, m + 1)
                dve.tensor_tensor(x_lo[s][:, :, :], square_x(ps_x), x_hi[s][:, :, :].bitcast(F32), ALU.subtract).then_inc(x_lo_done, 1)

            def step(n, s):
                x_split(n + 1, 1 - s)
                for s_ in (D0, D1):
                    split(chunk_of(n, s_), s_)
                dve.wait_ge(used, up_used(n))
                dve.wait_ge(silu_done, n + 2)
                dve.wait_ge(hid_turned, n) if not isinstance(n, int) or n > 0 else None
                dve.tensor_tensor(hid[:, :], ps_u[:, :], silu[:, :], ALU.mult).then_inc(hid_done, 1)
                split(chunk_of(n, U0), U0)
                dve.wait_ge(h_hi_done, n + 1)
                dve.tensor_tensor(h_lo[:, :, :], ps_h[:, :].rearrange("p (k c) -> p k c", c=P), h_hi[:, :, :].bitcast(F32),
                                  ALU.subtract).then_inc(h_lo_done, 1)
                for s_ in (U1, G0, G1):
                    split(chunk_of(n, s_), s_)

            x_split(0, 0)
            for s in range(SLOTS):
                split(s, s)
            step(0, 0)
            step(1, 1)
            with dve.Fori(0, more_pairs(dve)) as i:
                step(2 * i + 2, 0)
                step(2 * i + 3, 1)


def combine(nc, sem, a, eps_t, gate1, gate2, slots, h2_dram, y_dram, out):
    with ExitStack() as ctx:
        def sb(name, shape, dt=F32):
            return ctx.enter_context(nc.sbuf_tensor(name, shape, dt))

        DEPTH = 5
        g_final = sb("g_final", [P, D])
        z = [sb(f"z{s}", [P, D]) for s in range(DEPTH)]
        y = [[sb(f"cy{j}{s}", [P, D]) for s in range(DEPTH)] for j in range(2)]
        square = sb("c_square", [P, D])
        ssq = sb("c_ssq", [P, NB])
        rms = sb("c_rms", [P, NB])
        rstd = sb("c_rstd", [P, NB])
        g_in = sem("c_g_in")
        z_in = [sem(f"c_z_in{s}") for s in range(DEPTH)]
        y_in = [sem(f"c_y_in{s}") for s in range(DEPTH)]
        added = sem("c_added")
        squared = sem("c_squared")
        rms_done = sem("c_rms_done")
        rstd_done = sem("c_rstd_done")
        normed = sem("c_normed")
        stored = [sem(f"c_stored{s}") for s in range(DEPTH)]
        block = ctx.enter_context(nc.Block())

        @block.sync
        def _(sp):
            sp.dma_start(g_final[:, :], a["ln_final_g"][0].partition_broadcast(P)).then_inc(g_in, 16)
            for b in range(NB + DEPTH):
                s = b % DEPTH
                if b >= DEPTH:
                    sp.wait_ge(normed, b - DEPTH + 1)
                    sp.dma_start(out[(b - DEPTH) * P:(b - DEPTH + 1) * P, :], z[s][:, :]).then_inc(stored[s], 16)
                if b < NB:
                    if b >= DEPTH:
                        sp.wait_ge(stored[s], 16 * (b // DEPTH))
                    sp.dma_start(z[s][:, :], h2_dram[b * P:(b + 1) * P, :]).then_inc(z_in[s], 16)
            for s in range(DEPTH):
                sp.wait_ge(stored[s], 16 * (NB // DEPTH))

        @block.gpsimd
        def _(pool):
            for b in range(NB):
                s = b % DEPTH
                if b >= DEPTH:
                    pool.wait_ge(added, 2 * (b - DEPTH) + 2)
                for j in range(2):
                    pool.indirect_dma_start(y[j][s][:, :], None, y_dram,
                                            bass.IndirectOffsetOnAxis(ap=slots[j][:, b:b + 1], axis=0)).then_inc(y_in[s], 16)

        @block.scalar
        def _(act):
            for b in range(NB):
                act.wait_ge(added, 2 * b + 2)
                act.wait_ge(squared, b) if b else None
                act.activation(square[:, :], z[b % DEPTH][:, :], ACT.Square, accum_out=ssq[:, b:b + 1]).then_inc(squared, 1)
                act.wait_ge(squared, b + 1)
                act.activation(rms[:, b:b + 1], ssq[:, b:b + 1], ACT.Sqrt, bias=eps_t[:, :], scale=1.0 / D).then_inc(rms_done, 1)

        @block.vector
        def _(dve):
            def norm(b):
                dve.wait_ge(rms_done, b + 1)
                dve.reciprocal(rstd[:, b:b + 1], rms[:, b:b + 1]).then_inc(rstd_done, 1)
                dve.wait_ge(rstd_done, b + 1)
                zs = z[b % DEPTH]
                dve.scalar_tensor_tensor(out=zs[:, :], in0=zs[:, :], scalar=rstd[:, b:b + 1], in1=g_final[:, :],
                                         op0=ALU.mult, op1=ALU.mult).then_inc(normed, 1)

            dve.wait_ge(g_in, 16)
            for b in range(NB):
                s = b % DEPTH
                dve.wait_ge(z_in[s], 16 * (b // DEPTH + 1))
                dve.wait_ge(y_in[s], 32 * (b // DEPTH + 1))
                for j, gate in enumerate((gate1, gate2)):
                    dve.scalar_tensor_tensor(out=z[s][:, :], in0=y[j][s][:, :], scalar=gate[:, b:b + 1], in1=z[s][:, :],
                                             op0=ALU.mult, op1=ALU.add).then_inc(added, 1)
                    dve.wait_ge(added, 2 * b + j + 1)
                if b:
                    norm(b - 1)
            norm(NB - 1)


def layouts(i):
    f = np.float32

    def feature_tiles(w):
        w = w.reshape(KD, P, -1)
        q = [np.r_[h * HD:(h + 1) * HD, (h + 4) * HD:(h + 5) * HD] for h in range(4)]
        cols = q + [np.arange(c, c + P) for c in range(ATTN, w.shape[2], P)]
        return np.stack([w[:, :, c].transpose(1, 0, 2) for c in cols])

    def per_feature(v):
        return v.reshape(FT, P).T

    gates = np.zeros((FT, P, 4, P), f)
    for g, name in enumerate(("w_rgate_fwd", "w_igate_fwd", "w_rgate_bwd", "w_igate_bwd")):
        for ft in range(FT):
            gates[ft, 0:HD, g, 0:HD] = i[name][0, 2 * ft]
            gates[ft, HD:P, g, HD:P] = i[name][0, 2 * ft + 1]
    vecs = [i["conv_w"][0, j] for j in range(4)] + [i["conv_b"][0]]
    vecs += [i[n][0] for n in ("b_rgate_fwd", "b_igate_fwd", "b_rgate_bwd", "b_igate_bwd", "lam_fwd", "lam_bwd")]
    router = np.zeros((D, ROUT), f)
    router[:, 0:4] = i["w_router_grp"][0]
    router[:, 8:ROUT] = i["w_router_exp"][0]
    rbias = np.full(ROUT, NEG, f)
    rbias[0:4] = i["b_router_grp"][0]
    rbias[8:ROUT] = i["b_router_exp"][0]
    pos = np.r_[np.arange(META + SEQS[0]), META + np.arange(SEQS[1])].astype(f)
    inv = f(500000.0) ** (-np.arange(0, 16, 2, dtype=f) / f(16))
    ang = pos[:, None] * inv[None, :]
    cos, sin = np.ones((P, COLS), f), np.zeros((P, COLS), f)
    swap = np.zeros((P, P), f)
    for h in (0, HD):
        for j in range(8):
            cos[h + j] = cos[h + 8 + j] = np.cos(ang[:, j])
            sin[h + j] = -np.sin(ang[:, j])
            sin[h + 8 + j] = np.sin(ang[:, j])
            swap[h + 8 + j, h + j] = swap[h + j, h + 8 + j] = 1.0
    masks = np.zeros((NB, P, KEYS), f)
    qi, kj = np.arange(P)[:, None], np.arange(P)[None, :]
    last = (SEQS[0] // P - 1, NB - 1)
    first = (0, SEQS[0] // P)
    for b in range(NB):
        masks[b, :, 0:P] = NEG if b in first else np.where(kj >= qi, 0.0, NEG)
        masks[b, :, 2 * P:3 * P] = NEG if b in last else np.where(kj <= qi, 0.0, NEG)
    before = (np.arange(P)[:, None] < np.arange(P)[None, :]).astype(f)
    return {
        "x": np.concatenate([i["x_prompt"][0], i["x_sample"][0]]),
        "meta": i["meta_tokens"],
        "ln_mix_g": i["ln_mix_g"],
        "w_in": feature_tiles(i["w_in"][0]),
        "gates": gates,
        "vecs": np.stack([per_feature(v) for v in vecs], axis=2),
        "sink": i["attn_sink"],
        "g_out": np.stack([i["g_attn_out"][0].reshape(FT, P), i["g_rec_out"][0].reshape(FT, P)]).reshape(KD, P).T.copy(),
        "w_out": i["w_out"][0].reshape(KD, P, D).transpose(1, 0, 2),
        "ln_ffn_g": i["ln_ffn_g"],
        "router": router.reshape(KD, P, ROUT).transpose(1, 0, 2),
        "rbias": rbias[None],
        "w_gate": i["w_exp_gate"][0],
        "w_up": i["w_exp_up"][0],
        "w_down": i["w_exp_down"][0],
        "ln_final_g": i["ln_final_g"][None],
        "ident": np.eye(P, dtype=f),
        "swap": swap,
        "before": before,
        "cos": cos,
        "sin": sin,
        "masks": masks,
    }


def kernel(**inputs):
    import concourse.bacc as bacc
    from concourse.bass_utils import run_bass_kernel_spmd as run

    arrays = {n: np.ascontiguousarray(v) for n, v in layouts({n: np.asarray(v) for n, v in inputs.items()}).items()}
    nc = bacc.Bacc("TRN2", target_bir_lowering=False, num_devices=1)
    a = {n: nc.dram_tensor(f"in_{n}", v.shape, mybir.dt.from_np(v.dtype), kind="ExternalInput").ap()
         for n, v in arrays.items()}
    out = nc.dram_tensor("out", (REAL, D), F32, kind="ExternalOutput").ap()
    encoder(nc, a, out)
    got = run(nc, [{f"in_{n}": v for n, v in arrays.items()}], core_ids=[0]).results[0]["out"]
    return got[0:SEQS[0]][None], got[SEQS[0]:REAL][None]
```

```python
from contextlib import ExitStack, contextmanager

import numpy as np

import concourse.bass as bass
from concourse import mybir

F32 = mybir.dt.float32
F32R = mybir.dt.float32r
I32 = mybir.dt.int32
U32 = mybir.dt.uint32
ALU = mybir.AluOpType
ACT = mybir.ActivationFunctionType
AX = mybir.AxisListType

P = 128
D = 1024
META = 16
SEQS = (1024, 256)
REAL = sum(SEQS)
NB = REAL // P
COLS = META + REAL
KD = D // P
HEADS = 8
HD = 64
ATTN = HEADS * HD
REC = 512
FT = REC // P
FTILES = 14
NCH = 3
CH = COLS // NCH
BANK = 512
EXP = 32
FE = 512
EPS = 1e-6
NEG = -1e30
RING = 2
WIN = 3 * P
KEYS = WIN + META
T0 = META + SEQS[0]
T1 = META + SEQS[1]
XRW = 2 + T0 + 1 + 2 + T1 + 1
RW = XRW - 3
OFF1 = T0 + 3
LIST = 1280
MAXBLK = 64
FIELDS = 5
MAXPAIRS = (2 * REAL // P + EXP) // 2
YROWS = 2 * REAL + P
ROUT = 40


def done(t):
    return t + 1 + RING


def free(t):
    return t + 1


@contextmanager
def semaphores(nc):
    with ExitStack() as ctx:
        made = []

        def sem(name):
            made.append(ctx.enter_context(nc.semaphore(name)))
            return made[-1]

        yield sem
        with nc.Block() as block:
            @block.sync
            def _(sp):
                for one in made:
                    sp.sem_clear(one)


def encoder(nc, a, out):
    top = ExitStack()
    with top:
        def dram(name, shape, dt):
            return nc.dram_tensor(name, shape, dt, kind="Internal").ap()

        h2_dram = dram("h2_dram", [REAL, D], F32)
        u_dram = dram("u_dram", [REAL, D], F32)
        y_dram = dram("y_dram", [YROWS, D], F32)
        list_dram = dram("list_dram", [(EXP + 1) * LIST, 1], I32)
        table_dram = dram("table_dram", [MAXBLK, FIELDS], I32)

        def keep(name, shape, dt=F32):
            return top.enter_context(nc.sbuf_tensor(name, shape, dt))

        gate1 = keep("gate1", [P, NB])
        gate2 = keep("gate2", [P, NB])
        expert1 = keep("expert1", [P, NB])
        expert2 = keep("expert2", [P, NB])
        place1 = keep("place1", [P, NB])
        place2 = keep("place2", [P, NB])
        counts = keep("counts", [P, EXP])
        iota_e = keep("iota_e", [P, EXP])
        ident = keep("ident", [P, P])
        eps_t = keep("eps_t", [P, 1])

        with ExitStack() as mixer:
            def mk(name, shape, dt=F32):
                return mixer.enter_context(nc.sbuf_tensor(name, shape, dt))

            feat = mk("feat", [P, 2 * FT, COLS])
            k_pre = mk("k_pre", [P, COLS])
            v_pre = mk("v_pre", [P, COLS])
            with semaphores(nc) as sem:
                project(nc, sem, a, feat, k_pre, v_pre, ident, eps_t, iota_e, list_dram, y_dram)
            yg, q_pre = feat[:, 0:FT, :], feat[:, FT:2 * FT, :]
            rstd_rec = mk("rstd_rec", [P, NB])
            k_rot = mk("k_rot", [P, META + P + REAL + P])
            v_tok = mk("v_tok", [P, (NB + 2) * P])
            v_meta = mk("v_meta", [P, ATTN])
            with semaphores(nc) as sem:
                keys(nc, sem, a, k_pre, v_pre, yg, k_rot, v_tok, v_meta, rstd_rec, ident, eps_t)
            rec = yg[:, :, META:COLS]
            with semaphores(nc) as sem:
                mix(nc, sem, a, q_pre, rec, rstd_rec, k_rot, v_tok, v_meta, ident, eps_t, iota_e,
                    gate1, gate2, expert1, expert2, place1, place2, counts, h2_dram, u_dram, list_dram)
        slots = [top.enter_context(nc.sbuf_tensor(f"slot{j}", [P, NB], I32)) for j in range(2)]
        table = top.enter_context(nc.sbuf_tensor("table", [1, MAXBLK * FIELDS], I32))
        with semaphores(nc) as sem:
            plan(nc, sem, iota_e, counts, expert1, expert2, place1, place2, slots, table, table_dram)
        with semaphores(nc) as sem:
            experts(nc, sem, a, ident, table, list_dram, u_dram, y_dram)
        with semaphores(nc) as sem:
            combine(nc, sem, a, eps_t, gate1, gate2, slots, h2_dram, y_dram, out)


def project(nc, sem, a, feat, k_pre, v_pre, ident, eps_t, iota_e, list_dram, y_dram):
    with ExitStack() as ctx:
        def sb(name, shape, dt=F32):
            return ctx.enter_context(nc.sbuf_tensor(name, shape, dt))

        XT = FT
        xr = sb("xr", [P, FT, XRW])
        h_hi = sb("h_hi", [P, KD, COLS], F32R)
        h_lo = sb("h_lo", [P, KD, COLS], F32R)
        w_raw = [sb(f"w_raw{s}", [P, KD, P]) for s in range(RING)]
        w_hi = [sb(f"w_hi{s}", [P, KD, P], F32R) for s in range(RING)]
        w_lo = [sb(f"w_lo{s}", [P, KD, P], F32R) for s in range(RING)]
        r_g = sb("r_g", [P, RW])
        i_g = sb("i_g", [P, RW])
        t_g = sb("t_g", [P, RW])
        a_g = sb("a_g", [P, RW])
        h_g = sb("h_g", [P, RW])
        xn = [r_g[:, 0:D], i_g[:, 0:D]]
        x_in = [t_g[:, 0:D], h_g[:, 0:D]]
        zeros = a_g[:, 0:D]
        conv = h_g[:, :]
        g_bc = w_raw[1][:, :, :].rearrange("p k c -> p (k c)")
        vecs = sb("vecs", [P, FT, 11])
        gates = sb("gates", [P, 4, P])
        small = sb("lam_small", [P, 7, FT, 2])
        decay, ndecay, sp_e, sp_z, sp_z2, sp_p, lam_pos = (small[:, j, :, :] for j in range(7))
        ssq = [sb(f"ssq{s}", [P, 1]) for s in range(RING)]
        rms = [sb(f"rms{s}", [P, 1]) for s in range(RING)]
        rstd = [sb(f"rstd{s}", [P, 1]) for s in range(RING)]
        ps = ctx.enter_context(nc.psum_tensor("pj", [P, 8, BANK], F32))
        tr = [ps[:, 0:2, :], ps[:, 2:4, :]]
        ps_r, ps_i = ps[:, 2:5, :], ps[:, 5:8, :]
        flat_r = ps_r.rearrange("p b c -> p (b c)")
        flat_i = ps_i.rearrange("p b c -> p (b c)")

        consts_in = sem("consts_in")
        vecs_in = sem("vecs_in")
        gates_in = sem("gates_in")
        x_arrived = [sem(f"x_arrived{s}") for s in range(RING)]
        w_arrived = [sem(f"w_arrived{s}") for s in range(RING)]
        fills = sem("fills")
        fill_dma = sem("fill_dma")
        eps_set = sem("eps_set")
        squared = sem("squared")
        rms_done = sem("rms_done")
        rstd_done = sem("rstd_done")
        xn_done = sem("xn_done")
        x_turned = sem("x_turned")
        h_hi_done = sem("h_hi_done")
        h_lo_done = sem("h_lo_done")
        w_hi_done = sem("w_hi_done")
        w_lo_done = sem("w_lo_done")
        proj_done = sem("proj_done")
        proj_out = sem("proj_out")
        xr_cleared = sem("xr_cleared")
        lam_e = sem("lam_e")
        lam_step = sem("lam_step")
        conv_step = sem("conv_step")
        conv_done = sem("conv_done")
        gates_done = sem("gates_done")
        r_done = sem("r_done")
        i_done = sem("i_done")
        ta_done = sem("ta_done")
        v_done = sem("v_done")
        s_done = sem("s_done")
        a_cut = sem("a_cut")
        ix_done = sem("ix_done")
        u_done = sem("scan_u_done")
        scanned = sem("scanned")
        summed = sem("summed")
        gelu_done = sem("gelu_done")
        rec_done = sem("rec_done")

        block = ctx.enter_context(nc.Block())

        def rows(t):
            return META if isinstance(t, int) and t == NB else P

        def col(t):
            return 0 if isinstance(t, int) and t == NB else META + t * P

        def one(tensor, j, lo, hi):
            return tensor[:, bass.ds(j, 1), lo:hi].rearrange("p o c -> p (o c)")

        def vec(ft, j):
            return one(vecs, ft, j, j + 1)

        @block.sync
        def _(sp):
            sp.dma_start(ident[:, :], a["ident"]).then_inc(consts_in, 16)
            sp.dma_start(g_bc, a["ln_mix_g"][0].partition_broadcast(P)).then_inc(consts_in, 16)

            def load_x(t, s):
                sp.wait_ge(xn_done, free(t))
                src = a["meta"] if isinstance(t, int) and t == NB else a["x"][bass.ds(t * P, P), :]
                sp.dma_start(x_in[s][0:rows(t), :], src).then_inc(x_arrived[s], 16)

            load_x(0, 0)
            load_x(1, 1)
            sp.dma_start(vecs[:, :, :], a["vecs"]).then_inc(vecs_in, 16)
            sp.wait_ge(fills, 2)
            sp.dma_start(list_dram.rearrange("(p c) o -> p (c o)", p=P),
                         zeros[:, 0:(EXP + 1) * LIST // P].bitcast(I32)).then_inc(fill_dma, 16)
            sp.dma_start(y_dram[2 * REAL:YROWS, :], zeros).then_inc(fill_dma, 16)
            with sp.Fori(0, 4) as i:
                load_x(2 * i + 2, 0)
                load_x(2 * i + 3, 1)
            load_x(NB, 0)

            def load_w(f, s):
                sp.wait_ge(w_lo_done, free(f))
                sp.dma_start(w_raw[s][:, :, :], a["w_in"][bass.ds(f, 1), :, :, :].rearrange("o p k c -> p (o k) c")
                             ).then_inc(w_arrived[s], 16)

            load_w(0, 0)
            sp.wait_ge(xn_done, done(NB))
            load_w(1, 1)
            with sp.Fori(0, XT // 2) as i:
                load_w(2 * i + 2, 0)
                load_w(2 * i + 3, 1)
            with sp.Fori(0, FT) as k:
                sp.wait_ge(gates_done, 4 * k + 1)
                sp.dma_start(gates[:, :, :], a["gates"][bass.ds(k, 1), :, :, :].rearrange("o p g c -> p (o g) c")
                             ).then_inc(gates_in, 16)
                load_w(2 * k + 6, 0)
                load_w(2 * k + 7, 1)

        @block.gpsimd
        def _(pool):
            pool.memset(zeros, 0.0).then_inc(fills, 1)
            pool.iota(iota_e[:, :], pattern=[[1, EXP]], base=0, channel_multiplier=0,
                      allow_small_or_imprecise_dtypes=True).then_inc(fills, 1)
            pool.memset(xr[:, :, :], 0.0).then_inc(xr_cleared, 1)

        @block.scalar
        def _(act):
            act.sem_inc(h_hi_done, RING)
            act.sem_inc(w_hi_done, RING)
            act.sem_inc(proj_out, 2)
            act.sem_inc(r_done, 1)
            act.sem_inc(i_done, 1)
            act.sem_inc(s_done, 1)

            def norm(t, s, round_):
                n = rows(t)
                act.wait_ge(x_arrived[s], 16 * (round_ + 1))
                act.wait_ge(x_turned, free(t))
                act.activation(xn[s][0:n, :], x_in[s][0:n, :], ACT.Square, accum_out=ssq[s][0:n, :]).then_inc(squared, 1)
                act.wait_ge(squared, t + 1)
                act.activation(rms[s][0:n, :], ssq[s][0:n, :], ACT.Sqrt, bias=eps_t[0:n, :], scale=1.0 / D).then_inc(rms_done, 1)

            def hi(t, s):
                n = rows(t)
                act.wait_ge(x_turned, done(t))
                act.activation(h_hi[:, :, bass.ds(col(t), n)],
                               tr[s].rearrange("p b (k c) -> p (b k) c", c=P)[:, :, 0:n], ACT.Copy).then_inc(h_hi_done, 1)

            act.wait_ge(eps_set, 1)
            norm(0, 0, 0)
            with act.Fori(0, 4) as i:
                norm(2 * i + 1, 1, i)
                hi(2 * i, 0)
                norm(2 * i + 2, 0, i + 1)
                hi(2 * i + 1, 1)
            norm(9, 1, 4)
            hi(8, 0)
            norm(10, 0, 5)
            hi(9, 1)
            hi(10, 0)

            def split_w(f, s, round_):
                act.wait_ge(w_arrived[s], 16 * (round_ + 1))
                act.wait_ge(proj_done, NCH * f + NCH)
                act.activation(w_hi[s][:, :, :], w_raw[s][:, :, :], ACT.Copy).then_inc(w_hi_done, 1)

            def evacuate(f, s, c, put):
                act.wait_ge(proj_done, NCH * f + c + 1 + 2 * NCH)
                put(ps[:, (NCH * s + c) % 2, :], c).then_inc(proj_out, 1)

            def put_flat(dst):
                return lambda bank, c: act.activation(dst(c), bank[:, 0:CH], ACT.Copy)

            def put_xr(ft):
                def piece(dst, bank, lo, n):
                    return act.activation(one(xr, ft, dst, dst + n), bank[:, lo:lo + n], ACT.Copy)

                def put(bank, c):
                    if c == 0:
                        piece(2 + OFF1, bank, 0, META)
                        return piece(2, bank, 0, CH)
                    if c == 1:
                        return piece(2 + CH, bank, 0, CH)
                    n = T0 - 2 * CH
                    piece(2 + 2 * CH, bank, 0, n)
                    return piece(2 + OFF1 + META, bank, n, CH - n)
                return put

            act.wait_ge(lam_step, 1)
            act.activation(sp_e, sp_z, ACT.Exp).then_inc(lam_e, 1)
            split_w(0, 0, 0)
            act.wait_ge(xr_cleared, 1)
            with act.Fori(0, XT // 2) as i:
                split_w(2 * i + 1, 1, i)
                for c in range(NCH):
                    evacuate(2 * i, 0, c, put_xr(2 * i))
                split_w(2 * i + 2, 0, i + 1)
                for c in range(NCH):
                    evacuate(2 * i + 1, 1, c, put_xr(2 * i + 1))
            act.wait_ge(lam_step, LAM_STEPS)
            act.wait_ge(fill_dma, 32)
            with act.Fori(0, FT) as k:
                for d in range(2):
                    n, f = 2 * k + d, 2 * k + XT + d
                    put = put_flat(lambda c: one(feat, 2 * k + d, c * CH, (c + 1) * CH))
                    if d == 0:
                        split_w(f + 1, 1, k + XT // 2)
                    else:
                        split_w(f + 1, 0, k + XT // 2 + 1)
                    act.wait_ge(gates_done, 2 * n + 2)
                    act.wait_ge(u_done, n + 1)
                    act.wait_ge(s_done, n + 1)
                    act.activation(r_g[:, :], flat_r[:, 0:RW], ACT.Sigmoid, bias=vec(k, 5 + 2 * d)).then_inc(r_done, 1)
                    act.wait_ge(gates_done, 2 * n + 3)
                    act.wait_ge(scanned, n + 1)
                    act.activation(i_g[:, :], flat_i[:, 0:RW], ACT.Sigmoid, bias=vec(k, 6 + 2 * d)).then_inc(i_done, 1)
                    evacuate(f, d, 0, put)
                    act.wait_ge(r_done, n + 2)
                    if d == 0:
                        act.wait_ge(summed, k + 1)
                    act.activation(t_g[:, :], r_g[:, :], ACT.Tanh, scale=one(decay, k, d, d + 1)).then_inc(ta_done, 1)
                    act.activation(a_g[:, :], r_g[:, :], ACT.Exp, scale=one(ndecay, k, d, d + 1)).then_inc(ta_done, 1)
                    act.wait_ge(ta_done, 3 * n + 2)
                    act.activation(r_g[:, :], a_g[:, :], ACT.Square).then_inc(ta_done, 1)
                    evacuate(f, d, 1, put)
                    act.wait_ge(v_done, n + 1)
                    act.activation(r_g[:, :], t_g[:, :], ACT.Sqrt).then_inc(s_done, 1)
                    if d == 1:
                        act.wait_ge(proj_out, NCH * (XT + k + 1) + 2)
                        act.activation(one(feat, k, 0, COLS), one(feat, k, 0, COLS), ACT.Gelu_apprx_tanh).then_inc(gelu_done, 1)
                    evacuate(f, d, 2, put)
            split_w(FTILES - 1, 1, FTILES // 2 - 1)
            for s, dst in enumerate((k_pre, v_pre)):
                for c in range(NCH):
                    evacuate(FTILES - 2 + s, s, c, put_flat(lambda c: dst[:, c * CH:(c + 1) * CH]))

        @block.vector
        def _(dve):
            dve.memset(eps_t[:, :], EPS).then_inc(eps_set, 1)
            dve.sem_inc(xn_done, RING)
            dve.sem_inc(h_lo_done, RING)
            dve.sem_inc(w_lo_done, RING)
            dve.sem_inc(u_done, 1)
            dve.sem_inc(scanned, 1)
            dve.sem_inc(summed, 1)
            dve.sem_inc(conv_done, 1)
            dve.sem_inc(rec_done, 2)

            def norm(t, s):
                n = rows(t)
                dve.wait_ge(rms_done, t + 1)
                dve.reciprocal(rstd[s][0:n, :], rms[s][0:n, :]).then_inc(rstd_done, 1)
                dve.wait_ge(rstd_done, t + 1)
                dve.scalar_tensor_tensor(out=xn[s][0:n, :], in0=x_in[s][0:n, :], scalar=rstd[s][0:n, :],
                                         in1=g_bc[0:n, :], op0=ALU.mult, op1=ALU.mult).then_inc(xn_done, 1)

            def lo(t, s):
                n = rows(t)
                dve.wait_ge(h_hi_done, done(t))
                dst = bass.ds(col(t), n)
                dve.tensor_tensor(h_lo[:, :, dst], tr[s].rearrange("p b (k c) -> p (b k) c", c=P)[:, :, 0:n],
                                  h_hi[:, :, dst].bitcast(F32), ALU.subtract).then_inc(h_lo_done, 1)

            dve.wait_ge(consts_in, 32)
            norm(0, 0)
            with dve.Fori(0, 4) as i:
                norm(2 * i + 1, 1)
                lo(2 * i, 0)
                norm(2 * i + 2, 0)
                lo(2 * i + 1, 1)
            norm(9, 1)
            lo(8, 0)
            norm(10, 0)
            lo(9, 1)
            lo(10, 0)

            step = [0]

            def then(ins):
                step[0] += 1
                ins.then_inc(lam_step, 1)
                dve.wait_ge(lam_step, step[0])

            def split_w(f, s):
                dve.wait_ge(w_hi_done, done(f))
                dve.tensor_tensor(w_lo[s][:, :, :], w_raw[s][:, :, :], w_hi[s][:, :, :].bitcast(F32),
                                  ALU.subtract).then_inc(w_lo_done, 1)

            dve.wait_ge(vecs_in, 16)
            lam = vecs[:, :, 9:11]
            then(dve.scalar_tensor_tensor(out=sp_z, in0=lam, scalar=-1.0, in1=lam, op0=ALU.mult, op1=ALU.min))
            split_w(0, 0)
            then(dve.tensor_scalar(lam_pos, lam, -1.0, 0.0, ALU.mult, ALU.max))
            dve.wait_ge(lam_e, 1)
            then(dve.tensor_scalar(sp_z2, sp_e, 2.0, None, ALU.add))
            then(dve.reciprocal(sp_p, sp_z2))
            then(dve.tensor_tensor(sp_z, sp_e, sp_p, ALU.mult))
            then(dve.tensor_tensor(sp_z2, sp_z, sp_z, ALU.mult))
            then(dve.memset(sp_p, 1.0 / 17))
            for j in range(15, 0, -2):
                then(dve.tensor_tensor(sp_p, sp_p, sp_z2, ALU.mult))
                then(dve.tensor_scalar(sp_p, sp_p, 1.0 / j, None, ALU.add))
            then(dve.scalar_tensor_tensor(out=sp_p, in0=sp_p, scalar=2.0, in1=sp_z, op0=ALU.mult, op1=ALU.mult))
            then(dve.tensor_tensor(sp_p, sp_p, lam_pos, ALU.add))
            then(dve.tensor_scalar(decay, sp_p, 8.0, None, ALU.mult))
            then(dve.tensor_scalar(ndecay, sp_p, -8.0, None, ALU.mult))
            assert step[0] == LAM_STEPS

            def convolve(ft):
                dve.wait_ge(proj_out, NCH * ft + NCH + 2)
                dve.wait_ge(conv_done, ft + 1)
                src = [one(xr, ft, j, j + RW) for j in range(4)]
                dve.tensor_scalar(conv, src[0], vec(ft, 0), vec(ft, 4), ALU.mult, ALU.add).then_inc(conv_step, 1)
                for j in range(1, 4):
                    dve.wait_ge(conv_step, 3 * ft + j)
                    dve.scalar_tensor_tensor(out=conv if j < 3 else one(xr, ft, 0, RW), in0=src[j], scalar=vec(ft, j),
                                             in1=conv, op0=ALU.mult, op1=ALU.add).then_inc(conv_step if j < 3 else conv_done, 1)

            with dve.Fori(0, XT // 2) as i:
                for s in range(2):
                    split_w(2 * i + s + 1, 1 - s)
                    convolve(2 * i + s)

            dve.wait_ge(conv_done, FT + 1)
            with dve.Fori(0, FT) as k:
                for d in range(2):
                    n, f = 2 * k + d, 2 * k + XT + d
                    split_w(f + 1, 1 - d)
                    dve.wait_ge(i_done, n + 2)
                    dve.tensor_tensor(i_g[:, :], i_g[:, :], one(xr, k, 0, RW), ALU.mult).then_inc(ix_done, 1)
                    dve.wait_ge(ta_done, 3 * n + 3)
                    dve.scalar_tensor_tensor(out=t_g[:, :], in0=r_g[:, :], scalar=1.0, in1=t_g[:, :],
                                             op0=ALU.add, op1=ALU.mult).then_inc(v_done, 1)
                    cut = OFF1 if d == 0 else T0 - 1
                    dve.memset(a_g[:, cut:cut + 1], 0.0).then_inc(a_cut, 1)
                    dve.wait_ge(ix_done, n + 1)
                    dve.wait_ge(s_done, n + 2)
                    dve.tensor_tensor(i_g[:, :], i_g[:, :], r_g[:, :], ALU.mult).then_inc(u_done, 1)
                    dve.wait_ge(u_done, n + 2)
                    dve.wait_ge(a_cut, n + 1)
                    if d == 0:
                        dve.wait_ge(rec_done, 2 * k + 2)
                        dve.tensor_tensor_scan(h_g[:, :], a_g[:, :], i_g[:, :], 0.0, ALU.mult, ALU.add).then_inc(scanned, 1)
                    else:
                        dve.tensor_tensor_scan(t_g[:, ::-1], a_g[:, ::-1], i_g[:, ::-1], 0.0, ALU.mult,
                                               ALU.add).then_inc(scanned, 1)
                dve.wait_ge(scanned, 2 * k + 3)
                dve.tensor_tensor(h_g[:, :], h_g[:, :], t_g[:, :], ALU.add).then_inc(summed, 1)
                dve.wait_ge(summed, k + 2)
                dve.wait_ge(gelu_done, k + 1)
                for lo_, hi_, at in ((META, T0, META), (OFF1 + META, RW, T0)):
                    dst = one(feat, k, at, at + hi_ - lo_)
                    dve.tensor_tensor(dst, dst, h_g[:, lo_:hi_], ALU.mult).then_inc(rec_done, 1)
            split_w(FTILES - 1, 1)

        @block.tensor
        def _(pe):
            pe.sem_inc(x_turned, RING)
            pe.sem_inc(proj_done, 2 * NCH)
            pe.sem_inc(gates_done, 1)
            pe.wait_ge(consts_in, 32)

            def turn(t, s):
                n = rows(t)
                pe.wait_ge(xn_done, done(t))
                pe.wait_ge(h_lo_done, free(t))
                for k in range(KD):
                    mm = pe.transpose(tr[s][:, k // 4, (k % 4) * P:(k % 4) * P + n], xn[s][0:n, k * P:(k + 1) * P],
                                      ident[0:n, 0:n])
                mm.then_inc(x_turned, 1)

            turn(0, 0)
            with pe.Fori(0, 4) as i:
                turn(2 * i + 1, 1)
                turn(2 * i + 2, 0)
            turn(9, 1)
            turn(10, 0)
            pe.wait_ge(h_lo_done, done(NB))

            def tile(f, s):
                pe.wait_ge(w_lo_done, done(f))
                for c in range(NCH):
                    pe.wait_ge(proj_out, NCH * f + c + 1)
                    cols = slice(c * CH, (c + 1) * CH)
                    for k in range(KD):
                        for n, (w, h) in enumerate(((w_hi, h_hi), (w_hi, h_lo), (w_lo, h_hi))):
                            mm = pe.matmul(ps[:, (NCH * s + c) % 2, 0:CH], w[s][:, k, :], h[:, k, cols],
                                           start=(k == 0 and n == 0), stop=(k == KD - 1 and n == 2))
                    mm.then_inc(proj_done, 1)

            def gate_products(k, d):
                pe.wait_ge(gates_in, 16 * k + 16)
                pe.wait_ge(conv_done, k + 2)
                for bank, g, read in ((ps_r, 2 * d, r_done), (ps_i, 2 * d + 1, i_done)):
                    pe.wait_ge(read, 2 * k + d + 1)
                    for c in range(3):
                        n = min(BANK, RW - c * BANK)
                        mm = pe.matmul(bank[:, c, 0:n], gates[:, g, :], one(xr, k, c * BANK, c * BANK + n),
                                       start=True, stop=True)
                    mm.then_inc(gates_done, 1)

            with pe.Fori(0, XT // 2) as i:
                tile(2 * i, 0)
                tile(2 * i + 1, 1)
            with pe.Fori(0, FT) as k:
                for d in range(2):
                    gate_products(k, d)
                    tile(2 * k + XT + d, d)
            tile(FTILES - 2, 0)
            tile(FTILES - 1, 1)


def keys(nc, sem, a, k_pre, v_pre, yg, k_rot, v_tok, v_meta, rstd_rec, ident, eps_t):
    with ExitStack() as ctx:
        def sb(name, shape, dt=F32):
            return ctx.enter_context(nc.sbuf_tensor(name, shape, dt))

        cos = sb("cos_k", [P, COLS])
        sin = sb("sin_k", [P, COLS])
        swap = sb("swap_k", [P, P])
        ones = sb("ones_r", [P, 1])
        k_cos = sb("k_cos", [P, COLS])
        k_sin = sb("k_sin", [P, COLS])
        v_small = sb("v_small", [META, P])
        square = sb("square", [P, FT, REAL])
        rms_r = sb("rms_r", [P, NB])
        ssq_r = sb("ssq_r", [P, NB])
        ps_k = ctx.enter_context(nc.psum_tensor("ps_k", [P, 3, BANK], F32))
        ps_v = ctx.enter_context(nc.psum_tensor("ps_v", [P, 3, BANK], F32))
        ps_s = ctx.enter_context(nc.psum_tensor("ps_s", [P, BANK], F32))
        ps_m = ctx.enter_context(nc.psum_tensor("ps_m", [P, BANK], F32))

        swap_in = sem("k_swap_in")
        tables_in = sem("k_tables_in")
        cleared = sem("k_cleared")
        vmeta_in = sem("k_vmeta_in")
        k_swapped = sem("k_swapped")
        v_turned = sem("k_v_turned")
        k_cos_done = sem("k_cos_done")
        k_sin_done = sem("k_sin_done")
        v_out = sem("k_v_out")
        sq_done = sem("k_sq_done")
        ss_done = sem("k_ss_done")
        ss_summed = sem("k_ss_summed")
        rms_done = sem("k_rms_done")
        block = ctx.enter_context(nc.Block())

        @block.sync
        def _(sp):
            sp.dma_start(swap[:, :], a["swap"]).then_inc(swap_in, 16)
            sp.dma_start(cos[:, :], a["cos"]).then_inc(tables_in, 16)
            sp.dma_start(sin[:, :], a["sin"]).then_inc(tables_in, 16)
            sp.wait_ge(v_out, 1)
            sp.wait_ge(cleared, 4)
            for h in range(HEADS):
                g = h // 4
                sp.dma_start(v_meta[h * META:(h + 1) * META, h * HD:(h + 1) * HD],
                             v_small[:, g * HD:(g + 1) * HD]).then_inc(vmeta_in, 16)
            sp.wait_ge(vmeta_in, 16 * HEADS)

        @block.gpsimd
        def _(pool):
            pool.memset(v_meta[:, :], 0.0).then_inc(cleared, 1)
            pool.memset(ones[:, :], 1.0).then_inc(cleared, 1)
            for lo, hi, t in ((META, META + P, k_rot), (META + P + REAL, META + 2 * P + REAL, k_rot)):
                pool.memset(t[:, lo:hi], 0.0)
            pool.memset(v_tok[:, 0:P], 0.0).then_inc(cleared, 1)
            pool.memset(v_tok[:, (NB + 1) * P:(NB + 2) * P], 0.0).then_inc(cleared, 1)
            pool.wait_ge(tables_in, 32)
            pool.tensor_tensor(k_cos[:, :], k_pre[:, :], cos[:, :], ALU.mult).then_inc(k_cos_done, 1)

        @block.tensor
        def _(pe):
            pe.transpose(ps_m[0:META, 0:P], v_pre[:, 0:META], ident[:, :]).then_inc(v_turned, 1)
            for b in range(NB):
                mm = pe.transpose(ps_v[:, b // 4, (b % 4) * P:(b % 4 + 1) * P],
                                  v_pre[:, META + b * P:META + (b + 1) * P], ident[:, :])
            mm.then_inc(v_turned, 1)
            pe.wait_ge(swap_in, 16)
            for c in range(NCH):
                mm = pe.matmul(ps_k[:, c, 0:CH], swap[:, :], k_pre[:, c * CH:(c + 1) * CH], start=True, stop=True)
            mm.then_inc(k_swapped, 1)
            pe.wait_ge(cleared, 4)
            for ft in range(FT):
                pe.wait_ge(sq_done, ft + 1)
                for b in range(NB):
                    n = ft * NB + b
                    mm = pe.matmul(ps_s[:, n:n + 1], square[:, ft, b * P:(b + 1) * P], ones[:, :], start=True, stop=True)
            mm.then_inc(ss_done, 1)

        @block.scalar
        def _(act):
            act.wait_ge(v_turned, 1)
            act.activation(v_small[:, :], ps_m[0:META, 0:P], ACT.Copy).then_inc(v_out, 1)
            act.wait_ge(v_turned, 2)
            act.activation(v_tok[:, P:(NB + 1) * P], ps_v[:, :, :].rearrange("p b c -> p (b c)")[:, 0:REAL], ACT.Copy)
            for ft in range(FT):
                act.activation(square[:, ft, :], yg[:, ft, META:COLS], ACT.Square).then_inc(sq_done, 1)
            act.wait_ge(ss_summed, 1)
            act.activation(rms_r[:, :], ssq_r[:, :], ACT.Sqrt, bias=eps_t[:, :], scale=1.0 / REC).then_inc(rms_done, 1)

        @block.vector
        def _(dve):
            dve.wait_ge(k_swapped, 1)
            dve.wait_ge(tables_in, 32)
            for c in range(NCH):
                ins = dve.tensor_tensor(k_sin[:, c * CH:(c + 1) * CH], ps_k[:, c, 0:CH], sin[:, c * CH:(c + 1) * CH], ALU.mult)
            ins.then_inc(k_sin_done, 1)
            dve.wait_ge(k_sin_done, 1)
            dve.wait_ge(k_cos_done, 1)
            dve.tensor_tensor(k_rot[:, 0:META], k_cos[:, 0:META], k_sin[:, 0:META], ALU.add)
            dve.tensor_tensor(k_rot[:, META + P:META + P + REAL], k_cos[:, META:COLS], k_sin[:, META:COLS], ALU.add)
            dve.wait_ge(ss_done, 1)
            dve.tensor_reduce(ssq_r[:, :], ps_s[:, 0:FT * NB].rearrange("p (f b) -> p b f", b=NB), AX.X,
                              ALU.add).then_inc(ss_summed, 1)
            dve.wait_ge(rms_done, 1)
            dve.reciprocal(rstd_rec[:, :], rms_r[:, :])


LAM_STEPS = 27


def mix(nc, sem, a, q_pre, rec, rstd_rec, k_rot, v_tok, v_meta, ident, eps_t, iota_e,
        gate1, gate2, expert1, expert2, place1, place2, counts, h2_dram, u_dram, list_dram):
    with ExitStack() as ctx:
        def sb(name, shape, dt=F32):
            return ctx.enter_context(nc.sbuf_tensor(name, shape, dt))

        w_hi = sb("wo_hi", [P, KD, D], F32R)
        w_lo = sb("wo_lo", [P, KD, D], F32R)
        g_out = sb("g_out", [P, KD])
        g_ffn = sb("g_ffn", [P, D])
        router = sb("router", [P, KD, ROUT])
        rbias = sb("rbias_bc", [P, ROUT])
        sink = sb("sink_bc", [P, HEADS])
        swap = sb("swap_q", [P, P])
        before = sb("before_sb", [P, P])
        ones = sb("ones_m", [P, P])
        group_of = sb("group_of", [P, EXP])
        token = sb("token", [P, NB], I32)
        mask = [sb(f"mask{s}", [P, KEYS]) for s in range(RING)]
        cos = [sb(f"cos_q{s}", [P, P]) for s in range(RING)]
        sin = [sb(f"sin_q{s}", [P, P]) for s in range(RING)]
        xh = [sb(f"xh{s}", [P, D]) for s in range(RING)]
        u = sb("u_sb", [P, D])
        q_cos = sb("q_cos", [P, ATTN])
        q_sin = sb("q_sin", [P, ATTN])
        qz = sb("qz", [P, HEADS, P])
        probs = sb("probs", [P, HEADS, KEYS])
        probs_t = sb("probs_t", [P, HEADS, WIN])
        meta_p = sb("meta_p", [P, P])
        meta_t = sb("meta_t", [P, P])
        smax = sb("smax", [P, HEADS])
        nmax = sb("nmax", [P, HEADS])
        rowsum = sb("rowsum", [P, HEADS])
        sink_d = sb("sink_d", [P, HEADS])
        sink_e = sb("sink_e", [P, HEADS])
        den = sb("den", [P, HEADS])
        rden = sb("rden", [P, HEADS])
        attn_o = sb("attn_o", [P, ATTN])
        junk = sb("junk", [P, ATTN])
        ssq_a = sb("ssq_a", [P, 1])
        rms_a = sb("rms_a", [P, 1])
        rstd_a = sb("rstd_a", [P, 1])
        a_hi = sb("a_hi", [P, FT, P], F32R)
        a_lo = sb("a_lo", [P, FT, P], F32R)
        r_hi = sb("rec_hi", [P, FT, P], F32R)
        r_lo = sb("rec_lo", [P, FT, P], F32R)
        ssq_h = sb("ssq_h", [P, 1])
        rms_h = sb("rms_h", [P, 1])
        rstd_h = sb("rstd_h", [P, 1])
        u_t = sb("u_t", [P, KD, P])
        logits = sb("logits", [P, ROUT])
        gtop = sb("gtop", [P, 8])
        gidx = sb("gidx", [P, 8], U32)
        gidx_f = sb("gidx_f", [P, 1])
        ngtop = sb("ngtop", [P, 1])
        gexp = sb("gexp", [P, 4])
        gsum = sb("gsum", [P, 1])
        mlog = sb("mlog", [P, EXP])
        etop = sb("etop", [P, 8])
        eidx = sb("eidx", [P, 8], U32)
        ediff = sb("ediff", [P, 1])
        eexp = sb("eexp", [P, 1])
        gden = sb("gden", [P, 1])
        hot1 = sb("hot1", [P, EXP])
        hot2 = sb("hot2", [P, EXP])
        hot = sb("hot", [P, EXP])
        base = sb("base", [P, EXP])
        prod = [sb(f"prod{j}", [P, EXP]) for j in range(2)]
        token_s = [sb(f"token_s{s}", [P, 1], I32) for s in range(RING)]
        addr = [[sb(f"addr{j}{s}", [P, 1], I32) for s in range(RING)] for j in range(2)]

        ps_sc = [ctx.enter_context(nc.psum_tensor(f"ps_sc{s}", [P, BANK], F32)) for s in range(2)]
        ps_t = [ctx.enter_context(nc.psum_tensor(f"ps_t{s}", [P, BANK], F32)) for s in range(2)]
        ps_o = ctx.enter_context(nc.psum_tensor("ps_o", [P, BANK], F32))
        ps_y = [ctx.enter_context(nc.psum_tensor(f"ps_y{s}", [P, BANK], F32)) for s in range(2)]
        ps_x = ctx.enter_context(nc.psum_tensor("ps_x", [P, BANK], F32))

        waited = sem("m_waited")
        consts_in = sem("m_consts_in")
        w_in = [sem(f"m_w_in{s}") for s in range(RING)]
        w_hi_done = sem("m_w_hi_done")
        w_lo_done = sem("m_w_lo_done")
        cleared = sem("m_cleared")
        tables_in = [sem(f"m_tables_in{s}") for s in range(RING)]
        x_in = [sem(f"m_x_in{s}") for s in range(RING)]
        h2_out = sem("m_h2_out")
        u_out = sem("m_u_out")
        q_swapped = sem("m_q_swapped")
        q_cos_done = sem("m_q_cos_done")
        q_sin_done = sem("m_q_sin_done")
        qz_done = sem("m_qz_done")
        scored = sem("m_scored")
        scaled = sem("m_scaled")
        nmax_done = sem("m_nmax_done")
        exp_done = sem("m_exp_done")
        sink_d_done = sem("m_sink_d_done")
        sink_e_done = sem("m_sink_e_done")
        turned = sem("m_turned")
        pt_out = sem("m_pt_out")
        meta_packed = sem("m_meta_packed")
        meta_turned = sem("m_meta_turned")
        meta_out = sem("m_meta_out")
        av_done = sem("m_av_done")
        den_done = sem("m_den_done")
        ao_done = sem("m_ao_done")
        ssq_a_done = sem("m_ssq_a_done")
        rms_a_done = sem("m_rms_a_done")
        rstd_a_done = sem("m_rstd_a_done")
        ao_turned = sem("m_ao_turned")
        a_hi_done = sem("m_a_hi_done")
        a_lo_done = sem("m_a_lo_done")
        r_hi_done = sem("m_r_hi_done")
        r_lo_done = sem("m_r_lo_done")
        y_done = sem("m_y_done")
        y_read = sem("m_y_read")
        ssq_h_done = sem("m_ssq_h_done")
        rms_h_done = sem("m_rms_h_done")
        rstd_h_done = sem("m_rstd_h_done")
        u_done = sem("m_u_done")
        u_turned = sem("m_u_turned")
        u_t_out = sem("m_u_t_out")
        logits_done = sem("m_logits_done")
        route_step = sem("m_route_step")
        gexp_done = sem("m_gexp_done")
        eexp_done = sem("m_eexp_done")
        ranked = sem("m_ranked")
        place_step = sem("m_place_step")
        token_done = sem("m_token_done")
        addr_done = sem("m_addr_done")
        listed = [sem(f"m_listed{s}") for s in range(RING)]

        AT_LOGITS, AT_NGTOP, AT_EDIFF, AT_HOT, ROUTE_STEPS = 1, 5, 9, 18, 18
        PLACE_STEPS = 8
        PLACE0 = 2 * PLACE_STEPS

        block = ctx.enter_context(nc.Block())

        def take_waits(eng):
            eng.sem_inc(waited, 1)

        def run(eng, step, peeled=0, behind_first=lambda: None):
            step(0, None, None, 0)
            behind_first()
            step(1, 0, None, 1)
            with eng.Fori(0, (NB - peeled) // 2 - 1) as i:
                step(2 * i + 2, 2 * i + 1, 2 * i, 0)
                step(2 * i + 3, 2 * i + 2, 2 * i + 1, 1)
            for t in range(NB - peeled, NB):
                step(t, t - 1, t - 2, t % 2)
            step(None, NB - 1, NB - 2, 0)
            step(None, None, NB - 1, 1)

        def at_most_blocks(v):
            return min(v, NB) if isinstance(v, int) else v

        def half(i):
            return slice(i * BANK, (i + 1) * BANK)

        @block.sync
        def _(sp):
            for dst, src in ((g_out[:, :], a["g_out"]), (g_ffn[:, :], a["ln_ffn_g"][0].partition_broadcast(P)),
                             (router[:, :, :], a["router"]), (rbias[:, :], a["rbias"][0].partition_broadcast(P)),
                             (sink[:, :], a["sink"][0].partition_broadcast(P)), (swap[:, :], a["swap"]),
                             (before[:, :], a["before"])):
                sp.dma_start(dst, src).then_inc(consts_in, 16)

            def tables(t, s):
                sp.dma_start(mask[s][:, :], a["masks"][bass.ds(t, 1), :, :].rearrange("o p c -> (o p) c")).then_inc(tables_in[s], 16)
                sp.dma_start(cos[s][:, :], a["cos"][:, bass.ds(META + t * P, P)]).then_inc(tables_in[s], 16)
                sp.dma_start(sin[s][:, :], a["sin"][:, bass.ds(META + t * P, P)]).then_inc(tables_in[s], 16)

            def load_x(t, s):
                sp.dma_start(xh[s][:, :], a["x"][bass.ds(t * P, P), :]).then_inc(x_in[s], 16)

            tables(0, 0)
            for k in range(KD):
                if k >= RING:
                    sp.wait_ge(w_lo_done, k - RING + 1)
                sp.dma_start(xh[k % RING][:, :], a["w_out"][:, k, :]).then_inc(w_in[k % RING], 16)
            sp.wait_ge(w_lo_done, KD)
            load_x(0, 0)

            def attn(t, s):
                if isinstance(t, int) and t == 0:
                    tables(1, 1)
                    return
                if isinstance(t, int) and t == NB - 1:
                    return
                sp.wait_ge(nmax_done, 2 * t)
                sp.wait_ge(q_cos_done, t)
                sp.wait_ge(q_sin_done, t)
                tables(t + 1, 1 - s)

            def outer(b, s):
                sp.wait_ge(u_done, b + 1)
                sp.dma_start(h2_dram[bass.ds(b * P, P), :], xh[s][:, :]).then_inc(h2_out, 16)
                sp.dma_start(u_dram[bass.ds(b * P, P), :], u[:, :]).then_inc(u_out, 16)
                sp.wait_ge(h2_out, 16 * b + 16)
                if not isinstance(b, int) or b + 2 < NB:
                    load_x(b + 2, s)

            load_x(1, 1)

            def step(t, b1, b2, s):
                if t is not None:
                    attn(t, s)
                if b1 is not None:
                    outer(b1, 1 - s)

            run(sp, step, peeled=2)
            sp.wait_ge(u_out, 16 * NB)
            for s in range(RING):
                sp.wait_ge(listed[s], 32 * NB // 2)

        @block.gpsimd
        def _(pool):
            pool.memset(qz[:, :, :], 0.0).then_inc(cleared, 1)
            pool.memset(ones[:, :], 1.0).then_inc(cleared, 1)
            pool.memset(counts[:, :], 0.0).then_inc(cleared, 1)
            pool.iota(group_of[:, :], pattern=[[1, 4], [0, 8]], base=0, channel_multiplier=0,
                      allow_small_or_imprecise_dtypes=True).then_inc(cleared, 1)
            pool.iota(token[:, :], pattern=[[P, NB]], base=0, channel_multiplier=1).then_inc(cleared, 1)
            pool.wait_ge(cleared, 5)

            def attn(t, s):
                pool.wait_ge(tables_in[s], 48 * (t // 2 + 1) if isinstance(t, int) else 24 * (t - s) + 48)
                pool.wait_ge(qz_done, t + 1)
                pool.tensor_tensor(q_cos[:, :].rearrange("p (h c) -> p h c", c=P), q_pre[:, :, bass.ds(META + t * P, P)],
                                   cos[s][:, :].unsqueeze(1).to_broadcast([P, 4, P]), ALU.mult).then_inc(q_cos_done, 1)
                pool.wait_ge(exp_done, HEADS * t + HEADS)
                pool.wait_ge(meta_turned, t) if not isinstance(t, int) or t > 0 else None
                take_waits(pool)
                pool.tensor_copy(meta_p[:, :].rearrange("p (h m) -> p h m", m=META), probs[:, :, WIN:KEYS]).then_inc(meta_packed, 1)

                pool.wait_ge(r_hi_done, t + 1)
                pool.tensor_tensor(r_lo[:, :, :], rec[:, :, bass.ds(t * P, P)], r_hi[:, :, :].bitcast(F32),
                                   ALU.subtract).then_inc(r_lo_done, 1)

            def place(b, s):
                pool.wait_ge(addr_done, 2 * b + 2)
                if not isinstance(b, int) or b >= 2:
                    pool.wait_ge(listed[s], 16 * (b - s))
                take_waits(pool)
                pool.tensor_copy(token_s[s][:, :], token[:, bass.ds(b, 1)]).then_inc(token_done, 1)
                pool.wait_ge(token_done, b + 1)
                take_waits(pool)
                for j in range(2):
                    pool.indirect_dma_start(list_dram, bass.IndirectOffsetOnAxis(ap=addr[j][s][:, 0:1], axis=0),
                                            token_s[s][:, 0:1], None).then_inc(listed[s], 16)

            def step(t, b1, b2, s):
                if t is not None:
                    attn(t, s)
                if b2 is not None:
                    place(b2, s)

            run(pool, step)

        @block.tensor
        def _(pe):
            pe.wait_ge(consts_in, 112)
            pe.wait_ge(cleared, 5)
            pe.sem_inc(av_done, 1)
            pe.sem_inc(logits_done, 1)

            def swap_q(t):
                if not isinstance(t, int) or t >= 2:
                    pe.wait_ge(place_step, PLACE_STEPS * t - PLACE_STEPS + 2)
                pe.matmul(ps_x[:, :], swap[:, :], q_pre[:, :, bass.ds(META + t * P, P)], start=True, stop=True
                          ).then_inc(q_swapped, 1)

            def scores(t, heads):
                if heads[0] == 0:
                    pe.wait_ge(qz_done, t + 2)
                for h in heads:
                    pe.wait_ge(scaled, HEADS * t + h + 1)
                    pe.matmul(ps_sc[h % 2][:, 0:WIN], qz[:, h, :], k_rot[:, bass.ds(META + t * P, WIN)], start=True, stop=True,
                              skip_group_check=True)
                    pe.matmul(ps_sc[h % 2][:, WIN:KEYS], qz[:, h, :], k_rot[:, 0:META], start=True, stop=True,
                              skip_group_check=True).then_inc(scored, 1)

            def turn_probs(t, heads):
                for h in heads:
                    n = HEADS * t + h
                    pe.wait_ge(exp_done, n + 1)
                    pe.wait_ge(pt_out, n + 1)
                    for j in range(3):
                        mm = pe.transpose(ps_t[h % 2][:, j * P:(j + 1) * P], probs[:, h, j * P:(j + 1) * P], ident[:, :])
                    mm.then_inc(turned, 1)

            def times_v(t):
                pe.wait_ge(ao_done, t + 1)
                pe.wait_ge(meta_packed, t + 1)
                pe.transpose(ps_o[:, 0:P], meta_p[:, :], ident[:, :]).then_inc(meta_turned, 1)
                pe.wait_ge(meta_out, t + 1)
                pe.matmul(ps_o[:, :], meta_t[:, :], v_meta[:, :], start=True, stop=False, skip_group_check=True)
                for h in range(HEADS):
                    pe.wait_ge(pt_out, HEADS * t + h + 3)
                    for j in range(3):
                        last = h == HEADS - 1 and j == 2
                        mm = pe.matmul(ps_o[:, h * HD:(h + 1) * HD], probs_t[:, h, j * P:(j + 1) * P],
                                       v_tok[:, bass.ds(t * P + j * P + (h // 4) * HD, HD)], start=False, stop=last,
                                       skip_group_check=True)
                mm.then_inc(av_done, 1)

            def turn_u(b, i):
                if i == 0:
                    pe.wait_ge(u_done, b + 1)
                else:
                    pe.wait_ge(a_lo_done, at_most_blocks(b + 2) + 2)
                for k in range(4):
                    mm = pe.transpose(ps_t[1 - i][:, k * P:(k + 1) * P], u[:, (4 * i + k) * P:(4 * i + k + 1) * P], ident[:, :])
                mm.then_inc(u_turned, 1)

            def route(b):
                pe.wait_ge(u_t_out, 2 * b + 4)
                pe.wait_ge(q_sin_done, at_most_blocks(b + 3))
                if isinstance(b, int) and b >= NB - 2:
                    pe.wait_ge(place_step, PLACE_STEPS * (b - 1) + PLACE0 + 2)
                for k in range(KD):
                    mm = pe.matmul(ps_x[:, 0:ROUT], u_t[:, k, :], router[:, k, :], start=(k == 0), stop=(k == KD - 1))
                mm.then_inc(logits_done, 1)

            def turn_attn(b):
                pe.wait_ge(ao_done, b + 2)
                for k in range(FT):
                    mm = pe.transpose(ps_t[0][:, k * P:(k + 1) * P], attn_o[:, k * P:(k + 1) * P], ident[:, :])
                mm.then_inc(ao_turned, 1)

            def out_product(b, part, i):
                x_hi, x_lo, k0 = ((r_hi, r_lo, FT), (a_hi, a_lo, 0))[part]
                if isinstance(b, int) and b == 0:
                    pe.wait_ge(w_lo_done, KD)
                if part == 0:
                    pe.wait_ge(r_lo_done, b + 1)
                else:
                    pe.wait_ge(a_lo_done, b + 3)
                pe.wait_ge(y_read, 4 * b + 2 * part + i + 1)
                for k in range(FT):
                    for n, (x, w) in enumerate(((x_hi, w_hi), (x_hi, w_lo), (x_lo, w_hi))):
                        mm = pe.matmul(ps_y[i][:, :], x[:, k, :], w[:, k0 + k, half(i)],
                                       start=(k == 0 and n == 0), stop=(k == FT - 1 and n == 2))
                mm.then_inc(y_done, 1)

            def place(b):
                pe.wait_ge(route_step, ROUTE_STEPS * b + AT_HOT)
                pe.matmul(ps_x[:, 0:EXP], before[:, :], hot[:, :], start=True, stop=True)
                pe.matmul(ps_x[:, EXP:2 * EXP], ones[:, :], hot[:, :], start=True, stop=True).then_inc(ranked, 1)

            def step(t, b1, b2, s):
                if t is not None:
                    swap_q(t)
                if b1 is not None:
                    out_product(b1, 0, 0)
                    turn_attn(b1)
                if b2 is not None:
                    turn_u(b2, 0)
                if t is not None:
                    scores(t, range(0, 4))
                if b2 is not None:
                    turn_u(b2, 1)
                if b1 is not None:
                    out_product(b1, 0, 1)
                if t is not None:
                    scores(t, range(4, 8))
                if b2 is not None:
                    route(b2)
                if b1 is not None:
                    out_product(b1, 1, 0)
                if t is not None:
                    turn_probs(t, range(0, 4))
                if b1 is not None:
                    out_product(b1, 1, 1)
                if t is not None:
                    turn_probs(t, range(4, 8))
                if b2 is not None:
                    place(b2)
                if t is not None:
                    times_v(t)

            run(pe, step)

        @block.scalar
        def _(act):
            act.wait_ge(consts_in, 112)

            def split_w():
                for k in range(KD):
                    act.wait_ge(w_in[k % RING], 16 * (k // RING + 1))
                    act.activation(w_hi[:, k, :], xh[k % RING][:, :], ACT.Copy, scale=g_out[:, k:k + 1]).then_inc(w_hi_done, 1)

            def exponentials(t, heads):
                act.wait_ge(nmax_done, 2 * t + heads[0] // 4 + 1)
                if heads[0] == 0:
                    act.wait_ge(den_done, 2 * t + 1)
                for h in heads:
                    act.activation(probs[:, h, :], probs[:, h, :], ACT.Exp, bias=nmax[:, h:h + 1],
                                   accum_out=rowsum[:, h:h + 1]).then_inc(exp_done, 1)

            def sink_and_rec(t):
                act.wait_ge(sink_d_done, t + 1)
                act.activation(sink_e[:, :], sink_d[:, :], ACT.Exp).then_inc(sink_e_done, 1)
                if not isinstance(t, int) or t > 0:
                    act.wait_ge(y_done, 4 * t - 2)
                    act.wait_ge(r_lo_done, t)
                act.activation(r_hi[:, :, :], rec[:, :, bass.ds(t * P, P)], ACT.Copy).then_inc(r_hi_done, 1)

            def probs_out(t, heads):
                for h in heads:
                    act.wait_ge(turned, HEADS * t + h + 1)
                    if h == 0:
                        act.wait_ge(av_done, t + 1)
                    act.activation(probs_t[:, h, :], ps_t[h % 2][:, 0:WIN], ACT.Copy).then_inc(pt_out, 1)

            def meta_copy(t):
                act.wait_ge(meta_turned, t + 1)
                act.activation(meta_t[:, :], ps_o[:, 0:P], ACT.Copy).then_inc(meta_out, 1)

            def u_out_of_psum(b, i):
                act.wait_ge(logits_done, b + 1)
                act.wait_ge(u_turned, 2 * b + i + 1)
                act.activation(u_t[:, 4 * i:4 * i + 4, :], ps_t[1 - i][:, :].rearrange("p (k c) -> p k c", c=P), ACT.Copy
                               ).then_inc(u_t_out, 1)

            def route(b):
                act.wait_ge(route_step, ROUTE_STEPS * b + AT_NGTOP)
                act.activation(gexp[:, :], logits[:, 0:4], ACT.Exp, bias=ngtop[:, :], accum_out=gsum[:, :]).then_inc(gexp_done, 1)
                act.wait_ge(route_step, ROUTE_STEPS * b + AT_EDIFF)
                act.activation(eexp[:, :], ediff[:, :], ACT.Exp).then_inc(eexp_done, 1)

            def attn_rms(b):
                act.wait_ge(ao_done, b + 2)
                if not isinstance(b, int) or b > 0:
                    act.wait_ge(ssq_a_done, b)
                    act.wait_ge(rms_a_done, b)
                act.activation(junk[:, :], attn_o[:, :], ACT.Square, accum_out=ssq_a[:, :]).then_inc(ssq_a_done, 1)
                act.wait_ge(ssq_a_done, b + 1)
                act.wait_ge(rstd_a_done, b) if not isinstance(b, int) or b > 0 else None
                act.activation(rms_a[:, :], ssq_a[:, :], ACT.Sqrt, bias=eps_t[:, :], scale=1.0 / ATTN).then_inc(rms_a_done, 1)

            def attn_split(b):
                act.wait_ge(y_done, 4 * b) if not isinstance(b, int) or b > 0 else None
                act.wait_ge(ao_turned, b + 1)
                act.activation(a_hi[:, :, :], ps_t[0][:, :].rearrange("p (k c) -> p k c", c=P), ACT.Copy).then_inc(a_hi_done, 1)

            def h2_rms(b, s):
                act.wait_ge(y_read, 4 * b + 6)
                if not isinstance(b, int) or b > 0:
                    act.wait_ge(u_turned, 2 * b)
                    act.wait_ge(u_out, 16 * b)
                    act.wait_ge(rms_h_done, b)
                act.activation(u[:, :], xh[s][:, :], ACT.Square, accum_out=ssq_h[:, :]).then_inc(ssq_h_done, 1)
                act.wait_ge(ssq_h_done, b + 1)
                act.wait_ge(rstd_h_done, b) if not isinstance(b, int) or b > 0 else None
                act.activation(rms_h[:, :], ssq_h[:, :], ACT.Sqrt, bias=eps_t[:, :], scale=1.0 / D).then_inc(rms_h_done, 1)

            def step(t, b1, b2, s):
                if b1 is not None:
                    attn_rms(b1)
                    attn_split(b1)
                if b2 is not None:
                    u_out_of_psum(b2, 0)
                if t is not None:
                    exponentials(t, range(0, 4))
                if b2 is not None:
                    u_out_of_psum(b2, 1)
                if t is not None:
                    exponentials(t, range(4, 8))
                    sink_and_rec(t)
                if b2 is not None:
                    route(b2)
                if t is not None:
                    probs_out(t, range(HEADS))
                    meta_copy(t)
                if b1 is not None:
                    h2_rms(b1, 1 - s)

            act.sem_inc(u_t_out, 2)
            act.sem_inc(pt_out, 2)
            run(act, step, behind_first=split_w)

        @block.vector
        def _(dve):
            dve.sem_inc(a_lo_done, 2)
            dve.sem_inc(scaled, 2)
            dve.sem_inc(place_step, PLACE0)
            dve.sem_inc(ao_done, 1)
            dve.sem_inc(qz_done, 1)
            dve.sem_inc(den_done, 1)
            dve.sem_inc(y_read, 2)
            dve.wait_ge(consts_in, 112)

            def split_w():
                for k in range(KD):
                    dve.wait_ge(w_hi_done, k + 1)
                    dve.scalar_tensor_tensor(out=w_lo[:, k, :], in0=xh[k % RING][:, :], scalar=g_out[:, k:k + 1],
                                             in1=w_hi[:, k, :].bitcast(F32), op0=ALU.mult, op1=ALU.subtract).then_inc(w_lo_done, 1)

            dve.wait_ge(cleared, 5)

            def rope_q(t, s):
                dve.wait_ge(q_swapped, t + 1)
                dve.wait_ge(tables_in[s], 48 * (t // 2 + 1) if isinstance(t, int) else 24 * (t - s) + 48)
                dve.wait_ge(qz_done, t + 1)
                dve.tensor_tensor(q_sin[:, :].rearrange("p (h c) -> p h c", c=P), ps_x[:, :].rearrange("p (h c) -> p h c", c=P),
                                  sin[s][:, :].unsqueeze(1).to_broadcast([P, 4, P]), ALU.mult).then_inc(q_sin_done, 1)
                dve.wait_ge(q_sin_done, t + 1)
                dve.wait_ge(q_cos_done, t + 1)
                dve.wait_ge(scored, HEADS * t) if not isinstance(t, int) or t > 0 else None
                dve.tensor_tensor(qz[0:HD, 0:4, :], q_cos[0:HD, :].rearrange("p (h c) -> p h c", c=P),
                                  q_sin[0:HD, :].rearrange("p (h c) -> p h c", c=P), ALU.add)
                dve.tensor_tensor(qz[HD:P, 4:8, :], q_cos[HD:P, :].rearrange("p (h c) -> p h c", c=P),
                                  q_sin[HD:P, :].rearrange("p (h c) -> p h c", c=P), ALU.add).then_inc(qz_done, 1)
            def softmax_max(t, s, heads):
                for h in heads:
                    n = HEADS * t + h
                    dve.wait_ge(scored, n + 1)
                    if h == 0 and (not isinstance(t, int) or t > 0):
                        dve.wait_ge(meta_turned, t)
                        dve.wait_ge(exp_done, HEADS * t)
                        dve.wait_ge(sink_d_done, t)
                        dve.wait_ge(nmax_done, 2 * t)
                    take_waits(dve)
                    dve.tensor_tensor_reduce(probs[:, h, :], ps_sc[h % 2][:, 0:KEYS], mask[s][:, :], HD ** -0.5, sink[:, h:h + 1],
                                             ALU.add, ALU.max, smax[:, h:h + 1]).then_inc(scaled, 1)
                h = heads[-1]
                dve.wait_ge(scaled, HEADS * t + h + 3)
                dve.tensor_scalar(nmax[:, h - 3:h + 1], smax[:, h - 3:h + 1], -1.0, None, ALU.mult).then_inc(nmax_done, 1)

            def sink_diff(t):
                dve.wait_ge(nmax_done, 2 * t + 2)
                dve.wait_ge(sink_e_done, t) if not isinstance(t, int) or t > 0 else None
                dve.tensor_tensor(sink_d[:, :], sink[:, :], nmax[:, :], ALU.add).then_inc(sink_d_done, 1)

            def route(b):
                n = [0]

                def then(ins):
                    n[0] += 1
                    ins.then_inc(route_step, 1)
                    dve.wait_ge(route_step, ROUTE_STEPS * b + n[0])

                dve.wait_ge(logits_done, b + 2)
                if not isinstance(b, int) or b > 0:
                    dve.wait_ge(ranked, b)
                    dve.wait_ge(gexp_done, b)
                    dve.wait_ge(place_step, PLACE_STEPS * b + PLACE0)
                here = bass.ds(b, 1)
                then(dve.tensor_tensor(logits[:, :], ps_x[:, 0:ROUT], rbias[:, :], ALU.add))
                take_waits(dve)
                then(dve.max(gtop[:, :], logits[:, 0:8]))
                take_waits(dve)
                then(dve.max_index(gidx[:, :], gtop[:, :], logits[:, 0:8]))
                then(dve.tensor_copy(gidx_f[:, :], gidx[:, 0:1]))
                then(dve.tensor_scalar(ngtop[:, :], gtop[:, 0:1], -1.0, None, ALU.mult))
                assert n[0] == AT_NGTOP
                then(dve.tensor_scalar(mlog[:, :], group_of[:, :], gidx_f[:, 0:1], NEG, ALU.not_equal, ALU.mult))
                then(dve.tensor_tensor(mlog[:, :], mlog[:, :], logits[:, 8:ROUT], ALU.add))
                take_waits(dve)
                then(dve.max(etop[:, :], mlog[:, :]))
                then(dve.tensor_tensor(ediff[:, :], etop[:, 1:2], etop[:, 0:1], ALU.subtract))
                assert n[0] == AT_EDIFF
                take_waits(dve)
                then(dve.max_index(eidx[:, :], etop[:, :], mlog[:, :]))
                then(dve.tensor_copy(expert1[:, here], eidx[:, 0:1]))
                then(dve.tensor_copy(expert2[:, here], eidx[:, 1:2]))
                dve.wait_ge(gexp_done, b + 1)
                dve.wait_ge(eexp_done, b + 1)
                then(dve.scalar_tensor_tensor(out=gden[:, :], in0=eexp[:, :], scalar=1.0, in1=gsum[:, :], op0=ALU.add, op1=ALU.mult))
                then(dve.reciprocal(gate1[:, here], gden[:, :]))
                then(dve.tensor_tensor(gate2[:, here], gate1[:, here], eexp[:, :], ALU.mult))
                then(dve.tensor_scalar(hot1[:, :], iota_e[:, :], expert1[:, here], None, ALU.is_equal))
                then(dve.tensor_scalar(hot2[:, :], iota_e[:, :], expert2[:, here], None, ALU.is_equal))
                then(dve.tensor_tensor(hot[:, :], hot1[:, :], hot2[:, :], ALU.add))
                assert n[0] == ROUTE_STEPS

            def attn_split(b):
                dve.wait_ge(a_hi_done, b + 1)
                dve.wait_ge(y_done, 4 * b) if not isinstance(b, int) or b > 0 else None
                dve.tensor_tensor(a_lo[:, :, :], ps_t[0][:, :].rearrange("p (k c) -> p k c", c=P), a_hi[:, :, :].bitcast(F32),
                                  ALU.subtract).then_inc(a_lo_done, 1)

            def attn_rstd(b):
                dve.wait_ge(rms_a_done, b + 1)
                dve.wait_ge(y_read, 4 * b + 2)
                dve.reciprocal(rstd_a[:, :], rms_a[:, :]).then_inc(rstd_a_done, 1)

            def residual(b, s, part, i):
                if part == 0 and i == 0:
                    dve.wait_ge(x_in[s], 16 * (b // 2 + 1) if isinstance(b, int) else 8 * (b - s) + 16)
                if part == 1:
                    dve.wait_ge(rstd_a_done, b + 1)
                    dve.wait_ge(y_read, 4 * b + i + 3)
                factor = rstd_rec[:, bass.ds(b, 1)] if part == 0 else rstd_a[:, 0:1]
                dve.wait_ge(y_done, 4 * b + 2 * part + i + 1)
                dve.scalar_tensor_tensor(out=xh[s][:, half(i)], in0=ps_y[i][:, :], scalar=factor, in1=xh[s][:, half(i)],
                                         op0=ALU.mult, op1=ALU.add).then_inc(y_read, 1)

            def ffn_norm(b, s):
                dve.wait_ge(rms_h_done, b + 1)
                dve.wait_ge(u_done, b) if not isinstance(b, int) or b > 0 else None
                dve.reciprocal(rstd_h[:, :], rms_h[:, :]).then_inc(rstd_h_done, 1)
                dve.wait_ge(rstd_h_done, b + 1)
                dve.scalar_tensor_tensor(out=u[:, :], in0=xh[s][:, :], scalar=rstd_h[:, 0:1], in1=g_ffn[:, :],
                                         op0=ALU.mult, op1=ALU.mult).then_inc(u_done, 1)

            def place(b, s):
                n = [0]

                def then(ins):
                    n[0] += 1
                    ins.then_inc(place_step, 1)
                    dve.wait_ge(place_step, PLACE_STEPS * b + PLACE0 + n[0])

                dve.wait_ge(ranked, b + 1)
                if not isinstance(b, int) or b >= 2:
                    dve.wait_ge(listed[s], 16 * (b - s))
                here = bass.ds(b, 1)
                then(dve.tensor_tensor(base[:, :], ps_x[:, 0:EXP], counts[:, :], ALU.add))
                then(dve.tensor_tensor(counts[:, :], counts[:, :], ps_x[:, EXP:2 * EXP], ALU.add))
                for j, (hot_j, place_j, expert_j) in enumerate(((hot1, place1, expert1), (hot2, place2, expert2))):
                    then(dve.tensor_tensor(prod[j][:, :], base[:, :], hot_j[:, :], ALU.mult))
                    then(dve.tensor_reduce(place_j[:, here], prod[j][:, :], AX.X, ALU.add))
                    then(dve.scalar_tensor_tensor(out=gden[:, :], in0=expert_j[:, here], scalar=float(LIST), in1=place_j[:, here],
                                                  op0=ALU.mult, op1=ALU.add))
                    dve.tensor_copy(addr[j][s][:, :], gden[:, :]).then_inc(addr_done, 1)
                    dve.wait_ge(addr_done, 2 * b + j + 1)
                assert n[0] == PLACE_STEPS

            def attn_output(t):
                dve.wait_ge(exp_done, HEADS * t + HEADS)
                dve.wait_ge(sink_e_done, t + 1)
                dve.wait_ge(den_done, 2 * t + 1)
                dve.tensor_tensor(den[:, :], rowsum[:, :], sink_e[:, :], ALU.add).then_inc(den_done, 1)
                dve.wait_ge(den_done, 2 * t + 2)
                dve.wait_ge(ao_done, t + 1)
                dve.reciprocal(rden[:, :], den[:, :]).then_inc(den_done, 1)
                dve.wait_ge(den_done, 2 * t + 3)
                dve.wait_ge(av_done, t + 2)
                if not isinstance(t, int) or t > 0:
                    dve.wait_ge(ao_turned, t)
                    dve.wait_ge(ssq_a_done, t)
                dve.tensor_tensor(attn_o[:, :].rearrange("p (h c) -> p h c", c=HD), ps_o[:, :].rearrange("p (h c) -> p h c", c=HD),
                                  rden[:, :].unsqueeze(2).to_broadcast([P, HEADS, HD]), ALU.mult).then_inc(ao_done, 1)

            def step(t, b1, b2, s):
                if b1 is not None:
                    attn_output(b1)
                if t is not None:
                    rope_q(t, s)
                if b1 is not None:
                    attn_split(b1)
                if t is not None:
                    softmax_max(t, s, range(0, 4))
                if b1 is not None:
                    residual(b1, 1 - s, 0, 0)
                if t is not None:
                    softmax_max(t, s, range(4, 8))
                    sink_diff(t)
                if b1 is not None:
                    residual(b1, 1 - s, 0, 1)
                    attn_rstd(b1)
                if b2 is not None:
                    route(b2)
                if b1 is not None:
                    residual(b1, 1 - s, 1, 0)
                    residual(b1, 1 - s, 1, 1)
                if b2 is not None:
                    place(b2, s)
                if b1 is not None:
                    ffn_norm(b1, 1 - s)

            run(dve, step, behind_first=split_w)


PLAN_STEPS = 35


def plan(nc, sem, iota_e, counts, expert1, expert2, place1, place2, slots, table, table_dram):
    with ExitStack() as ctx:
        def sb(name, shape, dt=F32):
            return ctx.enter_context(nc.sbuf_tensor(name, shape, dt))

        ones = sb("p_ones", [P, EXP])
        blocks_i = sb("blocks_i", [P, EXP], I32)
        blocks = sb("blocks", [P, EXP])
        block_end = sb("block_end", [P, EXP])
        count_end = sb("count_end", [P, EXP])
        start = sb("start", [P, EXP])
        n_col = sb("n_col", [P, 1])
        before_n = sb("before_n", [P, EXP])
        weighed = sb("weighed", [P, EXP])
        n_experts = sb("n_experts", [P, 1])
        n_blocks = sb("n_blocks", [P, 1])
        n_tokens = sb("n_tokens", [P, 1])
        offset = sb("offset", [P, 1])
        row = sb("row", [P, FIELDS])
        row_i = sb("row_i", [P, FIELDS], I32)
        n_less_1 = sb("n_less_1", [P, 1])
        n_experts_1 = sb("n_experts_1", [P, 1])
        pairs_i = sb("pairs_i", [P, 1], I32)
        hot = sb("p_hot", [P, NB, EXP])
        slot_f = sb("slot_f", [P, NB])

        set_up = sem("p_set_up")
        step = sem("p_step")
        table_out = sem("p_table_out")
        table_in = sem("p_table_in")
        block = ctx.enter_context(nc.Block())

        @block.gpsimd
        def _(pool):
            pool.memset(ones[:, :], 1.0).then_inc(set_up, 1)
            pool.iota(n_col[:, :], pattern=[[0, 1]], base=0, channel_multiplier=1,
                      allow_small_or_imprecise_dtypes=True).then_inc(set_up, 1)
            pool.iota(n_less_1[:, :], pattern=[[0, 1]], base=-1, channel_multiplier=1,
                      allow_small_or_imprecise_dtypes=True).then_inc(set_up, 1)

        @block.vector
        def _(dve):
            n = [0]

            def then(ins):
                n[0] += 1
                ins.then_inc(step, 1)
                dve.wait_ge(step, n[0])

            dve.wait_ge(set_up, 3)
            then(dve.tensor_scalar(blocks_i[:, :], counts[:, :], float(P - 1), None, ALU.add))
            then(dve.tensor_single_scalar(blocks_i[:, :], blocks_i[:, :], P.bit_length() - 1, ALU.arith_shift_right))
            then(dve.tensor_copy(blocks[:, :], blocks_i[:, :]))
            then(dve.tensor_tensor_scan(block_end[:, :], ones[:, :], blocks[:, :], 0.0, ALU.mult, ALU.add))
            then(dve.tensor_tensor_scan(count_end[:, :], ones[:, :], counts[:, :], 0.0, ALU.mult, ALU.add))
            then(dve.tensor_tensor(start[:, :], count_end[:, :], counts[:, :], ALU.subtract))
            then(dve.tensor_scalar(before_n[:, :], block_end[:, :], n_col[:, 0:1], None, ALU.is_le))
            then(dve.tensor_reduce(n_experts[:, :], before_n[:, :], AX.X, ALU.add))
            for total, each in ((n_blocks, blocks), (n_tokens, counts)):
                then(dve.tensor_tensor(weighed[:, :], before_n[:, :], each[:, :], ALU.mult))
                then(dve.tensor_reduce(total[:, :], weighed[:, :], AX.X, ALU.add))
            then(dve.tensor_tensor(offset[:, :], n_col[:, :], n_blocks[:, :], ALU.subtract))
            then(dve.tensor_scalar(offset[:, :], offset[:, :], float(P), None, ALU.mult))
            then(dve.tensor_scalar(row[:, 0:1], n_experts[:, :], float(EXP - 1), None, ALU.min))
            then(dve.tensor_scalar(before_n[:, :], block_end[:, :], n_less_1[:, 0:1], None, ALU.is_le))
            then(dve.tensor_reduce(n_experts_1[:, :], before_n[:, :], AX.X, ALU.add))
            then(dve.scalar_tensor_tensor(out=n_experts_1[:, :], in0=n_less_1[:, :], scalar=0.0, in1=n_experts_1[:, :],
                                          op0=ALU.min, op1=ALU.add))
            then(dve.tensor_scalar(row[:, 3:4], n_experts_1[:, :], row[:, 0:1], None, ALU.is_lt))
            then(dve.scalar_tensor_tensor(out=row[:, 1:2], in0=n_experts[:, :], scalar=float(LIST), in1=offset[:, :],
                                          op0=ALU.mult, op1=ALU.add))
            then(dve.tensor_tensor(row[:, 2:3], n_tokens[:, :], offset[:, :], ALU.add))
            then(dve.tensor_scalar(pairs_i[:, :], block_end[:, EXP - 1:EXP], -1.0, None, ALU.add))
            then(dve.tensor_single_scalar(pairs_i[:, :], pairs_i[:, :], 1, ALU.arith_shift_right))
            then(dve.tensor_copy(row_i[:, 0:4], row[:, 0:4]))
            then(dve.tensor_copy(row_i[:, 4:5], pairs_i[:, :]))
            assert n[0] == PLAN_STEPS - 10
            for expert_j, place_j, slot in ((expert1, place1, slots[0]), (expert2, place2, slots[1])):
                wide = [P, NB, EXP]
                then(dve.tensor_tensor(hot[:, :, :], iota_e[:, :].unsqueeze(1).to_broadcast(wide),
                                       expert_j[:, :].unsqueeze(2).to_broadcast(wide), ALU.is_equal))
                then(dve.tensor_tensor(hot[:, :, :], hot[:, :, :], start[:, :].unsqueeze(1).to_broadcast(wide), ALU.mult))
                then(dve.tensor_reduce(slot_f[:, :], hot[:, :, :], AX.X, ALU.add))
                then(dve.tensor_tensor(slot_f[:, :], slot_f[:, :], place_j[:, :], ALU.add))
                then(dve.tensor_copy(slot[:, :], slot_f[:, :]))
            assert n[0] == PLAN_STEPS

        @block.sync
        def _(sp):
            sp.wait_ge(step, PLAN_STEPS - 10)
            sp.dma_start(table_dram, row_i[0:MAXBLK, :]).then_inc(table_out, 16)
            sp.wait_ge(table_out, 16)
            sp.dma_start(table[:, :], table_dram.rearrange("(o n) c -> o (n c)", o=1)).then_inc(table_in, 16)
            sp.wait_ge(table_in, 16)


def experts(nc, sem, a, ident, table, list_dram, u_dram, y_dram):
    with ExitStack() as ctx:
        def sb(name, shape, dt=F32):
            return ctx.enter_context(nc.sbuf_tensor(name, shape, dt))

        KG, KDN = 4, 2
        CHUNK = KG * FE
        SLOTS = 6
        D0, D1, U0, U1, G0, G1 = range(SLOTS)
        raw = [sb(f"raw{s}", [P, CHUNK]) for s in range(SLOTS)]
        w_hi = [sb(f"e_hi{s}", [P, CHUNK], F32R) for s in range(SLOTS)]
        w_lo = [sb(f"e_lo{s}", [P, CHUNK], F32R) for s in range(SLOTS)]
        ix = [sb(f"ix{s}", [P, 1], I32) for s in range(RING)]
        x = [sb(f"ex{s}", [P, D]) for s in range(RING)]
        x_hi = [sb(f"ex_hi{s}", [P, KD, P], F32R) for s in range(RING)]
        x_lo = [sb(f"ex_lo{s}", [P, KD, P], F32R) for s in range(RING)]
        silu = sb("silu", [P, FE])
        hid = sb("hid", [P, FE])
        h_hi = sb("hid_hi", [P, FT, P], F32R)
        h_lo = sb("hid_lo", [P, FT, P], F32R)
        y = sb("y_sb", [P, D])
        ps_g = ctx.enter_context(nc.psum_tensor("ps_g", [P, FE], F32))
        ps_u = ctx.enter_context(nc.psum_tensor("ps_u", [P, FE], F32))
        ps_y = ctx.enter_context(nc.psum_tensor("ps_ey", [P, 2, BANK], F32))
        ps_x = ctx.enter_context(nc.psum_tensor("ps_ex", [P, 2, BANK], F32))
        ps_h = ctx.enter_context(nc.psum_tensor("ps_eh", [P, FE], F32))

        waited = sem("e_waited")
        waited_sp = sem("e_waited_sp")
        arrived = [sem(f"e_arrived{s}") for s in range(SLOTS)]
        ix_in = [sem(f"e_ix_in{s}") for s in range(RING)]
        x_in = [sem(f"e_x_in{s}") for s in range(RING)]
        hi_done = sem("e_hi_done")
        lo_done = sem("e_lo_done")
        used = sem("e_used")
        x_turned = sem("e_x_turned")
        x_hi_done = sem("e_x_hi_done")
        x_lo_done = sem("e_x_lo_done")
        silu_done = sem("e_silu_done")
        hid_done = sem("e_hid_done")
        hid_turned = sem("e_hid_turned")
        h_hi_done = sem("e_h_hi_done")
        h_lo_done = sem("e_h_lo_done")
        y_out = sem("e_y_out")
        y_stored = sem("e_y_stored")

        block = ctx.enter_context(nc.Block())

        def field(eng, n, c, top):
            at = FIELDS * n + c
            where = slice(at, at + 1) if isinstance(n, int) else bass.ds(at, 1)
            return eng.value_load(table[0:1, where], min_val=0, max_val=top)

        def is_new(eng, m):
            return field(eng, m, 3, 1)

        def more_pairs(eng):
            return eng.value_load(table[0:1, 4:5], min_val=0, max_val=MAXPAIRS - 1)

        def chunk_of(n, s):
            return SLOTS * n + SLOTS + s

        def up_used(n):
            return SLOTS + SLOTS * n + 4

        def gate_used(n):
            return SLOTS + (2 if isinstance(n, int) and n == 0 else SLOTS * n)

        def down_used(n):
            return SLOTS + SLOTS * n + 8

        @block.sync
        def _(sp):
            def load(weights, k, e, c, s):
                src = weights[bass.ds(e, 1), :, :].rearrange("o (c p k) f -> c p (o k f)", p=P, k=k)[c]
                sp.dma_start(raw[s][:, :], src).then_inc(arrived[s], 16)

            def lists(m, s):
                at = field(sp, m, 1, EXP * LIST + 2 * P)
                sp.dma_start(ix[s][:, :], list_dram[bass.ds(at, P), :]).then_inc(ix_in[s], 16)

            def expert(n):
                return field(sp, n, 0, EXP - 1)

            for m in range(2):
                lists(m, m)
            e0, e1 = expert(0), expert(1)
            for weights, e, s0 in ((a["w_gate"], e0, D0), (a["w_up"], e0, U0), (a["w_gate"], e1, G0)):
                for c in range(2):
                    load(weights, KG, e, c, s0 + c)

            def step(n, s):
                sp.wait_ge(x_in[s], 8 * (n - s) + 16)
                lists(n + 2, s)
                for weights, k, m, s0 in ((a["w_down"], KDN, n, D0), (a["w_up"], KG, n + 1, U0), (a["w_gate"], KG, n + 2, G0)):
                    e, new = expert(m), is_new(sp, m)
                    for c in range(2):
                        sp.wait_ge(lo_done, chunk_of(n, s0 + c) + 1)
                        sp.sem_inc(waited_sp, 1)
                        with sp.If(new > 0):
                            load(weights, k, e, c, s0 + c)
                        with sp.If(new < 1):
                            sp.sem_inc(arrived[s0 + c], 16)

            more = more_pairs(sp)
            with sp.Fori(0, more + 1) as i:
                step(2 * i, 0)
                step(2 * i + 1, 1)
            last = 2 * more + 2
            for s in range(SLOTS):
                sp.wait_ge(arrived[s], 16 * last + 16)
            for s in range(RING):
                sp.wait_ge(x_in[s], 8 * last + 16)
            sp.sem_inc(waited_sp, 1)

        @block.gpsimd
        def _(pool):
            def gather(m, s):
                pool.wait_ge(ix_in[s], 8 * (m - s) + 16)
                if not isinstance(m, int) or m >= 2:
                    pool.wait_ge(x_turned, m - 1)
                pool.sem_inc(waited, 1)
                pool.indirect_dma_start(x[s][:, :], None, u_dram, bass.IndirectOffsetOnAxis(ap=ix[s][:, 0:1], axis=0)
                                        ).then_inc(x_in[s], 16)

            def store(n):
                at = field(pool, n, 2, 2 * REAL)
                pool.wait_ge(y_out, n + 2)
                pool.wait_ge(y_stored, 16 * n) if not isinstance(n, int) or n > 0 else None
                pool.sem_inc(waited, 1)
                pool.dma_start(y_dram[bass.ds(at, P), :], y[:, :]).then_inc(y_stored, 16)

            for m in range(3):
                gather(m, m % 2)
            gather(3, 1)
            store(0)
            more = more_pairs(pool)
            with pool.Fori(0, more) as i:
                gather(2 * i + 4, 0)
                store(2 * i + 1)
                gather(2 * i + 5, 1)
                store(2 * i + 2)
            store(2 * more + 1)
            pool.wait_ge(y_stored, 32 * more + 32)
            pool.sem_inc(waited, 1)

        @block.tensor
        def _(pe):
            def turn_x(m, s):
                pe.wait_ge(x_in[s], 8 * (m - s) + 16)
                pe.wait_ge(x_lo_done, m + 1)
                for c in range(2):
                    for k in range(KG):
                        mm = pe.transpose(ps_x[:, c, k * P:(k + 1) * P], x[s][:, c * FE + k:(c + 1) * FE:KG], ident[:, :])
                mm.then_inc(x_turned, 1)

            def half_product(ps, s, c, idx, slot):
                pe.wait_ge(lo_done, idx + 1 + SLOTS)
                for k in range(KG):
                    for n, (xs, w) in enumerate(((x_hi, w_hi), (x_hi, w_lo), (x_lo, w_hi))):
                        mm = pe.matmul(ps[:, :], xs[s][:, c * KG + k, :], w[slot][:, k * FE:(k + 1) * FE],
                                       start=(c == 0 and k == 0 and n == 0), stop=(c == 1 and k == KG - 1 and n == 2))
                mm.then_inc(used, 1)

            def up(n, s):
                pe.wait_ge(hid_done, n + 1)
                for c in range(2):
                    half_product(ps_u, s, c, SLOTS * n + 2 + c, U0 + c)

            def gate(m, s, c, idx, slot):
                if c == 0:
                    pe.wait_ge(x_lo_done, m + 2)
                    pe.wait_ge(silu_done, m + 1)
                half_product(ps_g, s, c, idx, slot)

            def down(n):
                pe.wait_ge(h_lo_done, n + 2)
                pe.wait_ge(y_out, n + 1)
                for c in range(2):
                    pe.wait_ge(lo_done, chunk_of(n, D0 + c) + 1 + SLOTS)
                    for k in range(KDN):
                        for i in range(2):
                            for j, (h, w) in enumerate(((h_hi, w_hi), (h_hi, w_lo), (h_lo, w_hi))):
                                mm = pe.matmul(ps_y[:, i, :], h[:, c * KDN + k, :], w[D0 + c][:, k * D + i * BANK:k * D + (i + 1) * BANK],
                                               start=(c == 0 and k == 0 and j == 0), stop=(c == 1 and k == KDN - 1 and j == 2))
                    mm.then_inc(used, 1)

            def step(n, s):
                turn_x(n + 1, 1 - s)
                up(n, s)
                gate(n + 1, 1 - s, 0, SLOTS * n + 4, G0)
                pe.wait_ge(hid_done, n + 2)
                pe.wait_ge(h_lo_done, n + 1)
                for c in range(2):
                    for k in range(KDN):
                        mm = pe.transpose(ps_h[:, (c * KDN + k) * P:(c * KDN + k + 1) * P],
                                          hid[:, c * 2 * P + k:(c + 1) * 2 * P:KDN], ident[:, :])
                mm.then_inc(hid_turned, 1)
                gate(n + 1, 1 - s, 1, SLOTS * n + 5, G1)
                down(n)

            turn_x(0, 0)
            for c in range(2):
                gate(0, 0, c, c, D0 + c)
            with pe.Fori(0, more_pairs(pe) + 1) as i:
                step(2 * i, 0)
                step(2 * i + 1, 1)

        def square_x(t):
            return t[:, :, :].rearrange("p b (k c) -> p (b k) c", c=P)

        @block.scalar
        def _(act):
            act.sem_inc(used, SLOTS)

            def split(idx, s, round_):
                act.wait_ge(arrived[s], 16 * round_ + 16)
                act.wait_ge(used, idx + 1)
                act.activation(w_hi[s][:, :], raw[s][:, :], ACT.Copy).then_inc(hi_done, 1)

            def split_new(n, m, slots_):
                new = is_new(act, m)
                with act.If(new > 0):
                    for s_ in slots_:
                        split(chunk_of(n, s_), s_, n + 1)
                with act.If(new < 1):
                    for s_ in slots_:
                        act.wait_ge(arrived[s_], 16 * n + 32)
                        act.wait_ge(hi_done, chunk_of(n, s_))
                        act.sem_inc(hi_done, 1)

            def x_split(m, s):
                act.wait_ge(x_turned, m + 1)
                act.activation(x_hi[s][:, :, :], square_x(ps_x), ACT.Copy).then_inc(x_hi_done, 1)

            def y_from_psum(n):
                act.wait_ge(used, down_used(n))
                act.wait_ge(y_stored, 16 * n) if not isinstance(n, int) or n > 0 else None
                act.activation(y[:, :], ps_y[:, :, :].rearrange("p b c -> p (b c)"), ACT.Copy).then_inc(y_out, 1)

            def step(n, s, before):
                act.wait_ge(used, gate_used(n))
                act.wait_ge(hid_done, n + 1)
                act.activation(silu[:, :], ps_g[:, :], ACT.Silu).then_inc(silu_done, 1)
                x_split(n + 1, 1 - s)
                if before is not None:
                    y_from_psum(before)
                split_new(n, n, (D0, D1))
                split_new(n, n + 1, (U0,))
                act.wait_ge(hid_turned, n + 1)
                act.activation(h_hi[:, :, :], ps_h[:, :].rearrange("p (k c) -> p k c", c=P), ACT.Copy).then_inc(h_hi_done, 1)
                split_new(n, n + 1, (U1,))
                split_new(n, n + 2, (G0, G1))

            for s in range(SLOTS):
                split(s, s, 0)
                if s == 0:
                    x_split(0, 0)
            act.sem_inc(y_out, 1)
            act.sem_inc(silu_done, 1)
            step(0, 0, None)
            step(1, 1, 0)
            more = more_pairs(act)
            with act.Fori(0, more) as i:
                step(2 * i + 2, 0, 2 * i + 1)
                step(2 * i + 3, 1, 2 * i + 2)
            y_from_psum(2 * more + 1)

        @block.vector
        def _(dve):
            dve.sem_inc(lo_done, SLOTS)
            dve.sem_inc(x_lo_done, 1)
            dve.sem_inc(h_lo_done, 1)
            dve.sem_inc(hid_done, 1)

            def split(idx, s):
                dve.wait_ge(hi_done, idx + 1)
                dve.tensor_tensor(w_lo[s][:, :], raw[s][:, :], w_hi[s][:, :].bitcast(F32), ALU.subtract).then_inc(lo_done, 1)

            def split_new(n, m, slots_):
                new = is_new(dve, m)
                with dve.If(new > 0):
                    for s_ in slots_:
                        split(chunk_of(n, s_), s_)
                with dve.If(new < 1):
                    for s_ in slots_:
                        dve.wait_ge(hi_done, chunk_of(n, s_) + 1)
                        dve.wait_ge(lo_done, chunk_of(n, s_) + SLOTS)
                        dve.sem_inc(lo_done, 1)

            def x_split(m, s):
                dve.wait_ge(x_hi_done, m + 1)
                dve.tensor_tensor(x_lo[s][:, :, :], square_x(ps_x), x_hi[s][:, :, :].bitcast(F32), ALU.subtract).then_inc(x_lo_done, 1)

            def step(n, s):
                x_split(n + 1, 1 - s)
                split_new(n, n, (D0,))
                dve.wait_ge(used, up_used(n))
                dve.wait_ge(silu_done, n + 2)
                dve.wait_ge(hid_turned, n) if not isinstance(n, int) or n > 0 else None
                dve.tensor_tensor(hid[:, :], ps_u[:, :], silu[:, :], ALU.mult).then_inc(hid_done, 1)
                split_new(n, n, (D1,))
                dve.wait_ge(h_hi_done, n + 1)
                dve.tensor_tensor(h_lo[:, :, :], ps_h[:, :].rearrange("p (k c) -> p k c", c=P), h_hi[:, :, :].bitcast(F32),
                                  ALU.subtract).then_inc(h_lo_done, 1)
                split_new(n, n + 1, (U0, U1))
                split_new(n, n + 2, (G0, G1))

            for s in range(SLOTS):
                split(s, s)
                if s == 0:
                    x_split(0, 0)
            step(0, 0)
            step(1, 1)
            with dve.Fori(0, more_pairs(dve)) as i:
                step(2 * i + 2, 0)
                step(2 * i + 3, 1)


def combine(nc, sem, a, eps_t, gate1, gate2, slots, h2_dram, y_dram, out):
    with ExitStack() as ctx:
        def sb(name, shape, dt=F32):
            return ctx.enter_context(nc.sbuf_tensor(name, shape, dt))

        DEPTH = 5
        g_final = sb("g_final", [P, D])
        z = [sb(f"z{s}", [P, D]) for s in range(DEPTH)]
        y = [[sb(f"cy{j}{s}", [P, D]) for s in range(DEPTH)] for j in range(2)]
        square = sb("c_square", [P, D])
        ssq = sb("c_ssq", [P, NB])
        rms = sb("c_rms", [P, NB])
        rstd = sb("c_rstd", [P, NB])
        g_in = sem("c_g_in")
        z_in = [sem(f"c_z_in{s}") for s in range(DEPTH)]
        y_in = [sem(f"c_y_in{s}") for s in range(DEPTH)]
        added = sem("c_added")
        squared = sem("c_squared")
        rms_done = sem("c_rms_done")
        rstd_done = sem("c_rstd_done")
        normed = sem("c_normed")
        stored = [sem(f"c_stored{s}") for s in range(DEPTH)]
        block = ctx.enter_context(nc.Block())

        @block.sync
        def _(sp):
            sp.dma_start(g_final[:, :], a["ln_final_g"][0].partition_broadcast(P)).then_inc(g_in, 16)
            for b in range(NB + DEPTH):
                s = b % DEPTH
                if b >= DEPTH:
                    sp.wait_ge(normed, b - DEPTH + 1)
                    sp.dma_start(out[(b - DEPTH) * P:(b - DEPTH + 1) * P, :], z[s][:, :]).then_inc(stored[s], 16)
                if b < NB:
                    if b >= DEPTH:
                        sp.wait_ge(stored[s], 16 * (b // DEPTH))
                    sp.dma_start(z[s][:, :], h2_dram[b * P:(b + 1) * P, :]).then_inc(z_in[s], 16)
            for s in range(DEPTH):
                sp.wait_ge(stored[s], 16 * (NB // DEPTH))

        @block.gpsimd
        def _(pool):
            for b in range(NB):
                s = b % DEPTH
                if b >= DEPTH:
                    pool.wait_ge(added, 2 * (b - DEPTH) + 2)
                for j in range(2):
                    pool.indirect_dma_start(y[j][s][:, :], None, y_dram,
                                            bass.IndirectOffsetOnAxis(ap=slots[j][:, b:b + 1], axis=0)).then_inc(y_in[s], 16)

        @block.scalar
        def _(act):
            for b in range(NB):
                act.wait_ge(added, 2 * b + 2)
                act.wait_ge(squared, b) if b else None
                act.activation(square[:, :], z[b % DEPTH][:, :], ACT.Square, accum_out=ssq[:, b:b + 1]).then_inc(squared, 1)
                act.wait_ge(squared, b + 1)
                act.activation(rms[:, b:b + 1], ssq[:, b:b + 1], ACT.Sqrt, bias=eps_t[:, :], scale=1.0 / D).then_inc(rms_done, 1)

        @block.vector
        def _(dve):
            def norm(b):
                dve.wait_ge(rms_done, b + 1)
                dve.reciprocal(rstd[:, b:b + 1], rms[:, b:b + 1]).then_inc(rstd_done, 1)
                dve.wait_ge(rstd_done, b + 1)
                zs = z[b % DEPTH]
                dve.scalar_tensor_tensor(out=zs[:, :], in0=zs[:, :], scalar=rstd[:, b:b + 1], in1=g_final[:, :],
                                         op0=ALU.mult, op1=ALU.mult).then_inc(normed, 1)

            dve.wait_ge(g_in, 16)
            for b in range(NB):
                s = b % DEPTH
                dve.wait_ge(z_in[s], 16 * (b // DEPTH + 1))
                dve.wait_ge(y_in[s], 32 * (b // DEPTH + 1))
                for j, gate in enumerate((gate1, gate2)):
                    dve.scalar_tensor_tensor(out=z[s][:, :], in0=y[j][s][:, :], scalar=gate[:, b:b + 1], in1=z[s][:, :],
                                             op0=ALU.mult, op1=ALU.add).then_inc(added, 1)
                    dve.wait_ge(added, 2 * b + j + 1)
                if b:
                    norm(b - 1)
            norm(NB - 1)


def layouts(i):
    f = np.float32

    def feature_tiles(w):
        w = w.reshape(KD, P, -1)
        q = [np.r_[h * HD:(h + 1) * HD, (h + 4) * HD:(h + 5) * HD] for h in range(4)]
        k, v, *rec = (np.arange(c, c + P) for c in range(ATTN, w.shape[2], P))
        cols = [*rec, *q, k, v]
        return np.stack([w[:, :, c].transpose(1, 0, 2) for c in cols])

    def per_feature(v):
        return v.reshape(FT, P).T

    gates = np.zeros((FT, P, 4, P), f)
    for g, name in enumerate(("w_rgate_fwd", "w_igate_fwd", "w_rgate_bwd", "w_igate_bwd")):
        for ft in range(FT):
            gates[ft, 0:HD, g, 0:HD] = i[name][0, 2 * ft]
            gates[ft, HD:P, g, HD:P] = i[name][0, 2 * ft + 1]
    vecs = [i["conv_w"][0, j] for j in range(4)] + [i["conv_b"][0]]
    vecs += [i[n][0] for n in ("b_rgate_fwd", "b_igate_fwd", "b_rgate_bwd", "b_igate_bwd", "lam_fwd", "lam_bwd")]
    router = np.zeros((D, ROUT), f)
    router[:, 0:4] = i["w_router_grp"][0]
    router[:, 8:ROUT] = i["w_router_exp"][0]
    rbias = np.full(ROUT, NEG, f)
    rbias[0:4] = i["b_router_grp"][0]
    rbias[8:ROUT] = i["b_router_exp"][0]
    pos = np.r_[np.arange(META + SEQS[0]), META + np.arange(SEQS[1])].astype(f)
    inv = f(500000.0) ** (-np.arange(0, 16, 2, dtype=f) / f(16))
    ang = pos[:, None] * inv[None, :]
    cos, sin = np.ones((P, COLS), f), np.zeros((P, COLS), f)
    swap = np.zeros((P, P), f)
    for h in (0, HD):
        for j in range(8):
            cos[h + j] = cos[h + 8 + j] = np.cos(ang[:, j])
            sin[h + j] = -np.sin(ang[:, j])
            sin[h + 8 + j] = np.sin(ang[:, j])
            swap[h + 8 + j, h + j] = swap[h + j, h + 8 + j] = 1.0
    masks = np.zeros((NB, P, KEYS), f)
    qi, kj = np.arange(P)[:, None], np.arange(P)[None, :]
    last = (SEQS[0] // P - 1, NB - 1)
    first = (0, SEQS[0] // P)
    for b in range(NB):
        masks[b, :, 0:P] = NEG if b in first else np.where(kj >= qi, 0.0, NEG)
        masks[b, :, 2 * P:3 * P] = NEG if b in last else np.where(kj <= qi, 0.0, NEG)
    before = (np.arange(P)[:, None] < np.arange(P)[None, :]).astype(f)
    return {
        "x": np.concatenate([i["x_prompt"][0], i["x_sample"][0]]),
        "meta": i["meta_tokens"],
        "ln_mix_g": i["ln_mix_g"],
        "w_in": feature_tiles(i["w_in"][0]),
        "gates": gates,
        "vecs": np.stack([per_feature(v) for v in vecs], axis=2),
        "sink": i["attn_sink"],
        "g_out": np.stack([i["g_attn_out"][0].reshape(FT, P), i["g_rec_out"][0].reshape(FT, P)]).reshape(KD, P).T.copy(),
        "w_out": i["w_out"][0].reshape(KD, P, D).transpose(1, 0, 2),
        "ln_ffn_g": i["ln_ffn_g"],
        "router": router.reshape(KD, P, ROUT).transpose(1, 0, 2),
        "rbias": rbias[None],
        "w_gate": i["w_exp_gate"][0],
        "w_up": i["w_exp_up"][0],
        "w_down": i["w_exp_down"][0],
        "ln_final_g": i["ln_final_g"][None],
        "ident": np.eye(P, dtype=f),
        "swap": swap,
        "before": before,
        "cos": cos,
        "sin": sin,
        "masks": masks,
    }


def kernel(**inputs):
    import concourse.bacc as bacc
    from concourse.bass_utils import run_bass_kernel_spmd as run

    arrays = {n: np.ascontiguousarray(v) for n, v in layouts({n: np.asarray(v) for n, v in inputs.items()}).items()}
    nc = bacc.Bacc("TRN2", target_bir_lowering=False, num_devices=1)
    a = {n: nc.dram_tensor(f"in_{n}", v.shape, mybir.dt.from_np(v.dtype), kind="ExternalInput").ap()
         for n, v in arrays.items()}
    out = nc.dram_tensor("out", (REAL, D), F32, kind="ExternalOutput").ap()
    encoder(nc, a, out)
    got = run(nc, [{f"in_{n}": v for n, v in arrays.items()}], core_ids=[0]).results[0]["out"]
    return got[0:SEQS[0]][None], got[SEQS[0]:REAL][None]
```

```python
from contextlib import ExitStack, contextmanager

import numpy as np

import concourse.bass as bass
from concourse import mybir

F32 = mybir.dt.float32
F32R = mybir.dt.float32r
I32 = mybir.dt.int32
U32 = mybir.dt.uint32
ALU = mybir.AluOpType
ACT = mybir.ActivationFunctionType
AX = mybir.AxisListType

P = 128
D = 1024
META = 16
SEQS = (1024, 256)
REAL = sum(SEQS)
NB = REAL // P
COLS = META + REAL
KD = D // P
HEADS = 8
HD = 64
ATTN = HEADS * HD
REC = 512
FT = REC // P
FTILES = 14
NCH = 3
CH = COLS // NCH
BANK = 512
EXP = 32
FE = 512
EPS = 1e-6
NEG = -1e30
RING = 2
WIN = 3 * P
KEYS = WIN + META
T0 = META + SEQS[0]
T1 = META + SEQS[1]
XRW = 2 + T0 + 1 + 2 + T1 + 1
RW = XRW - 3
OFF1 = T0 + 3
LIST = 1280
MAXBLK = 64
FIELDS = 6
MAXPAIRS = (2 * REAL // P + EXP) // 2
YROWS = 2 * REAL + P
ROUT = 40
DEPTH = 5


def done(t):
    return t + 1 + RING


def free(t):
    return t + 1


@contextmanager
def semaphores(nc):
    with ExitStack() as ctx:
        made = []

        def sem(name):
            made.append(ctx.enter_context(nc.semaphore(name)))
            return made[-1]

        yield sem
        with nc.Block() as block:
            @block.sync
            def _(sp):
                for one in made:
                    sp.sem_clear(one)


def encoder(nc, a, out):
    top = ExitStack()
    with top:
        def sem(name):
            return top.enter_context(nc.semaphore(name))

        def dram(name, shape, dt):
            return nc.dram_tensor(name, shape, dt, kind="Internal").ap()

        h2_dram = dram("h2_dram", [REAL, D], F32)
        u_dram = dram("u_dram", [REAL, D], F32)
        k_dram = dram("k_dram", [P, 2, 2, META + P + REAL + P], F32R)
        y_dram = dram("y_dram", [YROWS, D], F32)
        list_dram = dram("list_dram", [(EXP + 1) * LIST, 1], I32)
        table_dram = dram("table_dram", [MAXBLK, FIELDS], I32)

        def keep(name, shape, dt=F32):
            return top.enter_context(nc.sbuf_tensor(name, shape, dt))

        gate1 = keep("gate1", [P, NB])
        gate2 = keep("gate2", [P, NB])
        expert1 = keep("expert1", [P, NB])
        expert2 = keep("expert2", [P, NB])
        place1 = keep("place1", [P, NB])
        place2 = keep("place2", [P, NB])
        counts = keep("counts", [P, EXP])
        iota_e = keep("iota_e", [P, EXP])
        ident = keep("ident", [P, P])
        eps_t = keep("eps_t", [P, 1])

        with ExitStack() as mixer:
            def mk(name, shape, dt=F32):
                return mixer.enter_context(nc.sbuf_tensor(name, shape, dt))

            feat = mk("feat", [P, 2 * FT, COLS])
            k_pre = mk("k_pre", [P, COLS])
            v_pre = mk("v_pre", [P, COLS])
            with semaphores(nc) as own:
                project(nc, own, a, feat, k_pre, v_pre, ident, eps_t, iota_e, list_dram, y_dram)
            yg, q_pre = feat[:, 0:FT, :], feat[:, FT:2 * FT, :]
            rstd_rec = mk("rstd_rec", [P, NB])
            v_tok = mk("v_tok", [P, (NB + 2) * P])
            v_meta = mk("v_meta", [P, ATTN])
            wo_hi = mk("wo_hi", [P, KD, D], F32R)
            wo_lo = mk("wo_lo", [P, KD, D], F32R)
            keys(nc, sem, a, k_pre, v_pre, yg, k_dram, v_tok, v_meta, wo_hi, wo_lo, rstd_rec, ident, eps_t)
            rec = yg[:, :, META:COLS]
            mix(nc, sem, a, (k_pre, v_pre), q_pre, rec, rstd_rec, wo_hi, wo_lo, k_dram, v_tok, v_meta, ident, eps_t, iota_e,
                gate1, gate2, expert1, expert2, place1, place2, counts, h2_dram, u_dram, list_dram)
        slots = [top.enter_context(nc.sbuf_tensor(f"slot{j}", [P, NB], I32)) for j in range(2)]
        start = keep("start", [P, EXP])
        table = top.enter_context(nc.sbuf_tensor("table", [1, MAXBLK * FIELDS], I32))
        plan(nc, sem, counts, start, table, table_dram)
        z = [keep(f"z{s}", [P, D]) for s in range(DEPTH)]
        g_final = keep("g_final", [P, D])
        z_in = [sem(f"z_in{s}") for s in range(DEPTH)]
        g_in = sem("g_in")
        experts(nc, sem, a, ident, iota_e, start, expert1, expert2, place1, place2, slots, table, list_dram,
                u_dram, h2_dram, y_dram, g_final, z, g_in, z_in)
        combine(nc, sem, eps_t, gate1, gate2, slots, h2_dram, y_dram, out, g_final, z, g_in, z_in)


def project(nc, sem, a, feat, k_pre, v_pre, ident, eps_t, iota_e, list_dram, y_dram):
    with ExitStack() as ctx:
        def sb(name, shape, dt=F32):
            return ctx.enter_context(nc.sbuf_tensor(name, shape, dt))

        XT = FT
        xr = sb("xr", [P, FT, XRW])
        h_hi = sb("h_hi", [P, KD, COLS], F32R)
        h_lo = sb("h_lo", [P, KD, COLS], F32R)
        w_raw = [sb(f"w_raw{s}", [P, KD, P]) for s in range(RING)]
        w_hi = [sb(f"w_hi{s}", [P, KD, P], F32R) for s in range(RING)]
        w_lo = [sb(f"w_lo{s}", [P, KD, P], F32R) for s in range(RING)]
        r_g = sb("r_g", [P, RW])
        i_g = sb("i_g", [P, RW])
        t_g = sb("t_g", [P, RW])
        a_g = sb("a_g", [P, RW])
        h_g = sb("h_g", [P, RW])
        xn = [r_g[:, 0:D], i_g[:, 0:D]]
        x_in = [t_g[:, 0:D], h_g[:, 0:D]]
        zeros = a_g[:, 0:D]
        conv = h_g[:, :]
        g_bc = k_pre[:, 0:D]
        vecs = sb("vecs", [P, FT, 11])
        gates = sb("gates", [P, 4, P])
        small = sb("lam_small", [P, 7, FT, 2])
        decay, ndecay, sp_e, sp_z, sp_z2, sp_p, lam_pos = (small[:, j, :, :] for j in range(7))
        ssq = [sb(f"ssq{s}", [P, 1]) for s in range(RING)]
        rms = [sb(f"rms{s}", [P, 1]) for s in range(RING)]
        rstd = [sb(f"rstd{s}", [P, 1]) for s in range(RING)]
        ps = ctx.enter_context(nc.psum_tensor("pj", [P, 8, BANK], F32))
        tr = [ps[:, 0:2, :], ps[:, 2:4, :]]
        ps_r, ps_i = ps[:, 2:5, :], ps[:, 5:8, :]
        flat_r = ps_r.rearrange("p b c -> p (b c)")
        flat_i = ps_i.rearrange("p b c -> p (b c)")

        consts_in = sem("consts_in")
        vecs_in = sem("vecs_in")
        gates_in = sem("gates_in")
        x_arrived = [sem(f"x_arrived{s}") for s in range(RING)]
        w_arrived = [sem(f"w_arrived{s}") for s in range(RING)]
        fills = sem("fills")
        fill_dma = sem("fill_dma")
        eps_set = sem("eps_set")
        squared = sem("squared")
        rms_done = sem("rms_done")
        rstd_done = sem("rstd_done")
        xn_done = sem("xn_done")
        x_turned = sem("x_turned")
        h_hi_done = sem("h_hi_done")
        h_lo_done = sem("h_lo_done")
        w_hi_done = sem("w_hi_done")
        w_lo_done = sem("w_lo_done")
        proj_done = sem("proj_done")
        proj_out = sem("proj_out")
        xr_cleared = sem("xr_cleared")
        lam_e = sem("lam_e")
        lam_step = sem("lam_step")
        conv_step = sem("conv_step")
        conv_done = sem("conv_done")
        gates_done = sem("gates_done")
        r_done = sem("r_done")
        i_done = sem("i_done")
        ta_done = sem("ta_done")
        v_done = sem("v_done")
        s_done = sem("s_done")
        a_cut = sem("a_cut")
        ix_done = sem("ix_done")
        u_done = sem("scan_u_done")
        scanned = sem("scanned")
        summed = sem("summed")
        gelu_done = sem("gelu_done")
        rec_done = sem("rec_done")

        block = ctx.enter_context(nc.Block())

        def rows(t):
            return META if isinstance(t, int) and t == 0 else P

        def col(t):
            return 0 if isinstance(t, int) and t == 0 else META - P + t * P

        LAST_ROWS = [-(-((c + 1) * CH - META) // P) for c in range(NCH)]
        FIRST_BANKS = ((4, 5), (6, 7), (0, 1))

        def one(tensor, j, lo, hi):
            return tensor[:, bass.ds(j, 1), lo:hi].rearrange("p o c -> p (o c)")

        def vec(ft, j):
            return one(vecs, ft, j, j + 1)

        @block.sync
        def _(sp):
            sp.dma_start(ident[:, :], a["ident"]).then_inc(consts_in, 16)
            sp.dma_start(g_bc, a["ln_mix_g"][0].partition_broadcast(P)).then_inc(consts_in, 16)

            def load_x(t, s):
                sp.wait_ge(xn_done, free(t))
                src = a["meta"] if isinstance(t, int) and t == 0 else a["x"][bass.ds(t * P - P, P), :]
                sp.dma_start(x_in[s][0:rows(t), :], src).then_inc(x_arrived[s], 16)

            load_x(0, 0)
            load_x(1, 1)
            for f in range(2):
                sp.dma_start(w_raw[f][:, :, :], a["w_in"][f]).then_inc(w_arrived[f], 16)
            sp.dma_start(vecs[:, :, :], a["vecs"]).then_inc(vecs_in, 16)
            sp.wait_ge(fills, 2)
            sp.dma_start(list_dram.rearrange("(p c) o -> p (c o)", p=P),
                         zeros[:, 0:(EXP + 1) * LIST // P].bitcast(I32)).then_inc(fill_dma, 16)
            sp.dma_start(y_dram[2 * REAL:YROWS, :], zeros).then_inc(fill_dma, 16)
            with sp.Fori(0, 4) as i:
                load_x(2 * i + 2, 0)
                load_x(2 * i + 3, 1)
            load_x(NB, 0)

            def load_w(f, s):
                sp.wait_ge(w_lo_done, free(f))
                sp.dma_start(w_raw[s][:, :, :], a["w_in"][bass.ds(f, 1), :, :, :].rearrange("o p k c -> p (o k) c")
                             ).then_inc(w_arrived[s], 16)

            with sp.Fori(0, XT // 2) as i:
                load_w(2 * i + 2, 0)
                load_w(2 * i + 3, 1)
            with sp.Fori(0, FT) as k:
                sp.wait_ge(gates_done, 4 * k + 1)
                sp.dma_start(gates[:, :, :], a["gates"][bass.ds(k, 1), :, :, :].rearrange("o p g c -> p (o g) c")
                             ).then_inc(gates_in, 16)
                load_w(2 * k + 6, 0)
                load_w(2 * k + 7, 1)

        @block.gpsimd
        def _(pool):
            pool.memset(zeros, 0.0).then_inc(fills, 1)
            pool.iota(iota_e[:, :], pattern=[[1, EXP]], base=0, channel_multiplier=0,
                      allow_small_or_imprecise_dtypes=True).then_inc(fills, 1)
            pool.memset(xr[:, :, :], 0.0).then_inc(xr_cleared, 1)

        @block.scalar
        def _(act):
            act.sem_inc(h_hi_done, RING)
            act.sem_inc(w_hi_done, RING)
            act.sem_inc(proj_out, 2)
            act.sem_inc(r_done, 1)
            act.sem_inc(i_done, 1)
            act.sem_inc(s_done, 1)

            def norm(t, s, round_):
                n = rows(t)
                act.wait_ge(x_arrived[s], 16 * (round_ + 1))
                act.wait_ge(x_turned, free(t))
                act.activation(xn[s][0:n, :], x_in[s][0:n, :], ACT.Square, accum_out=ssq[s][0:n, :]).then_inc(squared, 1)
                act.wait_ge(squared, t + 1)
                act.activation(rms[s][0:n, :], ssq[s][0:n, :], ACT.Sqrt, bias=eps_t[0:n, :], scale=1.0 / D).then_inc(rms_done, 1)

            def hi(t, s):
                n = rows(t)
                act.wait_ge(x_turned, done(t))
                act.activation(h_hi[:, :, bass.ds(col(t), n)],
                               tr[s].rearrange("p b (k c) -> p (b k) c", c=P)[:, :, 0:n], ACT.Copy).then_inc(h_hi_done, 1)

            def split_w(f, s, round_):
                act.wait_ge(w_arrived[s], 16 * (round_ + 1))
                if isinstance(f, int) and f == 2:
                    act.wait_ge(proj_done, 2 * NCH + 2 * NCH - 1)
                else:
                    act.wait_ge(proj_done, NCH * f + NCH)
                act.activation(w_hi[s][:, :, :], w_raw[s][:, :, :], ACT.Copy).then_inc(w_hi_done, 1)

            def evacuate(f, s, c, put):
                act.wait_ge(proj_done, NCH * f + c + 1 + 2 * NCH)
                put(ps[:, (NCH * s + c) % 2, :], c).then_inc(proj_out, 1)

            def put_flat(dst):
                return lambda bank, c: act.activation(dst(c), bank[:, 0:CH], ACT.Copy)

            def put_xr(ft):
                def piece(dst, bank, lo, n):
                    return act.activation(one(xr, ft, dst, dst + n), bank[:, lo:lo + n], ACT.Copy)

                def put(bank, c):
                    if c == 0:
                        piece(2 + OFF1, bank, 0, META)
                        return piece(2, bank, 0, CH)
                    if c == 1:
                        return piece(2 + CH, bank, 0, CH)
                    n = T0 - 2 * CH
                    piece(2 + 2 * CH, bank, 0, n)
                    return piece(2 + OFF1 + META, bank, n, CH - n)
                return put

            act.wait_ge(eps_set, 1)
            norm(0, 0, 0)
            norm(1, 1, 0)
            hi(0, 0)
            split_w(0, 0, 0)
            split_w(1, 1, 0)
            with act.Fori(0, 4) as i:
                norm(2 * i + 2, 0, i + 1)
                hi(2 * i + 1, 1)
                norm(2 * i + 3, 1, i + 1)
                hi(2 * i + 2, 0)
            norm(NB, 0, NB // 2)
            hi(NB - 1, 1)
            hi(NB, 0)

            act.wait_ge(lam_step, 1)
            act.activation(sp_e, sp_z, ACT.Exp).then_inc(lam_e, 1)
            act.wait_ge(xr_cleared, 1)
            for c in range(NCH):
                for f in range(2):
                    n = 2 * c + f
                    act.wait_ge(proj_done, n + 1 + 2 * NCH)
                    put_xr(f)(ps[:, FIRST_BANKS[c][f], :], c).then_inc(proj_out, 1)
                    if n >= 2 * NCH - 2:
                        split_w(f + 2, f, 1)
            for f in range(2, XT):
                for c in range(NCH):
                    evacuate(f, f % 2, c, put_xr(f))
                if f == 2:
                    split_w(XT, 0, XT // 2)
            act.wait_ge(lam_step, LAM_STEPS)
            act.wait_ge(fill_dma, 32)
            with act.Fori(0, FT) as k:
                for d in range(2):
                    n, f = 2 * k + d, 2 * k + XT + d
                    put = put_flat(lambda c: one(feat, 2 * k + d, c * CH, (c + 1) * CH))
                    if d == 0:
                        split_w(f + 1, 1, k + XT // 2)
                    else:
                        split_w(f + 1, 0, k + XT // 2 + 1)
                    act.wait_ge(gates_done, 2 * n + 2)
                    act.wait_ge(u_done, n + 1)
                    act.wait_ge(s_done, n + 1)
                    act.activation(r_g[:, :], flat_r[:, 0:RW], ACT.Sigmoid, bias=vec(k, 5 + 2 * d)).then_inc(r_done, 1)
                    act.wait_ge(gates_done, 2 * n + 3)
                    act.wait_ge(scanned, n + 1)
                    act.activation(i_g[:, :], flat_i[:, 0:RW], ACT.Sigmoid, bias=vec(k, 6 + 2 * d)).then_inc(i_done, 1)
                    evacuate(f, d, 0, put)
                    act.wait_ge(r_done, n + 2)
                    if d == 0:
                        act.wait_ge(summed, k + 1)
                    act.activation(t_g[:, :], r_g[:, :], ACT.Tanh, scale=one(decay, k, d, d + 1)).then_inc(ta_done, 1)
                    act.activation(a_g[:, :], r_g[:, :], ACT.Exp, scale=one(ndecay, k, d, d + 1)).then_inc(ta_done, 1)
                    act.wait_ge(ta_done, 3 * n + 2)
                    act.activation(r_g[:, :], a_g[:, :], ACT.Square).then_inc(ta_done, 1)
                    evacuate(f, d, 1, put)
                    act.wait_ge(v_done, n + 1)
                    act.activation(r_g[:, :], t_g[:, :], ACT.Sqrt).then_inc(s_done, 1)
                    if d == 1:
                        act.wait_ge(proj_out, NCH * (XT + k + 1) + 2)
                        act.activation(one(feat, k, 0, COLS), one(feat, k, 0, COLS), ACT.Gelu_apprx_tanh).then_inc(gelu_done, 1)
                    evacuate(f, d, 2, put)
            split_w(FTILES - 1, 1, FTILES // 2 - 1)
            for s, dst in enumerate((k_pre, v_pre)):
                for c in range(NCH):
                    evacuate(FTILES - 2 + s, s, c, put_flat(lambda c: dst[:, c * CH:(c + 1) * CH]))

        @block.vector
        def _(dve):
            dve.memset(eps_t[:, :], EPS).then_inc(eps_set, 1)
            dve.sem_inc(xn_done, RING)
            dve.sem_inc(h_lo_done, RING)
            dve.sem_inc(w_lo_done, RING)
            dve.sem_inc(u_done, 1)
            dve.sem_inc(scanned, 1)
            dve.sem_inc(summed, 1)
            dve.sem_inc(conv_done, 1)
            dve.sem_inc(rec_done, 2)

            def norm(t, s):
                n = rows(t)
                dve.wait_ge(rms_done, t + 1)
                dve.reciprocal(rstd[s][0:n, :], rms[s][0:n, :]).then_inc(rstd_done, 1)
                dve.wait_ge(rstd_done, t + 1)
                dve.scalar_tensor_tensor(out=xn[s][0:n, :], in0=x_in[s][0:n, :], scalar=rstd[s][0:n, :],
                                         in1=g_bc[0:n, :], op0=ALU.mult, op1=ALU.mult).then_inc(xn_done, 1)

            def lo(t, s):
                n = rows(t)
                dve.wait_ge(h_hi_done, done(t))
                dst = bass.ds(col(t), n)
                dve.tensor_tensor(h_lo[:, :, dst], tr[s].rearrange("p b (k c) -> p (b k) c", c=P)[:, :, 0:n],
                                  h_hi[:, :, dst].bitcast(F32), ALU.subtract).then_inc(h_lo_done, 1)

            def split_w(f, s):
                dve.wait_ge(w_hi_done, done(f))
                dve.tensor_tensor(w_lo[s][:, :, :], w_raw[s][:, :, :], w_hi[s][:, :, :].bitcast(F32),
                                  ALU.subtract).then_inc(w_lo_done, 1)

            dve.wait_ge(consts_in, 32)
            norm(0, 0)
            norm(1, 1)
            lo(0, 0)
            split_w(0, 0)
            split_w(1, 1)
            with dve.Fori(0, 4) as i:
                norm(2 * i + 2, 0)
                lo(2 * i + 1, 1)
                norm(2 * i + 3, 1)
                lo(2 * i + 2, 0)
            norm(NB, 0)
            lo(NB - 1, 1)
            lo(NB, 0)

            step = [0]

            def then(ins):
                step[0] += 1
                ins.then_inc(lam_step, 1)
                dve.wait_ge(lam_step, step[0])

            dve.wait_ge(vecs_in, 16)
            lam = vecs[:, :, 9:11]
            then(dve.scalar_tensor_tensor(out=sp_z, in0=lam, scalar=-1.0, in1=lam, op0=ALU.mult, op1=ALU.min))
            then(dve.tensor_scalar(lam_pos, lam, -1.0, 0.0, ALU.mult, ALU.max))
            dve.wait_ge(lam_e, 1)
            then(dve.tensor_scalar(sp_z2, sp_e, 2.0, None, ALU.add))
            then(dve.reciprocal(sp_p, sp_z2))
            then(dve.tensor_tensor(sp_z, sp_e, sp_p, ALU.mult))
            then(dve.tensor_tensor(sp_z2, sp_z, sp_z, ALU.mult))
            then(dve.memset(sp_p, 1.0 / 17))
            for j in range(15, 0, -2):
                then(dve.tensor_tensor(sp_p, sp_p, sp_z2, ALU.mult))
                then(dve.tensor_scalar(sp_p, sp_p, 1.0 / j, None, ALU.add))
            then(dve.scalar_tensor_tensor(out=sp_p, in0=sp_p, scalar=2.0, in1=sp_z, op0=ALU.mult, op1=ALU.mult))
            then(dve.tensor_tensor(sp_p, sp_p, lam_pos, ALU.add))
            then(dve.tensor_scalar(decay, sp_p, 8.0, None, ALU.mult))
            then(dve.tensor_scalar(ndecay, sp_p, -8.0, None, ALU.mult))
            assert step[0] == LAM_STEPS

            def convolve(ft):
                dve.wait_ge(proj_out, NCH * max(ft, 1) + NCH + 2)
                dve.wait_ge(conv_done, ft + 1)
                src = [one(xr, ft, j, j + RW) for j in range(4)]
                dve.tensor_scalar(conv, src[0], vec(ft, 0), vec(ft, 4), ALU.mult, ALU.add).then_inc(conv_step, 1)
                for j in range(1, 4):
                    dve.wait_ge(conv_step, 3 * ft + j)
                    dve.scalar_tensor_tensor(out=conv if j < 3 else one(xr, ft, 0, RW), in0=src[j], scalar=vec(ft, j),
                                             in1=conv, op0=ALU.mult, op1=ALU.add).then_inc(conv_step if j < 3 else conv_done, 1)

            for ft in range(FT):
                if ft < FT - 1:
                    split_w(ft + 2, ft % 2)
                convolve(ft)

            dve.wait_ge(conv_done, FT + 1)
            with dve.Fori(0, FT) as k:
                for d in range(2):
                    n, f = 2 * k + d, 2 * k + XT + d
                    split_w(f + 1, 1 - d)
                    dve.wait_ge(i_done, n + 2)
                    dve.tensor_tensor(i_g[:, :], i_g[:, :], one(xr, k, 0, RW), ALU.mult).then_inc(ix_done, 1)
                    dve.wait_ge(ta_done, 3 * n + 3)
                    dve.scalar_tensor_tensor(out=t_g[:, :], in0=r_g[:, :], scalar=1.0, in1=t_g[:, :],
                                             op0=ALU.add, op1=ALU.mult).then_inc(v_done, 1)
                    cut = OFF1 if d == 0 else T0 - 1
                    dve.memset(a_g[:, cut:cut + 1], 0.0).then_inc(a_cut, 1)
                    dve.wait_ge(ix_done, n + 1)
                    dve.wait_ge(s_done, n + 2)
                    dve.tensor_tensor(i_g[:, :], i_g[:, :], r_g[:, :], ALU.mult).then_inc(u_done, 1)
                    dve.wait_ge(u_done, n + 2)
                    dve.wait_ge(a_cut, n + 1)
                    if d == 0:
                        dve.wait_ge(rec_done, 2 * k + 2)
                        dve.tensor_tensor_scan(h_g[:, :], a_g[:, :], i_g[:, :], 0.0, ALU.mult, ALU.add).then_inc(scanned, 1)
                    else:
                        dve.tensor_tensor_scan(t_g[:, ::-1], a_g[:, ::-1], i_g[:, ::-1], 0.0, ALU.mult,
                                               ALU.add).then_inc(scanned, 1)
                dve.wait_ge(scanned, 2 * k + 3)
                dve.tensor_tensor(h_g[:, :], h_g[:, :], t_g[:, :], ALU.add).then_inc(summed, 1)
                dve.wait_ge(summed, k + 2)
                dve.wait_ge(gelu_done, k + 1)
                for lo_, hi_, at in ((META, T0, META), (OFF1 + META, RW, T0)):
                    dst = one(feat, k, at, at + hi_ - lo_)
                    dve.tensor_tensor(dst, dst, h_g[:, lo_:hi_], ALU.mult).then_inc(rec_done, 1)
            split_w(FTILES - 1, 1)

        @block.tensor
        def _(pe):
            pe.sem_inc(x_turned, RING)
            pe.sem_inc(proj_done, 2 * NCH)
            pe.sem_inc(gates_done, 1)
            pe.wait_ge(consts_in, 32)

            def turn(t, s):
                n = rows(t)
                pe.wait_ge(xn_done, done(t))
                pe.wait_ge(h_lo_done, free(t))
                for k in range(KD):
                    mm = pe.transpose(tr[s][:, k // 4, (k % 4) * P:(k % 4) * P + n], xn[s][0:n, k * P:(k + 1) * P],
                                      ident[0:n, 0:n])
                mm.then_inc(x_turned, 1)

            def third(s, c, bank, ks=range(KD)):
                cols = slice(c * CH, (c + 1) * CH)
                for k in ks:
                    for n, (w, h) in enumerate(((w_hi, h_hi), (w_hi, h_lo), (w_lo, h_hi))):
                        mm = pe.matmul(ps[:, bank, 0:CH], w[s][:, k, :], h[:, k, cols],
                                       start=(k == 0 and n == 0), stop=(k == KD - 1 and n == 2))
                if ks[-1] == KD - 1:
                    mm.then_inc(proj_done, 1)

            def tile(f, s):
                pe.wait_ge(w_lo_done, done(f))
                for c in range(NCH):
                    pe.wait_ge(proj_out, NCH * f + c + 1)
                    third(s, c, (NCH * s + c) % 2)

            def gate_products(k, d):
                pe.wait_ge(gates_in, 16 * k + 16)
                pe.wait_ge(conv_done, k + 2)
                for bank, g, read in ((ps_r, 2 * d, r_done), (ps_i, 2 * d + 1, i_done)):
                    pe.wait_ge(read, 2 * k + d + 1)
                    for c in range(3):
                        n = min(BANK, RW - c * BANK)
                        mm = pe.matmul(bank[:, c, 0:n], gates[:, g, :], one(xr, k, c * BANK, c * BANK + n),
                                       start=True, stop=True)
                    mm.then_inc(gates_done, 1)

            for t in range(LAST_ROWS[0] + 1):
                turn(t, t % 2)
            ahead = LAST_ROWS[0] + 1
            for c in range(NCH):
                for f in range(2):
                    for ks in (range(0, KD // 2), range(KD // 2, KD)):
                        if ahead <= NB:
                            turn(ahead, ahead % 2)
                            ahead += 1
                        pe.wait_ge(h_lo_done, done(LAST_ROWS[c]))
                        pe.wait_ge(w_lo_done, done(f))
                        third(f, c, FIRST_BANKS[c][f], ks)
            assert ahead == NB + 1
            for f in range(2, XT):
                tile(f, f % 2)
            with pe.Fori(0, FT) as k:
                for d in range(2):
                    gate_products(k, d)
                    tile(2 * k + XT + d, d)
            tile(FTILES - 2, 0)
            tile(FTILES - 1, 1)


def keys(nc, sem, a, k_pre, v_pre, yg, k_dram, v_tok, v_meta, wo_hi, wo_lo, rstd_rec, ident, eps_t):
    with ExitStack() as ctx:
        def sb(name, shape, dt=F32):
            return ctx.enter_context(nc.sbuf_tensor(name, shape, dt))

        cos = sb("cos_k", [P, COLS])
        sin = sb("sin_k", [P, COLS])
        swap = sb("swap_k", [P, P])
        ones = sb("ones_r", [P, 1])
        k_cos = sb("k_cos", [P, COLS])
        k_hi = sb("k_hi", [P, META + P + REAL + P], F32R)
        k_lo = sb("k_lo", [P, META + P + REAL + P], F32R)
        k_sin = sin
        v_small = sb("v_small", [META, P])
        square = sb("square", [P, FT, REAL])
        g_out = sb("g_out", [P, KD])
        wo_raw = sb("wo_raw", [P, KD, D])
        rms_r = sb("rms_r", [P, NB])
        ssq_r = sb("ssq_r", [P, NB])
        ps_k = ctx.enter_context(nc.psum_tensor("ps_k", [P, 3, BANK], F32))
        ps_v = ctx.enter_context(nc.psum_tensor("ps_v", [P, 3, BANK], F32))
        ps_s = ctx.enter_context(nc.psum_tensor("ps_s", [P, BANK], F32))
        ps_m = ctx.enter_context(nc.psum_tensor("ps_m", [P, BANK], F32))

        swap_in = sem("k_swap_in")
        g_out_in = sem("k_g_out_in")
        wo_in = [sem(f"k_wo_in{k}") for k in range(KD)]
        wo_hi_done = sem("k_wo_hi_done")
        tables_in = sem("k_tables_in")
        cleared = sem("k_cleared")
        vmeta_in = sem("k_vmeta_in")
        k_swapped = sem("k_swapped")
        v_turned = sem("k_v_turned")
        k_cos_done = sem("k_cos_done")
        k_sin_done = sem("k_sin_done")
        k_summed = sem("k_summed")
        k_hi_done = sem("k_hi_done")
        k_lo_done = sem("k_lo_done")
        pads_done = sem("k_pads_done")
        k_stored = sem("k_stored")
        v_out = sem("k_v_out")
        sq_done = sem("k_sq_done")
        ss_done = sem("k_ss_done")
        ss_summed = sem("k_ss_summed")
        rms_done = sem("k_rms_done")
        columns = ((slice(0, META), slice(0, META)), (slice(META + P, META + P + REAL), slice(META, COLS)))
        block = ctx.enter_context(nc.Block())

        @block.sync
        def _(sp):
            sp.dma_start(swap[:, :], a["swap"]).then_inc(swap_in, 16)
            sp.dma_start(cos[:, :], a["cos"]).then_inc(tables_in, 16)
            sp.dma_start(sin[:, :], a["sin"]).then_inc(tables_in, 16)
            sp.dma_start(g_out[:, :], a["g_out"]).then_inc(g_out_in, 16)
            for k in range(KD):
                sp.dma_start(wo_raw[:, k, :], a["w_out"][:, k, :]).then_inc(wo_in[k], 16)
            sp.wait_ge(v_out, 1)
            sp.wait_ge(cleared, 4)
            for h in range(HEADS):
                g = h // 4
                sp.dma_start(v_meta[h * META:(h + 1) * META, h * HD:(h + 1) * HD],
                             v_small[:, g * HD:(g + 1) * HD]).then_inc(vmeta_in, 16)
            sp.wait_ge(pads_done, 4)
            for part, (k, done) in enumerate(((k_hi, k_hi_done), (k_lo, k_lo_done))):
                sp.wait_ge(done, 1)
                for g in range(2):
                    for rows in (slice(0, HD), slice(HD, P)):
                        sp.dma_start(k_dram[rows, g, part, :].bitcast(F32), k[g * HD:(g + 1) * HD, :].bitcast(F32)).then_inc(k_stored, 16)
            sp.wait_ge(k_stored, 16 * 8)
            sp.wait_ge(vmeta_in, 16 * HEADS)

        @block.gpsimd
        def _(pool):
            pool.memset(v_meta[:, :], 0.0).then_inc(cleared, 1)
            pool.memset(ones[:, :], 1.0).then_inc(cleared, 1)
            for t in (k_hi, k_lo):
                for lo in (META, META + P + REAL):
                    pool.memset(t[:, lo:lo + P].bitcast(F32), 0.0).then_inc(pads_done, 1)
            pool.memset(v_tok[:, 0:P], 0.0).then_inc(cleared, 1)
            pool.memset(v_tok[:, (NB + 1) * P:(NB + 2) * P], 0.0).then_inc(cleared, 1)
            pool.wait_ge(tables_in, 32)
            pool.tensor_tensor(k_cos[:, :], k_pre[:, :], cos[:, :], ALU.mult).then_inc(k_cos_done, 1)

        @block.tensor
        def _(pe):
            pe.transpose(ps_m[0:META, 0:P], v_pre[:, 0:META], ident[:, :]).then_inc(v_turned, 1)
            for b in range(NB):
                mm = pe.transpose(ps_v[:, b // 4, (b % 4) * P:(b % 4 + 1) * P],
                                  v_pre[:, META + b * P:META + (b + 1) * P], ident[:, :])
            mm.then_inc(v_turned, 1)
            pe.wait_ge(swap_in, 16)
            for c in range(NCH):
                mm = pe.matmul(ps_k[:, c, 0:CH], swap[:, :], k_pre[:, c * CH:(c + 1) * CH], start=True, stop=True)
            mm.then_inc(k_swapped, 1)
            pe.wait_ge(cleared, 4)
            for ft in range(FT):
                pe.wait_ge(sq_done, ft + 1)
                for b in range(NB):
                    n = ft * NB + b
                    mm = pe.matmul(ps_s[:, n:n + 1], square[:, ft, b * P:(b + 1) * P], ones[:, :], start=True, stop=True)
            mm.then_inc(ss_done, 1)

        @block.scalar
        def _(act):
            act.wait_ge(v_turned, 1)
            act.activation(v_small[:, :], ps_m[0:META, 0:P], ACT.Copy).then_inc(v_out, 1)
            act.wait_ge(v_turned, 2)
            act.activation(v_tok[:, P:(NB + 1) * P], ps_v[:, :, :].rearrange("p b c -> p (b c)")[:, 0:REAL], ACT.Copy)
            for ft in range(FT):
                act.activation(square[:, ft, :], yg[:, ft, META:COLS], ACT.Square).then_inc(sq_done, 1)
            act.wait_ge(k_summed, 1)
            for dst, src in columns:
                ins = act.activation(k_hi[:, dst], k_cos[:, src], ACT.Copy)
            ins.then_inc(k_hi_done, 1)
            act.wait_ge(g_out_in, 16)
            for k in range(KD):
                act.wait_ge(wo_in[k], 16)
                act.activation(wo_hi[:, k, :], wo_raw[:, k, :], ACT.Copy, scale=g_out[:, k:k + 1]).then_inc(wo_hi_done, 1)
            act.wait_ge(ss_summed, 1)
            act.activation(rms_r[:, :], ssq_r[:, :], ACT.Sqrt, bias=eps_t[:, :], scale=1.0 / REC).then_inc(rms_done, 1)

        @block.vector
        def _(dve):
            dve.wait_ge(k_swapped, 1)
            dve.wait_ge(tables_in, 32)
            for c in range(NCH):
                ins = dve.tensor_tensor(k_sin[:, c * CH:(c + 1) * CH], ps_k[:, c, 0:CH], sin[:, c * CH:(c + 1) * CH], ALU.mult)
            ins.then_inc(k_sin_done, 1)
            dve.wait_ge(k_sin_done, 1)
            dve.wait_ge(k_cos_done, 1)
            dve.tensor_tensor(k_cos[:, :], k_cos[:, :], k_sin[:, :], ALU.add).then_inc(k_summed, 1)
            dve.wait_ge(k_hi_done, 1)
            for dst, src in columns:
                ins = dve.tensor_tensor(k_lo[:, dst], k_cos[:, src], k_hi[:, dst].bitcast(F32), ALU.subtract)
            ins.then_inc(k_lo_done, 1)
            for k in range(KD):
                if k == KD // 2:
                    dve.wait_ge(ss_done, 1)
                    dve.tensor_reduce(ssq_r[:, :], ps_s[:, 0:FT * NB].rearrange("p (f b) -> p b f", b=NB), AX.X,
                                      ALU.add).then_inc(ss_summed, 1)
                dve.wait_ge(wo_hi_done, k + 1)
                dve.scalar_tensor_tensor(out=wo_lo[:, k, :], in0=wo_raw[:, k, :], scalar=g_out[:, k:k + 1],
                                         in1=wo_hi[:, k, :].bitcast(F32), op0=ALU.mult, op1=ALU.subtract)
            dve.wait_ge(rms_done, 1)
            dve.reciprocal(rstd_rec[:, :], rms_r[:, :])


LAM_STEPS = 27


def mix(nc, sem, a, spare, q_pre, rec, rstd_rec, w_hi, w_lo, k_dram, v_tok, v_meta, ident, eps_t, iota_e,
        gate1, gate2, expert1, expert2, place1, place2, counts, h2_dram, u_dram, list_dram):
    with ExitStack() as ctx:
        def sb(name, shape, dt=F32):
            return ctx.enter_context(nc.sbuf_tensor(name, shape, dt))

        g_ffn = sb("g_ffn", [P, D])
        router = sb("router", [P, KD, ROUT])
        rbias = sb("rbias_bc", [P, ROUT])
        sink = sb("sink_bc", [P, HEADS])
        swap = sb("swap_q", [P, P])
        before = sb("before_sb", [P, P])
        ones = sb("ones_m", [P, P])
        group_of = sb("group_of", [P, EXP])
        token = sb("token", [P, NB], I32)
        k_win = [[sb(f"k_win{s}{g}", [P, 2, KEYS], F32R) for g in range(2)] for s in range(RING)]
        mask = [sb(f"mask{s}", [P, KEYS]) for s in range(RING)]
        cos = [sb(f"cos_q{s}", [P, P]) for s in range(RING)]
        sin = [sb(f"sin_q{s}", [P, P]) for s in range(RING)]
        xh = [sb(f"xh{s}", [P, D]) for s in range(RING)]
        u = spare[0][:, 0:D]
        q_cos = sb("q_cos", [P, ATTN])
        q_sin = sb("q_sin", [P, ATTN])
        q_parts = sb("q_parts", [P, HEADS, P], F32R)
        probs = sb("probs", [P, HEADS, KEYS])
        probs_t = sb("probs_t", [P, HEADS, WIN])
        meta_p = sb("meta_p", [P, P])
        meta_t = sb("meta_t", [P, P])
        smax = sb("smax", [P, HEADS])
        nmax = sb("nmax", [P, HEADS])
        rowsum = sb("rowsum", [P, HEADS])
        sink_d = sb("sink_d", [P, HEADS])
        sink_e = sb("sink_e", [P, HEADS])
        den = sb("den", [P, HEADS])
        rden = sb("rden", [P, HEADS])
        attn_o = sb("attn_o", [P, ATTN])
        junk = sb("junk", [P, ATTN])
        ssq_a = sb("ssq_a", [P, 1])
        rms_a = sb("rms_a", [P, 1])
        rstd_a = sb("rstd_a", [P, 1])
        a_hi = sb("a_hi", [P, FT, P], F32R)
        a_lo = sb("a_lo", [P, FT, P], F32R)
        r_hi = sb("rec_hi", [P, FT, P], F32R)
        r_lo = sb("rec_lo", [P, FT, P], F32R)
        ssq_h = sb("ssq_h", [P, 1])
        rms_h = sb("rms_h", [P, 1])
        rstd_h = sb("rstd_h", [P, 1])
        u_t = spare[1][:, 0:D].rearrange("p (k c) -> p k c", c=P)
        logits = sb("logits", [P, ROUT])
        gtop = sb("gtop", [P, 8])
        gidx = sb("gidx", [P, 8], U32)
        gidx_f = sb("gidx_f", [P, 1])
        ngtop = sb("ngtop", [P, 1])
        gexp = sb("gexp", [P, 4])
        gsum = sb("gsum", [P, 1])
        mlog = sb("mlog", [P, EXP])
        etop = sb("etop", [P, 8])
        eidx = sb("eidx", [P, 8], U32)
        ediff = sb("ediff", [P, 1])
        eexp = sb("eexp", [P, 1])
        gden = sb("gden", [P, 1])
        hot1 = sb("hot1", [P, EXP])
        hot2 = sb("hot2", [P, EXP])
        hot = sb("hot", [P, EXP])
        base = sb("base", [P, EXP])
        prod = [sb(f"prod{j}", [P, EXP]) for j in range(2)]
        token_s = [sb(f"token_s{s}", [P, 1], I32) for s in range(RING)]
        addr = [[sb(f"addr{j}{s}", [P, 1], I32) for s in range(RING)] for j in range(2)]

        ps_sc = [ctx.enter_context(nc.psum_tensor(f"ps_sc{s}", [P, BANK], F32)) for s in range(2)]
        ps_t = [ctx.enter_context(nc.psum_tensor(f"ps_t{s}", [P, BANK], F32)) for s in range(2)]
        ps_o = ctx.enter_context(nc.psum_tensor("ps_o", [P, BANK], F32))
        ps_y = [ctx.enter_context(nc.psum_tensor(f"ps_y{s}", [P, BANK], F32)) for s in range(2)]
        ps_x = ctx.enter_context(nc.psum_tensor("ps_x", [P, BANK], F32))

        waited = sem("m_waited")
        swap_in = sem("m_swap_in")
        k_meta_in = [sem(f"m_k_meta_in{s}") for s in range(RING)]
        sink_in = sem("m_sink_in")
        consts_in = sem("m_consts_in")
        cleared = sem("m_cleared")
        tables_in = [sem(f"m_tables_in{s}") for s in range(RING)]
        keys_in = [sem(f"m_keys_in{s}") for s in range(RING)]
        x_in = [sem(f"m_x_in{s}") for s in range(RING)]
        h2_out = sem("m_h2_out")
        u_out = sem("m_u_out")
        q_swapped = sem("m_q_swapped")
        q_cos_done = sem("m_q_cos_done")
        q_sin_done = sem("m_q_sin_done")
        q_summed = sem("m_q_summed")
        q_hi_done = sem("m_q_hi_done")
        q_lo_done = sem("m_q_lo_done")
        scored = sem("m_scored")
        scaled = sem("m_scaled")
        nmax_done = sem("m_nmax_done")
        exp_done = sem("m_exp_done")
        sink_d_done = sem("m_sink_d_done")
        sink_e_done = sem("m_sink_e_done")
        turned = sem("m_turned")
        pt_out = sem("m_pt_out")
        meta_packed = sem("m_meta_packed")
        meta_turned = sem("m_meta_turned")
        meta_out = sem("m_meta_out")
        av_done = sem("m_av_done")
        den_done = sem("m_den_done")
        ao_done = sem("m_ao_done")
        ssq_a_done = sem("m_ssq_a_done")
        rms_a_done = sem("m_rms_a_done")
        rstd_a_done = sem("m_rstd_a_done")
        ao_turned = sem("m_ao_turned")
        a_hi_done = sem("m_a_hi_done")
        a_lo_done = sem("m_a_lo_done")
        r_hi_done = sem("m_r_hi_done")
        r_lo_done = sem("m_r_lo_done")
        y_done = sem("m_y_done")
        y_read = sem("m_y_read")
        ssq_h_done = sem("m_ssq_h_done")
        rms_h_done = sem("m_rms_h_done")
        rstd_h_done = sem("m_rstd_h_done")
        u_done = sem("m_u_done")
        u_turned = sem("m_u_turned")
        u_t_out = sem("m_u_t_out")
        logits_done = sem("m_logits_done")
        route_step = sem("m_route_step")
        gexp_done = sem("m_gexp_done")
        eexp_done = sem("m_eexp_done")
        ranked = sem("m_ranked")
        place_step = sem("m_place_step")
        token_done = sem("m_token_done")
        addr_done = sem("m_addr_done")
        listed = [sem(f"m_listed{s}") for s in range(RING)]

        AT_LOGITS, AT_NGTOP, AT_EDIFF, AT_HOT, ROUTE_STEPS = 1, 5, 9, 18, 18
        PLACE_STEPS = 8
        PLACE0 = 2 * PLACE_STEPS

        block = ctx.enter_context(nc.Block())

        def take_waits(eng):
            eng.sem_inc(waited, 1)

        def run(eng, step, peeled=2):
            step(0, None, None, 0)
            eng.wait_ge(consts_in, 64)
            step(1, 0, None, 1)
            with eng.Fori(0, (NB - peeled) // 2 - 1) as i:
                step(2 * i + 2, 2 * i + 1, 2 * i, 0)
                step(2 * i + 3, 2 * i + 2, 2 * i + 1, 1)
            for t in range(NB - peeled, NB):
                step(t, t - 1, t - 2, t % 2)
            step(None, NB - 1, NB - 2, 0)
            step(None, None, NB - 1, 1)

        def tables_of(t, s):
            return 48 * (t // 2 + 1) if isinstance(t, int) else 24 * (t - s) + 48

        group_rows = ((slice(0, HD), slice(0, 4)), (slice(HD, P), slice(4, 8)))

        def has_next(t):
            return not isinstance(t, int) or t + 1 < NB

        def at_most_blocks(v):
            return min(v, NB) if isinstance(v, int) else v

        def half(i):
            return slice(i * BANK, (i + 1) * BANK)

        @block.sync
        def _(sp):
            def tables(t, s):
                sp.dma_start(mask[s][:, :], a["masks"][bass.ds(t, 1), :, :].rearrange("o p c -> (o p) c")).then_inc(tables_in[s], 16)
                sp.dma_start(cos[s][:, :], a["cos"][:, bass.ds(META + t * P, P)]).then_inc(tables_in[s], 16)
                sp.dma_start(sin[s][:, :], a["sin"][:, bass.ds(META + t * P, P)]).then_inc(tables_in[s], 16)

            def load_x(t, s):
                sp.dma_start(xh[s][:, :], a["x"][bass.ds(t * P, P), :]).then_inc(x_in[s], 16)

            sp.dma_start(swap[:, :], a["swap"]).then_inc(swap_in, 16)
            tables(0, 0)
            sp.dma_start(sink[:, :], a["sink"][0].partition_broadcast(P)).then_inc(sink_in, 16)
            load_x(0, 0)
            for dst, src in ((g_ffn[:, :], a["ln_ffn_g"][0].partition_broadcast(P)),
                             (router[:, :, :], a["router"]), (rbias[:, :], a["rbias"][0].partition_broadcast(P)),
                             (before[:, :], a["before"])):
                sp.dma_start(dst, src).then_inc(consts_in, 16)
            load_x(1, 1)

            def attn(t, s):
                if isinstance(t, int) and t == 0:
                    tables(1, 1)
                    return
                if isinstance(t, int) and t == NB - 1:
                    return
                sp.wait_ge(nmax_done, 2 * t)
                sp.wait_ge(q_cos_done, t)
                sp.wait_ge(q_sin_done, t)
                tables(t + 1, 1 - s)

            def outer(b, s):
                sp.wait_ge(u_done, b + 1)
                sp.dma_start(h2_dram[bass.ds(b * P, P), :], xh[s][:, :]).then_inc(h2_out, 16)
                sp.dma_start(u_dram[bass.ds(b * P, P), :], u[:, :]).then_inc(u_out, 16)
                sp.wait_ge(h2_out, 16 * b + 16)
                if not isinstance(b, int) or b + 2 < NB:
                    load_x(b + 2, s)

            def step(t, b1, b2, s):
                if t is not None:
                    attn(t, s)
                if b1 is not None:
                    outer(b1, 1 - s)

            run(sp, step)
            sp.wait_ge(u_out, 16 * NB)
            for s in range(RING):
                sp.wait_ge(listed[s], 32 * NB // 2)

        @block.gpsimd
        def _(pool):
            def keys(s, dst, src, done):
                for g in range(2):
                    pool.dma_start(k_win[s][g][:, :, dst], k_dram[:, g, :, src]).then_inc(done, 16)

            def window(t, s):
                if not isinstance(t, int) or t >= 2:
                    pool.wait_ge(scored, HEADS * t - HEADS)
                    take_waits(pool)
                keys(s, slice(0, WIN), bass.ds(META + t * P, WIN), keys_in[s])

            pool.memset(ones[:, :], 1.0).then_inc(cleared, 1)
            pool.memset(counts[:, :], 0.0).then_inc(cleared, 1)
            pool.iota(group_of[:, :], pattern=[[1, 4], [0, 8]], base=0, channel_multiplier=0,
                      allow_small_or_imprecise_dtypes=True).then_inc(cleared, 1)
            pool.iota(token[:, :], pattern=[[P, NB]], base=0, channel_multiplier=1).then_inc(cleared, 1)
            pool.wait_ge(cleared, 4)

            def rope_cos(t, s):
                pool.wait_ge(tables_in[s], tables_of(t, s))
                pool.wait_ge(q_lo_done, t + 1)
                pool.tensor_tensor(q_cos[:, :].rearrange("p (h c) -> p h c", c=P), q_pre[:, :, bass.ds(META + t * P, P)],
                                   cos[s][:, :].unsqueeze(1).to_broadcast([P, 4, P]), ALU.mult).then_inc(q_cos_done, 1)

            def attn(t, s):
                if has_next(t):
                    window(t + 1, 1 - s)
                    rope_cos(t + 1, 1 - s)
                pool.wait_ge(exp_done, HEADS * t + HEADS)
                pool.wait_ge(meta_turned, t) if not isinstance(t, int) or t > 0 else None
                take_waits(pool)
                pool.tensor_copy(meta_p[:, :].rearrange("p (h m) -> p h m", m=META), probs[:, :, WIN:KEYS]).then_inc(meta_packed, 1)

                pool.wait_ge(r_hi_done, t + 1)
                pool.tensor_tensor(r_lo[:, :, :], rec[:, :, bass.ds(t * P, P)], r_hi[:, :, :].bitcast(F32),
                                   ALU.subtract).then_inc(r_lo_done, 1)

            def place(b, s):
                pool.wait_ge(addr_done, 2 * b + 2)
                if not isinstance(b, int) or b >= 2:
                    pool.wait_ge(listed[s], 16 * (b - s))
                take_waits(pool)
                pool.tensor_copy(token_s[s][:, :], token[:, bass.ds(b, 1)]).then_inc(token_done, 1)
                pool.wait_ge(token_done, b + 1)
                take_waits(pool)
                for j in range(2):
                    pool.indirect_dma_start(list_dram, bass.IndirectOffsetOnAxis(ap=addr[j][s][:, 0:1], axis=0),
                                            token_s[s][:, 0:1], None).then_inc(listed[s], 16)

            def step(t, b1, b2, s):
                if t is not None:
                    attn(t, s)
                if b2 is not None:
                    place(b2, s)

            window(0, 0)
            rope_cos(0, 0)
            for s in range(RING):
                keys(s, slice(WIN, KEYS), slice(0, META), k_meta_in[s])
            run(pool, step)

        @block.tensor
        def _(pe):
            pe.wait_ge(swap_in, 16)
            pe.sem_inc(av_done, 1)
            pe.sem_inc(logits_done, 1)

            def swap_q(t):
                if not isinstance(t, int) or t >= 2:
                    pe.wait_ge(place_step, PLACE_STEPS * t - PLACE_STEPS + 2)
                pe.matmul(ps_x[:, :], swap[:, :], q_pre[:, :, bass.ds(META + t * P, P)], start=True, stop=True
                          ).then_inc(q_swapped, 1)

            def scores(t, s, heads):
                if heads[0] == 0:
                    pe.wait_ge(q_lo_done, t + 2)
                    if isinstance(t, int) and t < RING:
                        pe.wait_ge(k_meta_in[s], 32)
                    pe.wait_ge(keys_in[s], 32 * (t // 2 + 1) if isinstance(t, int) else 16 * (t - s) + 32)
                for h in heads:
                    pe.wait_ge(scaled, HEADS * t + h + 1)
                    for part in range(2):
                        mm = pe.matmul(ps_sc[h % 2][:, 0:KEYS], q_parts[:, h, :], k_win[s][h // 4][:, part, :],
                                       start=(part == 0), stop=(part == 1))
                    mm.then_inc(scored, 1)

            def turn_probs(t, heads):
                for h in heads:
                    n = HEADS * t + h
                    pe.wait_ge(exp_done, n + 1)
                    pe.wait_ge(pt_out, n + 1)
                    for j in range(3):
                        mm = pe.transpose(ps_t[h % 2][:, j * P:(j + 1) * P], probs[:, h, j * P:(j + 1) * P], ident[:, :])
                    mm.then_inc(turned, 1)

            def turn_meta(t):
                pe.wait_ge(ao_done, t + 1)
                pe.wait_ge(meta_packed, t + 1)
                pe.transpose(ps_o[:, 0:P], meta_p[:, :], ident[:, :]).then_inc(meta_turned, 1)

            def times_v(t):
                pe.wait_ge(meta_out, t + 1)
                pe.matmul(ps_o[:, :], meta_t[:, :], v_meta[:, :], start=True, stop=False, skip_group_check=True)
                if has_next(t):
                    swap_q(t + 1)
                for h in range(HEADS):
                    pe.wait_ge(pt_out, HEADS * t + h + 3)
                    for j in range(3):
                        last = h == HEADS - 1 and j == 2
                        mm = pe.matmul(ps_o[:, h * HD:(h + 1) * HD], probs_t[:, h, j * P:(j + 1) * P],
                                       v_tok[:, bass.ds(t * P + j * P + (h // 4) * HD, HD)], start=False, stop=last,
                                       skip_group_check=True)
                mm.then_inc(av_done, 1)

            def turn_u(b, i):
                if i == 0:
                    pe.wait_ge(u_done, b + 1)
                else:
                    pe.wait_ge(a_lo_done, at_most_blocks(b + 2) + 2)
                for k in range(4):
                    mm = pe.transpose(ps_t[1 - i][:, k * P:(k + 1) * P], u[:, (4 * i + k) * P:(4 * i + k + 1) * P], ident[:, :])
                mm.then_inc(u_turned, 1)

            def route(b):
                pe.wait_ge(u_t_out, 2 * b + 4)
                pe.wait_ge(q_sin_done, at_most_blocks(b + 3))
                if isinstance(b, int) and b >= NB - 2:
                    pe.wait_ge(place_step, PLACE_STEPS * (b - 1) + PLACE0 + 2)
                for k in range(KD):
                    mm = pe.matmul(ps_x[:, 0:ROUT], u_t[:, k, :], router[:, k, :], start=(k == 0), stop=(k == KD - 1))
                mm.then_inc(logits_done, 1)

            def turn_attn(b):
                pe.wait_ge(ao_done, b + 2)
                for k in range(FT):
                    mm = pe.transpose(ps_t[0][:, k * P:(k + 1) * P], attn_o[:, k * P:(k + 1) * P], ident[:, :])
                mm.then_inc(ao_turned, 1)

            def out_product(b, part, i, ks=range(FT)):
                x_hi, x_lo, k0 = ((r_hi, r_lo, FT), (a_hi, a_lo, 0))[part]
                if part == 0:
                    pe.wait_ge(r_lo_done, b + 1)
                else:
                    pe.wait_ge(a_lo_done, b + 3)
                pe.wait_ge(y_read, 4 * b + 2 * part + i + 1)
                for k in ks:
                    for n, (x, w) in enumerate(((x_hi, w_hi), (x_hi, w_lo), (x_lo, w_hi))):
                        mm = pe.matmul(ps_y[i][:, :], x[:, k, :], w[:, k0 + k, half(i)],
                                       start=(k == 0 and n == 0), stop=(k == FT - 1 and n == 2))
                if ks[-1] == FT - 1:
                    mm.then_inc(y_done, 1)

            def place(b):
                pe.wait_ge(route_step, ROUTE_STEPS * b + AT_HOT)
                pe.matmul(ps_x[:, 0:EXP], before[:, :], hot[:, :], start=True, stop=True)
                pe.matmul(ps_x[:, EXP:2 * EXP], ones[:, :], hot[:, :], start=True, stop=True).then_inc(ranked, 1)

            def step(t, b1, b2, s):
                if t is not None:
                    scores(t, s, range(0, 2))
                if b1 is not None:
                    out_product(b1, 0, 0)
                if t is not None:
                    scores(t, s, range(2, 4))
                if b1 is not None:
                    turn_attn(b1)
                if b2 is not None:
                    turn_u(b2, 0)
                if b1 is not None:
                    out_product(b1, 0, 1)
                if t is not None:
                    scores(t, s, range(4, 6))
                if b2 is not None:
                    turn_u(b2, 1)
                if t is not None:
                    scores(t, s, range(6, 8))
                if b2 is not None:
                    route(b2)
                for i in range(2):
                    for j in range(2):
                        if b1 is not None:
                            out_product(b1, 1, i, range(2 * j, 2 * j + 2))
                        if t is not None:
                            turn_probs(t, range(4 * i + 2 * j, 4 * i + 2 * j + 2))
                if t is not None:
                    turn_meta(t)
                if b2 is not None:
                    place(b2)
                if t is not None:
                    times_v(t)

            swap_q(0)
            pe.wait_ge(cleared, 4)
            run(pe, step)

        @block.scalar
        def _(act):
            def exponentials(t, heads):
                act.wait_ge(nmax_done, 2 * t + heads[0] // 4 + 1)
                if heads[0] == 0:
                    act.wait_ge(den_done, 2 * t + 1)
                for h in heads:
                    act.activation(probs[:, h, :], probs[:, h, :], ACT.Exp, bias=nmax[:, h:h + 1],
                                   accum_out=rowsum[:, h:h + 1]).then_inc(exp_done, 1)

            def sink_and_rec(t):
                act.wait_ge(sink_d_done, t + 1)
                act.activation(sink_e[:, :], sink_d[:, :], ACT.Exp).then_inc(sink_e_done, 1)
                if not isinstance(t, int) or t > 0:
                    act.wait_ge(y_done, 4 * t - 2)
                    act.wait_ge(r_lo_done, t)
                act.activation(r_hi[:, :, :], rec[:, :, bass.ds(t * P, P)], ACT.Copy).then_inc(r_hi_done, 1)

            def probs_out(t, heads):
                for h in heads:
                    act.wait_ge(turned, HEADS * t + h + 1)
                    if h == 0:
                        act.wait_ge(av_done, t + 1)
                    act.activation(probs_t[:, h, :], ps_t[h % 2][:, 0:WIN], ACT.Copy).then_inc(pt_out, 1)

            def meta_copy(t):
                act.wait_ge(meta_turned, t + 1)
                act.activation(meta_t[:, :], ps_o[:, 0:P], ACT.Copy).then_inc(meta_out, 1)

            def u_out_of_psum(b, i):
                act.wait_ge(logits_done, b + 1)
                act.wait_ge(u_turned, 2 * b + i + 1)
                act.activation(u_t[:, 4 * i:4 * i + 4, :], ps_t[1 - i][:, :].rearrange("p (k c) -> p k c", c=P), ACT.Copy
                               ).then_inc(u_t_out, 1)

            def route(b):
                act.wait_ge(route_step, ROUTE_STEPS * b + AT_NGTOP)
                act.activation(gexp[:, :], logits[:, 0:4], ACT.Exp, bias=ngtop[:, :], accum_out=gsum[:, :]).then_inc(gexp_done, 1)
                act.wait_ge(route_step, ROUTE_STEPS * b + AT_EDIFF)
                act.activation(eexp[:, :], ediff[:, :], ACT.Exp).then_inc(eexp_done, 1)

            def q_split(t):
                act.wait_ge(q_summed, t + 1)
                act.wait_ge(scored, HEADS * t) if not isinstance(t, int) or t > 0 else None
                for rows, heads in group_rows:
                    ins = act.activation(q_parts[rows, heads, :], q_cos[rows, :].rearrange("p (h c) -> p h c", c=P), ACT.Copy)
                ins.then_inc(q_hi_done, 1)

            def attn_rms(b):
                act.wait_ge(ao_done, b + 2)
                if not isinstance(b, int) or b > 0:
                    act.wait_ge(ssq_a_done, b)
                    act.wait_ge(rms_a_done, b)
                act.activation(junk[:, :], attn_o[:, :], ACT.Square, accum_out=ssq_a[:, :]).then_inc(ssq_a_done, 1)
                act.wait_ge(ssq_a_done, b + 1)
                act.wait_ge(rstd_a_done, b) if not isinstance(b, int) or b > 0 else None
                act.activation(rms_a[:, :], ssq_a[:, :], ACT.Sqrt, bias=eps_t[:, :], scale=1.0 / ATTN).then_inc(rms_a_done, 1)

            def attn_split(b):
                act.wait_ge(y_done, 4 * b) if not isinstance(b, int) or b > 0 else None
                act.wait_ge(ao_turned, b + 1)
                act.activation(a_hi[:, :, :], ps_t[0][:, :].rearrange("p (k c) -> p k c", c=P), ACT.Copy).then_inc(a_hi_done, 1)

            def h2_rms(b, s):
                act.wait_ge(y_read, 4 * b + 6)
                if not isinstance(b, int) or b > 0:
                    act.wait_ge(u_turned, 2 * b)
                    act.wait_ge(u_out, 16 * b)
                    act.wait_ge(rms_h_done, b)
                act.activation(u[:, :], xh[s][:, :], ACT.Square, accum_out=ssq_h[:, :]).then_inc(ssq_h_done, 1)
                act.wait_ge(ssq_h_done, b + 1)
                act.wait_ge(rstd_h_done, b) if not isinstance(b, int) or b > 0 else None
                act.activation(rms_h[:, :], ssq_h[:, :], ACT.Sqrt, bias=eps_t[:, :], scale=1.0 / D).then_inc(rms_h_done, 1)

            def step(t, b1, b2, s):
                if b1 is not None:
                    attn_rms(b1)
                    attn_split(b1)
                if b2 is not None:
                    u_out_of_psum(b2, 0)
                if t is not None:
                    exponentials(t, range(0, 4))
                if b2 is not None:
                    u_out_of_psum(b2, 1)
                if t is not None:
                    exponentials(t, range(4, 8))
                    sink_and_rec(t)
                if b2 is not None:
                    route(b2)
                if t is not None:
                    probs_out(t, range(HEADS))
                    meta_copy(t)
                if b1 is not None:
                    h2_rms(b1, 1 - s)
                if t is not None and has_next(t):
                    q_split(t + 1)

            act.sem_inc(u_t_out, 2)
            act.sem_inc(pt_out, 2)
            q_split(0)
            run(act, step)

        @block.vector
        def _(dve):
            dve.sem_inc(a_lo_done, 2)
            dve.sem_inc(scaled, 2)
            dve.sem_inc(place_step, PLACE0)
            dve.sem_inc(ao_done, 1)
            dve.sem_inc(q_lo_done, 1)
            dve.sem_inc(den_done, 1)
            dve.sem_inc(y_read, 2)

            def rope_q(t, s):
                dve.wait_ge(q_swapped, t + 1)
                dve.wait_ge(tables_in[s], tables_of(t, s))
                dve.tensor_tensor(q_sin[:, :].rearrange("p (h c) -> p h c", c=P), ps_x[:, :].rearrange("p (h c) -> p h c", c=P),
                                  sin[s][:, :].unsqueeze(1).to_broadcast([P, 4, P]), ALU.mult).then_inc(q_sin_done, 1)
                dve.wait_ge(q_sin_done, t + 1)
                dve.wait_ge(q_cos_done, t + 1)
                dve.tensor_tensor(q_cos[:, :], q_cos[:, :], q_sin[:, :], ALU.add).then_inc(q_summed, 1)

            def split_q(t):
                dve.wait_ge(q_hi_done, t + 1)
                for (own, heads), (other, _) in (group_rows, group_rows[::-1]):
                    ins = dve.tensor_tensor(q_parts[other, heads, :], q_cos[own, :].rearrange("p (h c) -> p h c", c=P),
                                            q_parts[own, heads, :].bitcast(F32), ALU.subtract)
                ins.then_inc(q_lo_done, 1)

            def softmax_max(t, s, heads):
                for h in heads:
                    n = HEADS * t + h
                    dve.wait_ge(scored, n + 1)
                    if h == 0 and (not isinstance(t, int) or t > 0):
                        dve.wait_ge(meta_turned, t)
                        dve.wait_ge(exp_done, HEADS * t)
                        dve.wait_ge(sink_d_done, t)
                        dve.wait_ge(nmax_done, 2 * t)
                    take_waits(dve)
                    dve.tensor_tensor_reduce(probs[:, h, :], ps_sc[h % 2][:, 0:KEYS], mask[s][:, :], HD ** -0.5, sink[:, h:h + 1],
                                             ALU.add, ALU.max, smax[:, h:h + 1]).then_inc(scaled, 1)
                h = heads[-1]
                dve.wait_ge(scaled, HEADS * t + h + 3)
                dve.tensor_scalar(nmax[:, h - 3:h + 1], smax[:, h - 3:h + 1], -1.0, None, ALU.mult).then_inc(nmax_done, 1)

            def sink_diff(t):
                dve.wait_ge(nmax_done, 2 * t + 2)
                dve.wait_ge(sink_e_done, t) if not isinstance(t, int) or t > 0 else None
                dve.tensor_tensor(sink_d[:, :], sink[:, :], nmax[:, :], ALU.add).then_inc(sink_d_done, 1)

            def route(b):
                n = [0]

                def then(ins):
                    n[0] += 1
                    ins.then_inc(route_step, 1)
                    dve.wait_ge(route_step, ROUTE_STEPS * b + n[0])

                dve.wait_ge(logits_done, b + 2)
                if not isinstance(b, int) or b > 0:
                    dve.wait_ge(ranked, b)
                    dve.wait_ge(gexp_done, b)
                    dve.wait_ge(place_step, PLACE_STEPS * b + PLACE0)
                here = bass.ds(b, 1)
                then(dve.tensor_tensor(logits[:, :], ps_x[:, 0:ROUT], rbias[:, :], ALU.add))
                take_waits(dve)
                then(dve.max(gtop[:, :], logits[:, 0:8]))
                take_waits(dve)
                then(dve.max_index(gidx[:, :], gtop[:, :], logits[:, 0:8]))
                then(dve.tensor_copy(gidx_f[:, :], gidx[:, 0:1]))
                then(dve.tensor_scalar(ngtop[:, :], gtop[:, 0:1], -1.0, None, ALU.mult))
                assert n[0] == AT_NGTOP
                then(dve.tensor_scalar(mlog[:, :], group_of[:, :], gidx_f[:, 0:1], NEG, ALU.not_equal, ALU.mult))
                then(dve.tensor_tensor(mlog[:, :], mlog[:, :], logits[:, 8:ROUT], ALU.add))
                take_waits(dve)
                then(dve.max(etop[:, :], mlog[:, :]))
                then(dve.tensor_tensor(ediff[:, :], etop[:, 1:2], etop[:, 0:1], ALU.subtract))
                assert n[0] == AT_EDIFF
                take_waits(dve)
                then(dve.max_index(eidx[:, :], etop[:, :], mlog[:, :]))
                then(dve.tensor_copy(expert1[:, here], eidx[:, 0:1]))
                then(dve.tensor_copy(expert2[:, here], eidx[:, 1:2]))
                dve.wait_ge(gexp_done, b + 1)
                dve.wait_ge(eexp_done, b + 1)
                then(dve.scalar_tensor_tensor(out=gden[:, :], in0=eexp[:, :], scalar=1.0, in1=gsum[:, :], op0=ALU.add, op1=ALU.mult))
                then(dve.reciprocal(gate1[:, here], gden[:, :]))
                then(dve.tensor_tensor(gate2[:, here], gate1[:, here], eexp[:, :], ALU.mult))
                then(dve.tensor_scalar(hot1[:, :], iota_e[:, :], expert1[:, here], None, ALU.is_equal))
                then(dve.tensor_scalar(hot2[:, :], iota_e[:, :], expert2[:, here], None, ALU.is_equal))
                then(dve.tensor_tensor(hot[:, :], hot1[:, :], hot2[:, :], ALU.add))
                assert n[0] == ROUTE_STEPS

            def attn_split(b):
                dve.wait_ge(a_hi_done, b + 1)
                dve.wait_ge(y_done, 4 * b) if not isinstance(b, int) or b > 0 else None
                dve.tensor_tensor(a_lo[:, :, :], ps_t[0][:, :].rearrange("p (k c) -> p k c", c=P), a_hi[:, :, :].bitcast(F32),
                                  ALU.subtract).then_inc(a_lo_done, 1)

            def attn_rstd(b):
                dve.wait_ge(rms_a_done, b + 1)
                dve.wait_ge(y_read, 4 * b + 2)
                dve.reciprocal(rstd_a[:, :], rms_a[:, :]).then_inc(rstd_a_done, 1)

            def residual(b, s, part, i):
                if part == 0 and i == 0:
                    dve.wait_ge(x_in[s], 16 * (b // 2 + 1) if isinstance(b, int) else 8 * (b - s) + 16)
                if part == 1:
                    dve.wait_ge(rstd_a_done, b + 1)
                    dve.wait_ge(y_read, 4 * b + i + 3)
                factor = rstd_rec[:, bass.ds(b, 1)] if part == 0 else rstd_a[:, 0:1]
                dve.wait_ge(y_done, 4 * b + 2 * part + i + 1)
                dve.scalar_tensor_tensor(out=xh[s][:, half(i)], in0=ps_y[i][:, :], scalar=factor, in1=xh[s][:, half(i)],
                                         op0=ALU.mult, op1=ALU.add).then_inc(y_read, 1)

            def ffn_norm(b, s):
                dve.wait_ge(rms_h_done, b + 1)
                dve.wait_ge(u_done, b) if not isinstance(b, int) or b > 0 else None
                dve.reciprocal(rstd_h[:, :], rms_h[:, :]).then_inc(rstd_h_done, 1)
                dve.wait_ge(rstd_h_done, b + 1)
                dve.scalar_tensor_tensor(out=u[:, :], in0=xh[s][:, :], scalar=rstd_h[:, 0:1], in1=g_ffn[:, :],
                                         op0=ALU.mult, op1=ALU.mult).then_inc(u_done, 1)

            def place(b, s):
                n = [0]

                def then(ins):
                    n[0] += 1
                    ins.then_inc(place_step, 1)
                    dve.wait_ge(place_step, PLACE_STEPS * b + PLACE0 + n[0])

                dve.wait_ge(ranked, b + 1)
                if not isinstance(b, int) or b >= 2:
                    dve.wait_ge(listed[s], 16 * (b - s))
                here = bass.ds(b, 1)
                then(dve.tensor_tensor(base[:, :], ps_x[:, 0:EXP], counts[:, :], ALU.add))
                then(dve.tensor_tensor(counts[:, :], counts[:, :], ps_x[:, EXP:2 * EXP], ALU.add))
                for j, (hot_j, place_j, expert_j) in enumerate(((hot1, place1, expert1), (hot2, place2, expert2))):
                    then(dve.tensor_tensor(prod[j][:, :], base[:, :], hot_j[:, :], ALU.mult))
                    then(dve.tensor_reduce(place_j[:, here], prod[j][:, :], AX.X, ALU.add))
                    then(dve.scalar_tensor_tensor(out=gden[:, :], in0=expert_j[:, here], scalar=float(LIST), in1=place_j[:, here],
                                                  op0=ALU.mult, op1=ALU.add))
                    dve.tensor_copy(addr[j][s][:, :], gden[:, :]).then_inc(addr_done, 1)
                    dve.wait_ge(addr_done, 2 * b + j + 1)
                assert n[0] == PLACE_STEPS

            def attn_output(t):
                dve.wait_ge(exp_done, HEADS * t + HEADS)
                dve.wait_ge(sink_e_done, t + 1)
                dve.wait_ge(den_done, 2 * t + 1)
                dve.tensor_tensor(den[:, :], rowsum[:, :], sink_e[:, :], ALU.add).then_inc(den_done, 1)
                dve.wait_ge(den_done, 2 * t + 2)
                dve.wait_ge(ao_done, t + 1)
                dve.reciprocal(rden[:, :], den[:, :]).then_inc(den_done, 1)
                dve.wait_ge(den_done, 2 * t + 3)
                dve.wait_ge(av_done, t + 2)
                if not isinstance(t, int) or t > 0:
                    dve.wait_ge(ao_turned, t)
                    dve.wait_ge(ssq_a_done, t)
                dve.tensor_tensor(attn_o[:, :].rearrange("p (h c) -> p h c", c=HD), ps_o[:, :].rearrange("p (h c) -> p h c", c=HD),
                                  rden[:, :].unsqueeze(2).to_broadcast([P, HEADS, HD]), ALU.mult).then_inc(ao_done, 1)

            def step(t, b1, b2, s):
                if b1 is not None:
                    attn_output(b1)
                if t is not None:
                    softmax_max(t, s, range(0, 4))
                if b1 is not None:
                    attn_split(b1)
                    residual(b1, 1 - s, 0, 0)
                if t is not None:
                    softmax_max(t, s, range(4, 8))
                    sink_diff(t)
                if b1 is not None:
                    residual(b1, 1 - s, 0, 1)
                    attn_rstd(b1)
                if b2 is not None:
                    route(b2)
                if b1 is not None:
                    residual(b1, 1 - s, 1, 0)
                    residual(b1, 1 - s, 1, 1)
                if b2 is not None:
                    place(b2, s)
                if t is not None and has_next(t):
                    rope_q(t + 1, 1 - s)
                if b1 is not None:
                    ffn_norm(b1, 1 - s)
                if t is not None and has_next(t):
                    split_q(t + 1)

            rope_q(0, 0)
            split_q(0)
            dve.wait_ge(sink_in, 16)
            dve.wait_ge(cleared, 4)
            run(dve, step)


PLAN_STEPS = 27


def plan(nc, sem, counts, start, table, table_dram):
    with ExitStack() as ctx:
        def sb(name, shape, dt=F32):
            return ctx.enter_context(nc.sbuf_tensor(name, shape, dt))

        ones = sb("p_ones", [P, EXP])
        blocks_i = sb("blocks_i", [P, EXP], I32)
        blocks = sb("blocks", [P, EXP])
        block_end = sb("block_end", [P, EXP])
        count_end = sb("count_end", [P, EXP])
        n_col = sb("n_col", [P, 1])
        before_n = sb("before_n", [P, EXP])
        weighed = sb("weighed", [P, EXP])
        n_experts = sb("n_experts", [P, 1])
        n_blocks = sb("n_blocks", [P, 1])
        n_tokens = sb("n_tokens", [P, 1])
        offset = sb("offset", [P, 1])
        row = sb("row", [P, FIELDS])
        row_i = sb("row_i", [P, FIELDS], I32)
        n_less_1 = sb("n_less_1", [P, 1])
        n_experts_1 = sb("n_experts_1", [P, 1])
        pairs_i = sb("pairs_i", [P, 1], I32)

        set_up = sem("p_set_up")
        step = sem("p_step")
        table_out = sem("p_table_out")
        table_in = sem("p_table_in")
        block = ctx.enter_context(nc.Block())

        @block.gpsimd
        def _(pool):
            pool.memset(ones[:, :], 1.0).then_inc(set_up, 1)
            pool.iota(n_col[:, :], pattern=[[0, 1]], base=0, channel_multiplier=1,
                      allow_small_or_imprecise_dtypes=True).then_inc(set_up, 1)
            pool.iota(n_less_1[:, :], pattern=[[0, 1]], base=-1, channel_multiplier=1,
                      allow_small_or_imprecise_dtypes=True).then_inc(set_up, 1)

        @block.vector
        def _(dve):
            n = [0]

            def then(ins):
                n[0] += 1
                ins.then_inc(step, 1)
                dve.wait_ge(step, n[0])

            dve.wait_ge(set_up, 3)
            then(dve.tensor_scalar(blocks_i[:, :], counts[:, :], float(P - 1), None, ALU.add))
            then(dve.tensor_single_scalar(blocks_i[:, :], blocks_i[:, :], P.bit_length() - 1, ALU.arith_shift_right))
            then(dve.tensor_copy(blocks[:, :], blocks_i[:, :]))
            then(dve.tensor_tensor_scan(block_end[:, :], ones[:, :], blocks[:, :], 0.0, ALU.mult, ALU.add))
            then(dve.tensor_tensor_scan(count_end[:, :], ones[:, :], counts[:, :], 0.0, ALU.mult, ALU.add))
            then(dve.tensor_tensor(start[:, :], count_end[:, :], counts[:, :], ALU.subtract))
            then(dve.tensor_scalar(before_n[:, :], block_end[:, :], n_col[:, 0:1], None, ALU.is_le))
            then(dve.tensor_reduce(n_experts[:, :], before_n[:, :], AX.X, ALU.add))
            for total, each in ((n_blocks, blocks), (n_tokens, counts)):
                then(dve.tensor_tensor(weighed[:, :], before_n[:, :], each[:, :], ALU.mult))
                then(dve.tensor_reduce(total[:, :], weighed[:, :], AX.X, ALU.add))
            then(dve.tensor_tensor(offset[:, :], n_col[:, :], n_blocks[:, :], ALU.subtract))
            then(dve.tensor_scalar(offset[:, :], offset[:, :], float(P), None, ALU.mult))
            then(dve.tensor_scalar(row[:, 0:1], n_experts[:, :], float(EXP - 1), None, ALU.min))
            then(dve.tensor_scalar(before_n[:, :], block_end[:, :], n_less_1[:, 0:1], None, ALU.is_le))
            then(dve.tensor_reduce(n_experts_1[:, :], before_n[:, :], AX.X, ALU.add))
            then(dve.scalar_tensor_tensor(out=n_experts_1[:, :], in0=n_less_1[:, :], scalar=0.0, in1=n_experts_1[:, :],
                                          op0=ALU.min, op1=ALU.add))
            then(dve.tensor_scalar(row[:, 3:4], n_experts_1[:, :], row[:, 0:1], None, ALU.is_lt))
            then(dve.scalar_tensor_tensor(out=row[:, 1:2], in0=n_experts[:, :], scalar=float(LIST), in1=offset[:, :],
                                          op0=ALU.mult, op1=ALU.add))
            then(dve.tensor_tensor(row[:, 2:3], n_tokens[:, :], offset[:, :], ALU.add))
            then(dve.tensor_scalar(pairs_i[:, :], block_end[:, EXP - 1:EXP], -2.0, None, ALU.add))
            then(dve.tensor_single_scalar(pairs_i[:, :], pairs_i[:, :], 1, ALU.arith_shift_right))
            then(dve.tensor_copy(row_i[:, 0:4], row[:, 0:4]))
            then(dve.tensor_copy(row_i[:, 4:5], pairs_i[:, :]))
            then(dve.scalar_tensor_tensor(out=n_blocks[:, :], in0=pairs_i[:, :], scalar=-2.0, in1=block_end[:, EXP - 1:EXP],
                                          op0=ALU.mult, op1=ALU.add))
            then(dve.tensor_scalar(row_i[:, 5:6], n_blocks[:, :], -2.0, None, ALU.add))
            assert n[0] == PLAN_STEPS

        @block.sync
        def _(sp):
            sp.wait_ge(step, PLAN_STEPS)
            sp.dma_start(table_dram, row_i[0:MAXBLK, :]).then_inc(table_out, 16)
            sp.wait_ge(table_out, 16)
            sp.dma_start(table[:, :], table_dram.rearrange("(o n) c -> o (n c)", o=1)).then_inc(table_in, 16)
            sp.wait_ge(table_in, 16)


def experts(nc, sem, a, ident, iota_e, start, expert1, expert2, place1, place2, slots, table, list_dram,
            u_dram, h2_dram, y_dram, g_final, z, g_in, z_in):
    with ExitStack() as ctx:
        def sb(name, shape, dt=F32):
            return ctx.enter_context(nc.sbuf_tensor(name, shape, dt))

        KG, KDN = 4, 2
        CHUNK = KG * FE
        SLOTS = 6
        D0, D1, U0, U1, G0, G1 = range(SLOTS)
        raw = [sb(f"raw{s}", [P, CHUNK]) for s in range(SLOTS)]
        w_hi = [sb(f"e_hi{s}", [P, CHUNK], F32R) for s in range(SLOTS)]
        w_lo = [sb(f"e_lo{s}", [P, CHUNK], F32R) for s in range(SLOTS)]
        ix = [sb(f"ix{s}", [P, 1], I32) for s in range(RING)]
        x = [sb(f"ex{s}", [P, D]) for s in range(RING)]
        x_hi = [sb(f"ex_hi{s}", [P, KD, P], F32R) for s in range(RING)]
        x_lo = [sb(f"ex_lo{s}", [P, KD, P], F32R) for s in range(RING)]
        silu = sb("silu", [P, FE])
        hid = sb("hid", [P, FE])
        h_hi = sb("hid_hi", [P, FT, P], F32R)
        h_lo = sb("hid_lo", [P, FT, P], F32R)
        y = sb("y_sb", [P, D])
        hot = [t[:, 0:NB * EXP].rearrange("p (b e) -> p b e", e=EXP) for t in (silu, hid)]
        slot_f = sb("slot_f", [P, NB])
        ps_g = ctx.enter_context(nc.psum_tensor("ps_g", [P, FE], F32))
        ps_u = ctx.enter_context(nc.psum_tensor("ps_u", [P, FE], F32))
        ps_y = ctx.enter_context(nc.psum_tensor("ps_ey", [P, 2, BANK], F32))
        ps_x = ctx.enter_context(nc.psum_tensor("ps_ex", [P, 2, BANK], F32))
        ps_h = ctx.enter_context(nc.psum_tensor("ps_eh", [P, FE], F32))

        waited = sem("e_waited")
        waited_sp = sem("e_waited_sp")
        slot_step = sem("e_slot_step")
        arrived = [sem(f"e_arrived{s}") for s in range(SLOTS)]
        ix_in = [sem(f"e_ix_in{s}") for s in range(RING)]
        x_in = [sem(f"e_x_in{s}") for s in range(RING)]
        hi_done = sem("e_hi_done")
        lo_done = sem("e_lo_done")
        used = sem("e_used")
        x_turned = sem("e_x_turned")
        x_hi_done = sem("e_x_hi_done")
        x_lo_done = sem("e_x_lo_done")
        silu_done = sem("e_silu_done")
        hid_done = sem("e_hid_done")
        hid_turned = sem("e_hid_turned")
        h_hi_done = sem("e_h_hi_done")
        h_lo_done = sem("e_h_lo_done")
        y_out = sem("e_y_out")
        y_stored = sem("e_y_stored")

        block = ctx.enter_context(nc.Block())

        def field(eng, n, c, top):
            at = FIELDS * n + c
            where = slice(at, at + 1) if isinstance(n, int) else bass.ds(at, 1)
            return eng.value_load(table[0:1, where], min_val=0, max_val=top)

        def is_new(eng, m):
            return field(eng, m, 3, 1)

        def one_more(eng):
            return eng.value_load(table[0:1, 5:6], min_val=0, max_val=1)

        def more_pairs(eng):
            return eng.value_load(table[0:1, 4:5], min_val=0, max_val=MAXPAIRS - 1)

        def chunk_of(n, s):
            return SLOTS * n + SLOTS + s

        def up_used(n):
            return SLOTS + SLOTS * n + 4

        def gate_used(n):
            return SLOTS + (2 if isinstance(n, int) and n == 0 else SLOTS * n)

        def down_used(n):
            return SLOTS + SLOTS * n + 8

        @block.sync
        def _(sp):
            def load(weights, k, e, c, s):
                src = weights[bass.ds(e, 1), :, :].rearrange("o (c p k) f -> c p (o k f)", p=P, k=k)[c]
                sp.dma_start(raw[s][:, :], src).then_inc(arrived[s], 16)

            def lists(m, s):
                at = field(sp, m, 1, EXP * LIST + 2 * P)
                sp.dma_start(ix[s][:, :], list_dram[bass.ds(at, P), :]).then_inc(ix_in[s], 16)

            def expert(n):
                return field(sp, n, 0, EXP - 1)

            for m in range(2):
                lists(m, m)
            e0, e1 = expert(0), expert(1)
            for weights, e, s0 in ((a["w_gate"], e0, D0), (a["w_up"], e0, U0), (a["w_gate"], e1, G0)):
                for c in range(2):
                    load(weights, KG, e, c, s0 + c)
                    if s0 + c == D0:
                        sp.wait_ge(x_in[0], 16)

            def step(n, s):
                sp.wait_ge(x_in[s], 8 * (n - s) + 16)
                lists(n + 2, s)
                for weights, k, m, s0 in ((a["w_down"], KDN, n, D0), (a["w_up"], KG, n + 1, U0), (a["w_gate"], KG, n + 2, G0)):
                    e, new = expert(m), is_new(sp, m)
                    for c in range(2):
                        sp.wait_ge(lo_done, chunk_of(n, s0 + c) + 1)
                        sp.sem_inc(waited_sp, 1)
                        with sp.If(new > 0):
                            load(weights, k, e, c, s0 + c)
                        with sp.If(new < 1):
                            sp.sem_inc(arrived[s0 + c], 16)

            more = more_pairs(sp)
            with sp.Fori(0, more + 1) as i:
                step(2 * i, 0)
                step(2 * i + 1, 1)
            odd = one_more(sp)
            with sp.If(odd > 0):
                step(2 * more + 2, 0)
            for s in range(len(z)):
                sp.dma_start(z[s][:, :], h2_dram[s * P:(s + 1) * P, :]).then_inc(z_in[s], 16)
            sp.dma_start(g_final[:, :], a["ln_final_g"][0].partition_broadcast(P)).then_inc(g_in, 16)
            for s in range(SLOTS):
                sp.wait_ge(arrived[s], 32 * more + 48 + 16 * odd)
            sp.wait_ge(x_in[0], 16 * more + 32 + 16 * odd)
            sp.wait_ge(x_in[1], 16 * more + 32)
            sp.sem_inc(waited_sp, 1)

        @block.gpsimd
        def _(pool):
            def gather(m, s):
                pool.wait_ge(ix_in[s], 8 * (m - s) + 16)
                if not isinstance(m, int) or m >= 2:
                    pool.wait_ge(x_turned, m - 1)
                pool.sem_inc(waited, 1)
                pool.indirect_dma_start(x[s][:, :], None, u_dram, bass.IndirectOffsetOnAxis(ap=ix[s][:, 0:1], axis=0)
                                        ).then_inc(x_in[s], 16)

            def store(n):
                at = field(pool, n, 2, 2 * REAL)
                pool.wait_ge(y_out, n + 2)
                pool.wait_ge(y_stored, 16 * n) if not isinstance(n, int) or n > 0 else None
                pool.sem_inc(waited, 1)
                pool.dma_start(y_dram[bass.ds(at, P), :], y[:, :]).then_inc(y_stored, 16)

            for m in range(3):
                gather(m, m % 2)
            gather(3, 1)
            store(0)
            more = more_pairs(pool)
            with pool.Fori(0, more) as i:
                gather(2 * i + 4, 0)
                store(2 * i + 1)
                gather(2 * i + 5, 1)
                store(2 * i + 2)
            odd = one_more(pool)
            with pool.If(odd > 0):
                gather(2 * more + 4, 0)
            store(2 * more + 1)
            with pool.If(odd > 0):
                store(2 * more + 2)
            pool.wait_ge(y_stored, 32 * more + 32 + 16 * odd)
            pool.sem_inc(waited, 1)

        @block.tensor
        def _(pe):
            def turn_x(m, s):
                pe.wait_ge(x_in[s], 8 * (m - s) + 16)
                pe.wait_ge(x_lo_done, m + 1)
                for c in range(2):
                    for k in range(KG):
                        mm = pe.transpose(ps_x[:, c, k * P:(k + 1) * P], x[s][:, c * FE + k:(c + 1) * FE:KG], ident[:, :])
                mm.then_inc(x_turned, 1)

            def half_product(ps, s, c, idx, slot):
                pe.wait_ge(lo_done, idx + 1 + SLOTS)
                for k in range(KG):
                    for n, (xs, w) in enumerate(((x_hi, w_hi), (x_hi, w_lo), (x_lo, w_hi))):
                        mm = pe.matmul(ps[:, :], xs[s][:, c * KG + k, :], w[slot][:, k * FE:(k + 1) * FE],
                                       start=(c == 0 and k == 0 and n == 0), stop=(c == 1 and k == KG - 1 and n == 2))
                mm.then_inc(used, 1)

            def up(n, s):
                pe.wait_ge(hid_done, n + 1)
                for c in range(2):
                    half_product(ps_u, s, c, SLOTS * n + 2 + c, U0 + c)

            def gate(m, s, c, idx, slot):
                if c == 0:
                    pe.wait_ge(x_lo_done, m + 2)
                    pe.wait_ge(silu_done, m + 1)
                half_product(ps_g, s, c, idx, slot)

            def down(n):
                pe.wait_ge(h_lo_done, n + 2)
                pe.wait_ge(y_out, n + 1)
                for c in range(2):
                    pe.wait_ge(lo_done, chunk_of(n, D0 + c) + 1 + SLOTS)
                    for k in range(KDN):
                        for i in range(2):
                            for j, (h, w) in enumerate(((h_hi, w_hi), (h_hi, w_lo), (h_lo, w_hi))):
                                mm = pe.matmul(ps_y[:, i, :], h[:, c * KDN + k, :], w[D0 + c][:, k * D + i * BANK:k * D + (i + 1) * BANK],
                                               start=(c == 0 and k == 0 and j == 0), stop=(c == 1 and k == KDN - 1 and j == 2))
                    mm.then_inc(used, 1)

            def step(n, s):
                turn_x(n + 1, 1 - s)
                up(n, s)
                gate(n + 1, 1 - s, 0, SLOTS * n + 4, G0)
                pe.wait_ge(hid_done, n + 2)
                pe.wait_ge(h_lo_done, n + 1)
                for c in range(2):
                    for k in range(KDN):
                        mm = pe.transpose(ps_h[:, (c * KDN + k) * P:(c * KDN + k + 1) * P],
                                          hid[:, c * 2 * P + k:(c + 1) * 2 * P:KDN], ident[:, :])
                mm.then_inc(hid_turned, 1)
                gate(n + 1, 1 - s, 1, SLOTS * n + 5, G1)
                down(n)

            turn_x(0, 0)
            for c in range(2):
                gate(0, 0, c, c, D0 + c)
            more = more_pairs(pe)
            with pe.Fori(0, more + 1) as i:
                step(2 * i, 0)
                step(2 * i + 1, 1)
            with pe.If(one_more(pe) > 0):
                step(2 * more + 2, 0)

        def square_x(t):
            return t[:, :, :].rearrange("p b (k c) -> p (b k) c", c=P)

        @block.scalar
        def _(act):
            act.sem_inc(used, SLOTS)
            act.sem_inc(y_out, 1)
            act.sem_inc(silu_done, 1)

            def split(idx, s, round_):
                act.wait_ge(arrived[s], 16 * round_ + 16)
                act.wait_ge(used, idx + 1)
                act.activation(w_hi[s][:, :], raw[s][:, :], ACT.Copy).then_inc(hi_done, 1)

            def split_new(n, m, slots_):
                new = is_new(act, m)
                with act.If(new > 0):
                    for s_ in slots_:
                        split(chunk_of(n, s_), s_, n + 1)
                with act.If(new < 1):
                    for s_ in slots_:
                        act.wait_ge(arrived[s_], 16 * n + 32)
                        act.wait_ge(hi_done, chunk_of(n, s_))
                        act.sem_inc(hi_done, 1)

            def x_split(m, s):
                act.wait_ge(x_turned, m + 1)
                act.activation(x_hi[s][:, :, :], square_x(ps_x), ACT.Copy).then_inc(x_hi_done, 1)

            def y_from_psum(n):
                act.wait_ge(used, down_used(n))
                act.wait_ge(y_stored, 16 * n) if not isinstance(n, int) or n > 0 else None
                act.activation(y[:, :], ps_y[:, :, :].rearrange("p b c -> p (b c)"), ACT.Copy).then_inc(y_out, 1)

            def step(n, s, before):
                act.wait_ge(used, gate_used(n))
                act.wait_ge(hid_done, n + 1)
                act.activation(silu[:, :], ps_g[:, :], ACT.Silu).then_inc(silu_done, 1)
                x_split(n + 1, 1 - s)
                if before is not None:
                    y_from_psum(before)
                split_new(n, n, (D0, D1))
                split_new(n, n + 1, (U0,))
                act.wait_ge(hid_turned, n + 1)
                act.activation(h_hi[:, :, :], ps_h[:, :].rearrange("p (k c) -> p k c", c=P), ACT.Copy).then_inc(h_hi_done, 1)
                split_new(n, n + 1, (U1,))
                split_new(n, n + 2, (G0, G1))

            for s in range(SLOTS):
                split(s, s, 0)
                if s == 0:
                    x_split(0, 0)
            step(0, 0, None)
            step(1, 1, 0)
            more = more_pairs(act)
            with act.Fori(0, more) as i:
                step(2 * i + 2, 0, 2 * i + 1)
                step(2 * i + 3, 1, 2 * i + 2)
            odd = one_more(act)
            with act.If(odd > 0):
                step(2 * more + 2, 0, 2 * more + 1)
            y_from_psum(2 * more + 1 + odd)

        @block.vector
        def _(dve):
            dve.sem_inc(lo_done, SLOTS)
            dve.sem_inc(x_lo_done, 1)
            dve.sem_inc(h_lo_done, 1)
            dve.sem_inc(hid_done, 1)

            def split(idx, s):
                dve.wait_ge(hi_done, idx + 1)
                dve.tensor_tensor(w_lo[s][:, :], raw[s][:, :], w_hi[s][:, :].bitcast(F32), ALU.subtract).then_inc(lo_done, 1)

            def split_new(n, m, slots_):
                new = is_new(dve, m)
                with dve.If(new > 0):
                    for s_ in slots_:
                        split(chunk_of(n, s_), s_)
                with dve.If(new < 1):
                    for s_ in slots_:
                        dve.wait_ge(hi_done, chunk_of(n, s_) + 1)
                        dve.wait_ge(lo_done, chunk_of(n, s_) + SLOTS)
                        dve.sem_inc(lo_done, 1)

            def x_split(m, s):
                dve.wait_ge(x_hi_done, m + 1)
                dve.tensor_tensor(x_lo[s][:, :, :], square_x(ps_x), x_hi[s][:, :, :].bitcast(F32), ALU.subtract).then_inc(x_lo_done, 1)

            def step(n, s):
                x_split(n + 1, 1 - s)
                split_new(n, n, (D0,))
                dve.wait_ge(used, up_used(n))
                dve.wait_ge(silu_done, n + 2)
                dve.wait_ge(hid_turned, n) if not isinstance(n, int) or n > 0 else None
                dve.tensor_tensor(hid[:, :], ps_u[:, :], silu[:, :], ALU.mult).then_inc(hid_done, 1)
                split_new(n, n, (D1,))
                dve.wait_ge(h_hi_done, n + 1)
                dve.tensor_tensor(h_lo[:, :, :], ps_h[:, :].rearrange("p (k c) -> p k c", c=P), h_hi[:, :, :].bitcast(F32),
                                  ALU.subtract).then_inc(h_lo_done, 1)
                split_new(n, n + 1, (U0, U1))
                split_new(n, n + 2, (G0, G1))

            n = [0]

            def then(ins):
                n[0] += 1
                ins.then_inc(slot_step, 1)
                dve.wait_ge(slot_step, n[0])

            wide = [P, NB, EXP]
            for j, (expert_j, place_j) in enumerate(((expert1, place1), (expert2, place2))):
                then(dve.tensor_tensor(hot[j], iota_e[:, :].unsqueeze(1).to_broadcast(wide),
                                       expert_j[:, :].unsqueeze(2).to_broadcast(wide), ALU.is_equal))
                then(dve.tensor_tensor(hot[j], hot[j], start[:, :].unsqueeze(1).to_broadcast(wide), ALU.mult))
                then(dve.tensor_reduce(slot_f[:, :], hot[j], AX.X, ALU.add))
                then(dve.tensor_tensor(slot_f[:, :], slot_f[:, :], place_j[:, :], ALU.add))
                then(dve.tensor_copy(slots[j][:, :], slot_f[:, :]))

            for s in range(SLOTS):
                split(s, s)
                if s == 0:
                    x_split(0, 0)
            step(0, 0)
            step(1, 1)
            more = more_pairs(dve)
            with dve.Fori(0, more) as i:
                step(2 * i + 2, 0)
                step(2 * i + 3, 1)
            with dve.If(one_more(dve) > 0):
                step(2 * more + 2, 0)


def combine(nc, sem, eps_t, gate1, gate2, slots, h2_dram, y_dram, out, g_final, z, g_in, z_in):
    with ExitStack() as ctx:
        def sb(name, shape, dt=F32):
            return ctx.enter_context(nc.sbuf_tensor(name, shape, dt))

        early = len(z)
        z = z + [sb(f"cz{b}", [P, D]) for b in range(early, NB)]
        y = [[sb(f"cy{j}{b}", [P, D]) for b in range(NB)] for j in range(2)]
        square = sb("c_square", [P, D])
        ssq = sb("c_ssq", [P, NB])
        rms = sb("c_rms", [P, NB])
        rstd = sb("c_rstd", [P, NB])
        z_in = z_in + [sem(f"c_z_in{b}") for b in range(early, NB)]
        y_in = [sem(f"c_y_in{b}") for b in range(NB)]
        added = sem("c_added")
        squared = sem("c_squared")
        rms_done = sem("c_rms_done")
        rstd_done = sem("c_rstd_done")
        normed = sem("c_normed")
        stored = sem("c_stored")
        block = ctx.enter_context(nc.Block())

        @block.sync
        def _(sp):
            for b in range(early, NB):
                sp.wait_ge(y_in[b - early], 32)
                sp.dma_start(z[b][:, :], h2_dram[b * P:(b + 1) * P, :]).then_inc(z_in[b], 16)
            for b in range(NB):
                sp.wait_ge(normed, b + 1)
                sp.dma_start(out[b * P:(b + 1) * P, :], z[b][:, :]).then_inc(stored, 16)
            sp.wait_ge(stored, 16 * NB)

        @block.gpsimd
        def _(pool):
            for b in range(NB):
                for j in range(2):
                    pool.indirect_dma_start(y[j][b][:, :], None, y_dram,
                                            bass.IndirectOffsetOnAxis(ap=slots[j][:, b:b + 1], axis=0)).then_inc(y_in[b], 16)

        @block.scalar
        def _(act):
            for b in range(NB):
                act.wait_ge(added, 2 * b + 2)
                act.wait_ge(squared, b) if b else None
                act.activation(square[:, :], z[b][:, :], ACT.Square, accum_out=ssq[:, b:b + 1]).then_inc(squared, 1)
                act.wait_ge(squared, b + 1)
                act.activation(rms[:, b:b + 1], ssq[:, b:b + 1], ACT.Sqrt, bias=eps_t[:, :], scale=1.0 / D).then_inc(rms_done, 1)

        @block.vector
        def _(dve):
            def norm(b):
                dve.wait_ge(rms_done, b + 1)
                dve.reciprocal(rstd[:, b:b + 1], rms[:, b:b + 1]).then_inc(rstd_done, 1)
                dve.wait_ge(rstd_done, b + 1)
                zs = z[b]
                dve.scalar_tensor_tensor(out=zs[:, :], in0=zs[:, :], scalar=rstd[:, b:b + 1], in1=g_final[:, :],
                                         op0=ALU.mult, op1=ALU.mult).then_inc(normed, 1)

            dve.wait_ge(g_in, 16)
            for b in range(NB):
                dve.wait_ge(z_in[b], 16)
                dve.wait_ge(y_in[b], 32)
                for j, gate in enumerate((gate1, gate2)):
                    dve.scalar_tensor_tensor(out=z[b][:, :], in0=y[j][b][:, :], scalar=gate[:, b:b + 1], in1=z[b][:, :],
                                             op0=ALU.mult, op1=ALU.add).then_inc(added, 1)
                    dve.wait_ge(added, 2 * b + j + 1)
                if b:
                    norm(b - 1)
            norm(NB - 1)


def layouts(i):
    f = np.float32

    def feature_tiles(w):
        w = w.reshape(KD, P, -1)
        q = [np.r_[h * HD:(h + 1) * HD, (h + 4) * HD:(h + 5) * HD] for h in range(4)]
        k, v, *rec = (np.arange(c, c + P) for c in range(ATTN, w.shape[2], P))
        cols = [*rec, *q, k, v]
        return np.stack([w[:, :, c].transpose(1, 0, 2) for c in cols])

    def per_feature(v):
        return v.reshape(FT, P).T

    gates = np.zeros((FT, P, 4, P), f)
    for g, name in enumerate(("w_rgate_fwd", "w_igate_fwd", "w_rgate_bwd", "w_igate_bwd")):
        for ft in range(FT):
            gates[ft, 0:HD, g, 0:HD] = i[name][0, 2 * ft]
            gates[ft, HD:P, g, HD:P] = i[name][0, 2 * ft + 1]
    vecs = [i["conv_w"][0, j] for j in range(4)] + [i["conv_b"][0]]
    vecs += [i[n][0] for n in ("b_rgate_fwd", "b_igate_fwd", "b_rgate_bwd", "b_igate_bwd", "lam_fwd", "lam_bwd")]
    router = np.zeros((D, ROUT), f)
    router[:, 0:4] = i["w_router_grp"][0]
    router[:, 8:ROUT] = i["w_router_exp"][0]
    rbias = np.full(ROUT, NEG, f)
    rbias[0:4] = i["b_router_grp"][0]
    rbias[8:ROUT] = i["b_router_exp"][0]
    pos = np.r_[np.arange(META + SEQS[0]), META + np.arange(SEQS[1])].astype(f)
    inv = f(500000.0) ** (-np.arange(0, 16, 2, dtype=f) / f(16))
    ang = pos[:, None] * inv[None, :]
    cos, sin = np.ones((P, COLS), f), np.zeros((P, COLS), f)
    swap = np.zeros((P, P), f)
    for h in (0, HD):
        for j in range(8):
            cos[h + j] = cos[h + 8 + j] = np.cos(ang[:, j])
            sin[h + j] = -np.sin(ang[:, j])
            sin[h + 8 + j] = np.sin(ang[:, j])
            swap[h + 8 + j, h + j] = swap[h + j, h + 8 + j] = 1.0
    masks = np.zeros((NB, P, KEYS), f)
    qi, kj = np.arange(P)[:, None], np.arange(P)[None, :]
    last = (SEQS[0] // P - 1, NB - 1)
    first = (0, SEQS[0] // P)
    for b in range(NB):
        masks[b, :, 0:P] = NEG if b in first else np.where(kj >= qi, 0.0, NEG)
        masks[b, :, 2 * P:3 * P] = NEG if b in last else np.where(kj <= qi, 0.0, NEG)
    before = (np.arange(P)[:, None] < np.arange(P)[None, :]).astype(f)
    return {
        "x": np.concatenate([i["x_prompt"][0], i["x_sample"][0]]),
        "meta": i["meta_tokens"],
        "ln_mix_g": i["ln_mix_g"],
        "w_in": feature_tiles(i["w_in"][0]),
        "gates": gates,
        "vecs": np.stack([per_feature(v) for v in vecs], axis=2),
        "sink": i["attn_sink"],
        "g_out": np.stack([i["g_attn_out"][0].reshape(FT, P), i["g_rec_out"][0].reshape(FT, P)]).reshape(KD, P).T.copy(),
        "w_out": i["w_out"][0].reshape(KD, P, D).transpose(1, 0, 2),
        "ln_ffn_g": i["ln_ffn_g"],
        "router": router.reshape(KD, P, ROUT).transpose(1, 0, 2),
        "rbias": rbias[None],
        "w_gate": i["w_exp_gate"][0],
        "w_up": i["w_exp_up"][0],
        "w_down": i["w_exp_down"][0],
        "ln_final_g": i["ln_final_g"][None],
        "ident": np.eye(P, dtype=f),
        "swap": swap,
        "before": before,
        "cos": cos,
        "sin": sin,
        "masks": masks,
    }


def kernel(**inputs):
    import concourse.bacc as bacc
    from concourse.bass_utils import run_bass_kernel_spmd as run

    arrays = {n: np.ascontiguousarray(v) for n, v in layouts({n: np.asarray(v) for n, v in inputs.items()}).items()}
    nc = bacc.Bacc("TRN2", target_bir_lowering=False, num_devices=1)
    a = {n: nc.dram_tensor(f"in_{n}", v.shape, mybir.dt.from_np(v.dtype), kind="ExternalInput").ap()
         for n, v in arrays.items()}
    out = nc.dram_tensor("out", (REAL, D), F32, kind="ExternalOutput").ap()
    encoder(nc, a, out)
    got = run(nc, [{f"in_{n}": v for n, v in arrays.items()}], core_ids=[0]).results[0]["out"]
    return got[0:SEQS[0]][None], got[SEQS[0]:REAL][None]
```
